# Optimizing a Trainium2 kernel written in Bass

```python
import math
import jax, jax.numpy as jnp
from jax import lax
import numpy as np

D_MODEL = 1024
BATCH = 1
SEQ = 4096
DEPTH = 1

N_META = 16
RET_HEADS = 4
RET_WIDTH = D_MODEL // 2
RET_DV = RET_WIDTH // RET_HEADS
RET_DK = RET_DV // 2
RET_QK_WIDTH = RET_HEADS * RET_DK
CHUNK = 128
ROPE_BASE = 10000.0
POOL_WINDOWS = (2, 4, 8, 16)
POOL_GROUPS = len(POOL_WINDOWS)
POOL_WIDTH = D_MODEL // 2
POOL_CH = POOL_WIDTH // POOL_GROUPS
MIX_WIDTH = RET_WIDTH + POOL_WIDTH
IN_COLS = 2 * RET_QK_WIDTH + 2 * RET_WIDTH + POOL_WIDTH
N_GROUPS = 4
EXPERTS_PER_GROUP = 8
N_EXPERTS = N_GROUPS * EXPERTS_PER_GROUP
D_EXPERT = D_MODEL // 2
TOP_K = 2
MOE_BLOCK = 128
LN_EPS = 1e-5
GN_EPS = 1e-6
ALPHA = (2 * DEPTH) ** 0.25
BETA = (8 * DEPTH) ** -0.25

kernel_name = 'hybrid_retention_pool_hmoe'

def layer_norm(x, g, b):
    xf = x.astype(jnp.float32)
    mu = jnp.mean(xf, axis=-1, keepdims=True)
    var = jnp.mean(jnp.square(xf - mu), axis=-1, keepdims=True)
    return ((xf - mu) * lax.rsqrt(var + LN_EPS) * g.astype(jnp.float32) + b.astype(jnp.float32)).astype(x.dtype)

def rotary(x, pos):
    half = x.shape[-1] // 2
    inv = ROPE_BASE ** (-jnp.arange(half, dtype=jnp.float32) / half)
    ang = pos.astype(jnp.float32)[:, None] * inv[None, :]
    cos = jnp.cos(ang)[None, :, None, :]
    sin = jnp.sin(ang)[None, :, None, :]
    x1, x2 = x[..., :half], x[..., half:]
    return jnp.concatenate([x1 * cos - x2 * sin, x1 * sin + x2 * cos], axis=-1).astype(x.dtype)

def retention_chunkwise(q, k, v):
    B, L, H, _ = q.shape
    pad = CHUNK - N_META
    padw = ((0, 0), (pad, 0), (0, 0), (0, 0))
    q, k, v = jnp.pad(q, padw), jnp.pad(k, padw), jnp.pad(v, padw)
    Lp = L + pad
    nc = Lp // CHUNK
    qc = q.reshape(B, nc, CHUNK, H, RET_DK)
    kc = k.reshape(B, nc, CHUNK, H, RET_DK)
    vc = v.reshape(B, nc, CHUNK, H, RET_DV)
    log_g = jnp.log1p(-jnp.power(2.0, -5.0 - jnp.arange(H, dtype=jnp.float32)))
    i = jnp.arange(CHUNK, dtype=jnp.float32)
    rel = i[:, None] - i[None, :]
    dmask = jnp.where(rel[None] >= 0, jnp.exp(jnp.maximum(rel, 0.0)[None] * log_g[:, None, None]), 0.0)
    scores = jnp.einsum('bnihd,bnjhd->bnhij', qc, kc) * dmask
    inner = jnp.einsum('bnhij,bnjhv->bnihv', scores, vc)
    zeta = jnp.exp((CHUNK - 1 - i)[None, :] * log_g[:, None])
    kv = jnp.einsum('bnjhd,hj,bnjhv->nbhdv', kc, zeta, vc)
    chunk_decay = jnp.exp(CHUNK * log_g)[:, None, None]

    def step(state, kv_n):
        return chunk_decay * state + kv_n, state

    _, prev = lax.scan(step, jnp.zeros((B, H, RET_DK, RET_DV), kv.dtype), kv)
    xi = jnp.exp((i + 1)[None, :] * log_g[:, None])
    cross = jnp.einsum('bnihd,nbhdv,hi->bnihv', qc, prev, xi)
    out = (inner + cross).reshape(B, Lp, H, RET_DV)
    return out[:, pad:]

def head_group_norm(y):
    yf = y.astype(jnp.float32)
    mu = jnp.mean(yf, axis=-1, keepdims=True)
    var = jnp.mean(jnp.square(yf - mu), axis=-1, keepdims=True)
    return (yf - mu) * lax.rsqrt(var + GN_EPS)

def causal_multiscale_pool(u):
    L = u.shape[1]
    uf = u.astype(jnp.float32)
    cs = jnp.cumsum(uf, axis=1)
    t = jnp.arange(L)
    outs = []
    for gi, w in enumerate(POOL_WINDOWS):
        sl = slice(gi * POOL_CH, (gi + 1) * POOL_CH)
        c = cs[..., sl]
        shifted = jnp.pad(c, ((0, 0), (w, 0), (0, 0)))[:, :L]
        count = jnp.minimum(t + 1, w).astype(jnp.float32)[None, :, None]
        outs.append((c - shifted) / count - uf[..., sl])
    return jnp.concatenate(outs, axis=-1)

def token_mixer(h, w_in, pool_w, pool_b, pool_scale, w_out):
    B, L, _ = h.shape
    proj = h @ w_in
    q, k, v, gate, u = jnp.split(
        proj, [RET_QK_WIDTH, 2 * RET_QK_WIDTH, 2 * RET_QK_WIDTH + RET_WIDTH, 2 * RET_QK_WIDTH + 2 * RET_WIDTH], axis=-1)
    pos = jnp.arange(L)
    q = rotary(q.reshape(B, L, RET_HEADS, RET_DK), pos)
    k = rotary(k.reshape(B, L, RET_HEADS, RET_DK), pos) * (RET_DK ** -0.5)
    ret = retention_chunkwise(q, k, v.reshape(B, L, RET_HEADS, RET_DV))
    ret = head_group_norm(ret).reshape(B, L, RET_WIDTH).astype(h.dtype)
    ret_out = jax.nn.silu(gate) * ret
    pooled = causal_multiscale_pool(u).astype(h.dtype).reshape(B, L, POOL_GROUPS, POOL_CH)
    pooled = jnp.einsum('blgc,gcd->blgd', pooled, pool_w) + pool_b[None, None]
    pool_out = pooled.reshape(B, L, POOL_WIDTH) * pool_scale
    return jnp.concatenate([ret_out, pool_out], axis=-1) @ w_out

def hierarchical_moe(h2d, rg_w, rg_b, re_w, re_b, w_gate, w_up, w_down):
    N = h2d.shape[0]
    g_logits = (h2d @ rg_w + rg_b).astype(jnp.float32)
    g_p, g_idx = lax.top_k(jax.nn.softmax(g_logits, axis=-1), 1)
    e_logits = (h2d @ re_w + re_b).astype(jnp.float32).reshape(N, N_GROUPS, EXPERTS_PER_GROUP)
    sel = e_logits[jnp.arange(N), g_idx[:, 0]]
    e_p, e_idx = lax.top_k(jax.nn.softmax(sel, axis=-1), TOP_K)
    e_p = e_p / jnp.sum(e_p, axis=-1, keepdims=True)
    pair_w = (g_p * e_p).reshape(-1).astype(h2d.dtype)
    pair_e = (g_idx * EXPERTS_PER_GROUP + e_idx).reshape(-1).astype(jnp.int32)
    pair_tok = jnp.repeat(jnp.arange(N, dtype=jnp.int32), TOP_K)
    P = N * TOP_K
    order = jnp.argsort(pair_e)
    se = pair_e[order]
    stok = pair_tok[order]
    sw = pair_w[order]
    counts = jnp.bincount(pair_e, length=N_EXPERTS)
    starts = jnp.cumsum(counts) - counts
    padded = ((counts + MOE_BLOCK - 1) // MOE_BLOCK) * MOE_BLOCK
    pends = jnp.cumsum(padded)
    pstarts = pends - padded
    dest = pstarts[se] + (jnp.arange(P, dtype=jnp.int32) - starts[se])
    n_blocks = P // MOE_BLOCK + N_EXPERTS + 1
    buf = jnp.zeros((n_blocks * MOE_BLOCK, h2d.shape[1]), h2d.dtype).at[dest].set(h2d[stok])
    block_start = jnp.arange(n_blocks, dtype=jnp.int32) * MOE_BLOCK
    block_e = jnp.minimum(jnp.searchsorted(pends, block_start, side='right'), N_EXPERTS - 1)

    def expert_block(args):
        xb, e = args
        return (jax.nn.silu(xb @ w_gate[e]) * (xb @ w_up[e])) @ w_down[e]

    y_buf = lax.map(expert_block, (buf.reshape(n_blocks, MOE_BLOCK, -1), block_e)).reshape(n_blocks * MOE_BLOCK, -1)
    y_pairs = y_buf[dest] * sw[:, None]
    return jax.ops.segment_sum(y_pairs, stok, num_segments=N)

def setup_inputs(seed: int = 0) -> dict:
    key = jax.random.key(seed)
    ks = jax.random.split(key, 22)

    def nrm(k, shape, scale):
        return jax.random.normal(k, shape, jnp.float32) * scale

    return {
        'x': nrm(ks[0], (BATCH, SEQ, D_MODEL), 1.0),
        'meta_tokens': nrm(ks[1], (N_META, D_MODEL), 1.0),
        'ln_emb_g': 1.0 + nrm(ks[2], (D_MODEL,), 0.02),
        'ln_emb_b': nrm(ks[3], (D_MODEL,), 0.02),
        'w_in': nrm(ks[4], (DEPTH, D_MODEL, IN_COLS), D_MODEL ** -0.5),
        'pool_w': nrm(ks[5], (DEPTH, POOL_GROUPS, POOL_CH, POOL_CH), POOL_CH ** -0.5),
        'pool_b': nrm(ks[6], (DEPTH, POOL_GROUPS, POOL_CH), 0.01),
        'pool_scale': 1.0 + nrm(ks[7], (DEPTH, POOL_WIDTH), 0.02),
        'w_out': nrm(ks[8], (DEPTH, MIX_WIDTH, D_MODEL), BETA * MIX_WIDTH ** -0.5),
        'ln1_g': 1.0 + nrm(ks[9], (DEPTH, D_MODEL), 0.02),
        'ln1_b': nrm(ks[10], (DEPTH, D_MODEL), 0.02),
        'router_group_w': nrm(ks[11], (DEPTH, D_MODEL, N_GROUPS), D_MODEL ** -0.5),
        'router_group_b': nrm(ks[12], (DEPTH, N_GROUPS), 0.01),
        'router_expert_w': nrm(ks[13], (DEPTH, D_MODEL, N_EXPERTS), D_MODEL ** -0.5),
        'router_expert_b': nrm(ks[14], (DEPTH, N_EXPERTS), 0.01),
        'expert_w_gate': nrm(ks[15], (DEPTH, N_EXPERTS, D_MODEL, D_EXPERT), D_MODEL ** -0.5),
        'expert_w_up': nrm(ks[16], (DEPTH, N_EXPERTS, D_MODEL, D_EXPERT), D_MODEL ** -0.5),
        'expert_w_down': nrm(ks[17], (DEPTH, N_EXPERTS, D_EXPERT, D_MODEL), BETA * D_EXPERT ** -0.5),
        'ln2_g': 1.0 + nrm(ks[18], (DEPTH, D_MODEL), 0.02),
        'ln2_b': nrm(ks[19], (DEPTH, D_MODEL), 0.02),
    }

def reference(x, meta_tokens, ln_emb_g, ln_emb_b, w_in, pool_w, pool_b, pool_scale, w_out,
              ln1_g, ln1_b, router_group_w, router_group_b, router_expert_w, router_expert_b,
              expert_w_gate, expert_w_up, expert_w_down, ln2_g, ln2_b):
    B = x.shape[0]
    meta = jnp.broadcast_to(meta_tokens[None].astype(x.dtype), (B, N_META, D_MODEL))
    h = jnp.concatenate([meta, x], axis=1)
    h = layer_norm(h, ln_emb_g, ln_emb_b)
    for l in range(DEPTH):
        mix = token_mixer(h, w_in[l], pool_w[l], pool_b[l], pool_scale[l], w_out[l])
        h = layer_norm(ALPHA * h + mix, ln1_g[l], ln1_b[l])
        y = hierarchical_moe(h.reshape(-1, D_MODEL), router_group_w[l], router_group_b[l],
                             router_expert_w[l], router_expert_b[l],
                             expert_w_gate[l], expert_w_up[l], expert_w_down[l]).reshape(h.shape)
        h = layer_norm(ALPHA * h + y, ln2_g[l], ln2_b[l])
    return h[:, N_META:]


_drawn_inputs = setup_inputs


def setup_inputs(seed=0):
    import zlib

    import numpy as np

    out = dict(_drawn_inputs(seed))
    spreads = {}
    factors = {'meta_tokens': 14.487,
     'pool_b': 7.91,
     'pool_scale': 5.467,
     'router_group_b': 19.037,
     'router_expert_b': 19.616,
     'ln2_g': 8.426,
     'ln2_b': 8.266,
     'ln_emb_b': 3.491}
    for name, (base, spread) in spreads.items():
        noise = np.random.default_rng([zlib.crc32(name.encode()), seed]).standard_normal(out[name].shape)
        drawn = base * np.exp(spread * noise) if base else spread * noise
        out[name] = __import__('jax').numpy.asarray(drawn.astype(out[name].dtype))
    for name, factor in factors.items():
        out[name] = (out[name] * factor).astype(out[name].dtype)
    return out
```

```python
from contextlib import ExitStack

import numpy as np

import concourse.bass as bass
from concourse import mybir

ALU = mybir.AluOpType
ACT = mybir.ActivationFunctionType
AX = mybir.AxisListType
F32 = mybir.dt.float32
BF16 = mybir.dt.bfloat16
I32 = mybir.dt.int32
U32 = mybir.dt.uint32

P = 128
D = 1024
KT = D // P
SEQ = 4096
TILES = SEQ // P
N_META = 16
HEADS = 4
DK = 64
DV = 128
HALF = DK // 2
QK = 2 * HEADS * DK
RET = HEADS * DV
POOL_WINDOWS = (2, 4, 8, 16)
GROUPS_P = len(POOL_WINDOWS)
POOL = GROUPS_P * P
IN_COLS = QK + 2 * RET + POOL
BANK = 512
N_GROUPS = 4
PER_GROUP = 8
EXPERTS = N_GROUPS * PER_GROUP
LOGITS = N_GROUPS + EXPERTS
D_E = 512
HT = D_E // P
TOP = 2
BLOCKS = SEQ * TOP // P + EXPERTS
SLOT = 2 * KT * D_E + HT * D
PART = SLOT // 3
LN_EPS = 1e-5
GN_EPS = 1e-6
ALPHA = 2 ** 0.25


def shape_constants():
    inv = np.power(10000.0, -np.arange(HALF) / HALF).astype(np.float32)
    row = np.arange(P)
    pos = (np.arange(-1, TILES)[:, None] * P + row[None, :] + N_META).astype(np.float32)
    angle = (np.maximum(pos, 0)[:, :, None] * inv).astype(np.float64)
    cos = np.cos(angle).astype(np.float32).transpose(1, 0, 2)
    sin = np.sin(angle).astype(np.float32).transpose(1, 0, 2)
    log_g = np.log1p(-np.power(2.0, -5.0 - np.arange(HEADS)))
    decay = np.concatenate([np.exp((row[:, None] + 1) * log_g), np.exp(-(row[:, None] + 1) * log_g) * DK ** -0.5], 1)
    chunk = np.exp(P * log_g)
    chunk_decay = np.stack([np.repeat(chunk[2 * p:2 * p + 2], DK) for p in range(HEADS // 2)], 1)
    j, i = row[:, None], row[None, :]
    causal = (j <= i).astype(np.float32)
    band = np.stack([((i - j >= 0) & (i - j < w)) / w - (i == j) for w in POOL_WINDOWS], 1)
    band_prev = np.stack([(i - j + P < w) / w for w in POOL_WINDOWS], 1)
    return {
        "cos": np.ascontiguousarray(cos), "sin": np.ascontiguousarray(sin),
        "decay": decay.astype(np.float32), "chunk_decay": chunk_decay.astype(np.float32),
        "causal": causal, "band": band.astype(np.float32), "band_prev": band_prev.astype(np.float32),
        "ident": np.eye(P, dtype=np.float32), "meta_rows": (row >= P - N_META).astype(np.float32)[:, None],
        "before": (j < i).astype(np.float32),
    }


class Tile:

    def __init__(self, i, k):
        self.i, self.k = i, k

    @property
    def n(self):
        return 2 * self.i + self.k

    @property
    def slot(self):
        return self.k % 2

    @property
    def half(self):
        return self.i + self.k // 2

    def __add__(self, d):
        return Tile(self.i, self.k + d)

    def __sub__(self, d):
        return Tile(self.i, self.k - d)


def run_tiles(eng, first, last, loop_from, loop_to, body):
    for t in range(first, loop_from):
        body(Tile(0, t))
    pairs = (loop_to - loop_from + 1) // 2
    with eng.Fori(0, pairs) as i:
        body(Tile(i, loop_from))
        body(Tile(i, loop_from + 1))
    for t in range(loop_to + 1, last + 1):
        body(Tile(0, t))


class Chain:

    def __init__(self, eng, sem):
        self.eng, self.sem, self.base, self.steps = eng, sem, 0, 0

    def link(self, ins, passed=None):
        ins.then_inc(self.sem, 1)
        self.steps += 1
        self.eng.wait_ge(self.sem, self.base + self.steps)
        if passed is not None:
            self.eng.sem_inc(passed, 1)


class Memory:
    def __init__(self, nc, ctx):
        self.nc, self.ctx = nc, ctx

    def sb(self, name, shape, dt):
        return self.ctx.enter_context(self.nc.sbuf_tensor(name, shape, dt))

    def ps(self, name, shape, dt):
        return self.ctx.enter_context(self.nc.psum_tensor(name, shape, dt))

    def sem(self, name):
        return self.ctx.enter_context(self.nc.semaphore(name))


def mixer(nc, a, keep):
    ctx = ExitStack()
    with ctx:
        m = Memory(nc, ctx)
        w_in = m.sb("w_in", [P, 2, KT, IN_COLS], BF16)
        w_out = m.sb("w_out", [P, 2, KT, D], BF16)
        stage = m.sb("stage", [P, 2, 2 * D], F32)
        h1 = stage[:, :, 0:D]
        h1_parts = stage[:, :, D:2 * D].bitcast(BF16)
        ln0_g, ln0_b = m.sb("ln0_g", [P, D], F32), m.sb("ln0_b", [P, D], F32)
        ln1_g, ln1_b = m.sb("ln1_g", [P, D], F32), m.sb("ln1_b", [P, D], F32)
        cos, sin = m.sb("cos_sb", [P, TILES + 1, HALF], F32), m.sb("sin_sb", [P, TILES + 1, HALF], F32)
        decay = m.sb("decay_sb", [P, 2 * HEADS], F32)
        chunk_decay = m.sb("chunk_decay_sb", [P, 2], F32)
        causal = m.sb("causal_sb", [P, P], F32)
        band, band_prev = m.sb("band_sb", [P, GROUPS_P, P], F32), m.sb("band_prev_sb", [P, GROUPS_P, P], F32)
        ident = m.sb("ident_sb", [P, P], F32)
        meta_rows = m.sb("meta_rows_sb", [P, 1], F32)
        pool_w = m.sb("pool_w_sb", [P, GROUPS_P, P], F32)
        pool_b, pool_scale = m.sb("pool_b_sb", [P, GROUPS_P], F32), m.sb("pool_scale_sb", [P, GROUPS_P], F32)
        router_w = m.sb("router_w_sb", [P, KT, LOGITS], F32)
        router_b = m.sb("router_b_sb", [P, LOGITS], F32)
        x_in = m.sb("x_in", [P, 2, D], F32)
        h = m.sb("h", [P, 2, D], F32)
        h_t = m.sb("h_t", [P, 2, D], BF16)
        mix_t = m.sb("mix_t", [P, 2, D], BF16)
        rot_a, rot_b = m.sb("rot_a", [P, QK], F32), m.sb("rot_b", [P, QK], F32)
        qk = m.sb("qk", [P, QK], F32)
        v = m.sb("v", [P, RET], F32)
        u = m.sb("u", [P, 2, POOL], F32)
        gate = m.sb("gate", [P, RET], F32)
        q_t = m.sb("q_t", [P, 2, 2, P], F32)
        k_t = m.sb("k_t", [P, 2, P], F32)
        scores = m.sb("scores", [P, HEADS, P], F32)
        state = m.sb("state", [P, 2, DV], F32)
        ret = m.sb("ret", [P, RET], F32)
        pooled_t = m.sb("pooled_t", [P, POOL], F32)
        pool_out = m.sb("pool_out", [P, POOL], F32)
        h1_t = m.sb("h1_t", [P, D], F32)
        stats = m.sb("stats", [P, 2, 2, 6], F32)
        moments = m.sb("moments", [P, 2, 2], F32)
        rstd = m.sb("rstd", [P, 2, 2], F32)
        g_stats = m.sb("g_stats", [P, HEADS, 6], F32)
        g_moments = m.sb("g_moments", [P, HEADS, 2], F32)
        g_rstd = m.sb("g_rstd", [P, 2, HEADS], F32)
        minus_half = m.sb("minus_half", [P, HEADS], F32)
        eps = m.sb("eps", [P, 2, HEADS], F32)

        bank = m.ps("bank", [P, 8, BANK], F32)
        QK_B, V_B, U_B, GATE_B, OUT_B, TR_B, TR2_B = 0, 1, 2, 3, 4, 6, 7

        weights_loaded = [m.sem(f"weights_loaded{s}") for s in range(2)]
        w_hi, w_lo = m.sem("w_hi"), m.sem("w_lo")
        params = m.sem("params")
        ready = m.sem("constants_ready")
        x_loaded = [m.sem(f"x_loaded{s}") for s in range(2)]
        stored = [m.sem(f"h1_stored{s}") for s in range(2)]
        names = ("stats0 rstd0 hdone htr hthi htlo qkdone vdone udone gatedone rotdone qkscaled vcopied ucopied "
                 "silu qktr qkt_copied bandmm band_copied scoremm masked poolmm pool_fin pool_hi pool_lo kvmm retmm "
                 "state_new gstats grstd ret_fin ret_tr ret_hi ret_lo outmm residual stats1 rstd1 h1done h1hi h1lo h1tr "
                 "h1t_copied routermm logits_done").split()
        s = {n: m.sem(n) for n in names}
        dve_chain, pool_chain, passed = m.sem("dve_chain"), m.sem("pool_chain"), m.sem("passed")
        params0 = m.sem("params0")

        FIRST, LOOP_FROM, LOOP_TO = 0, 3, TILES - 2
        block = ctx.enter_context(nc.Block())

        @block.sync
        def _(sp):
            def param(dst, src, sem=params):
                sp.dma_start(dst, src).then_inc(sem, 16)

            def load_x(t, rows=None):
                if not (isinstance(t.i, int) and t.n < 1):
                    sp.wait_ge(s["hdone"], t.n)
                src = a["x"][bass.ds(t.n * P, P), :]
                sp.dma_start(x_in[:, t.slot, :], src).then_inc(x_loaded[t.slot], 16)

            sp.wait_ge(ready, 1)
            sp.dma_start(x_in[P - N_META:P, 1, :], a["meta"]).then_inc(x_loaded[1], 16)
            load_x(Tile(0, 0))
            param(ln0_g[:], a["ln0_g"].partition_broadcast(P), params0)
            param(ln0_b[:], a["ln0_b"].partition_broadcast(P), params0)
            param(ident[:], a["ident"], params0)
            param(meta_rows[:], a["meta_rows"], params0)
            w_in_v = a["w_in"].rearrange("(k p) n -> k p n", p=P)
            w_out_v = a["w_out"].rearrange("(k two p) n -> k p two n", p=P, two=2)
            for k in range(KT + KT // 2):
                if k >= 2:
                    sp.wait_ge(w_lo, k - 1)
                if k < KT:
                    sp.dma_start(stage[:, k % 2, :], w_in_v[k]).then_inc(weights_loaded[k % 2], 16)
                else:
                    sp.dma_start(stage[:, k % 2, :].rearrange("p (two n) -> p two n", two=2),
                                 w_out_v[k - KT]).then_inc(weights_loaded[k % 2], 16)
                if k == 1:
                    param(cos[:], a["cos"])
                    param(sin[:], a["sin"])
                    for dst, name in ((decay, "decay"), (chunk_decay, "chunk_decay"), (causal, "causal"),
                                      (band, "band"), (band_prev, "band_prev"), (pool_b, "pool_b"),
                                      (pool_scale, "pool_scale")):
                        param(dst[:], a[name])
                    param(pool_w[:], a["pool_w"].rearrange("g c d -> c g d"))
                    param(ln1_g[:], a["ln1_g"].partition_broadcast(P))
                    param(ln1_b[:], a["ln1_b"].partition_broadcast(P))
                    param(router_w[:, :, 0:N_GROUPS], a["rg_w"].rearrange("(k p) n -> p k n", p=P))
                    param(router_w[:, :, N_GROUPS:], a["re_w"].rearrange("(k p) n -> p k n", p=P))
                    param(router_b[:, 0:N_GROUPS], a["rg_b"].partition_broadcast(P))
                    param(router_b[:, N_GROUPS:], a["re_b"].partition_broadcast(P))
            load_x(Tile(0, 1))
            load_x(Tile(0, 2))

            def body(t):
                static = isinstance(t.i, int)
                if not static or t.n + 3 < TILES:
                    load_x(t + 3)
                if not static or t.n >= 1:
                    p = t - 1
                    rows = bass.ds(p.n * P, P)
                    sp.wait_ge(s["h1done"], p.n + 1)
                    sp.dma_start(keep["h1_dram"][rows, :], h1[:, p.slot, :]).then_inc(stored[p.slot], 16)
                    sp.wait_ge(s["h1hi"], p.n + 1)
                    sp.wait_ge(s["h1lo"], p.n + 1)
                    sp.dma_start(keep["parts_dram"][rows, :], h1_parts[:, p.slot, :]).then_inc(stored[p.slot], 16)

            for t in range(0, 1):
                body(Tile(0, t))
            with sp.Fori(0, (TILES - 4) // 2) as i:
                body(Tile(i, 1))
                body(Tile(i, 2))
            for t in range(TILES - 3, TILES + 1):
                body(Tile(0, t))
            for slot in range(2):
                sp.wait_ge(stored[slot], TILES // 2 * 32)

        @block.gpsimd
        def _(pool):
            chain = Chain(pool, pool_chain)
            nc.gpsimd.memset(x_in[:, 1, :], 0.0).then_inc(ready, 1)
            nc.gpsimd.memset(q_t[:], 0.0).then_inc(ready, 1)
            nc.gpsimd.memset(state[:], 0.0).then_inc(ready, 1)
            nc.gpsimd.memset(minus_half[:], -0.5)
            nc.gpsimd.memset(eps[:, 0, :], LN_EPS)
            chain.link(nc.gpsimd.memset(eps[:, 1, :], GN_EPS))

            def inverse_root(out, tmp, var, eps_in, n):
                chain.link(nc.gpsimd.tensor_tensor(tmp, var, eps_in, ALU.add))
                return nc.gpsimd.tensor_tensor(out, tmp, minus_half[:, 0:n], ALU.pow)

            def ln_rstd(which, count):
                pool.wait_ge(s[f"stats{which}"], count)
                inverse_root(rstd[:, which, 0:1], rstd[:, which, 1:2], moments[:, which, 1:2],
                             eps[:, 0, 0:1], 1).then_inc(s[f"rstd{which}"], 1)

            def scale_qk(t, count):
                pool.wait_ge(s["rotdone"], count)
                nc.gpsimd.tensor_tensor(qk[:].rearrange("p (h d) -> p h d", d=DK),
                                        rot_a[:].rearrange("p (h d) -> p h d", d=DK),
                                        decay[:].unsqueeze(2).to_broadcast([P, 2 * HEADS, DK]),
                                        ALU.mult).then_inc(s["qkscaled"], 1)

            def body(t):
                static = isinstance(t.i, int)
                if not static or t.n < TILES:
                    if not static or t.n >= 0:
                        scale_qk(t, t.n + 2)
                    if not static or t.n + 1 < TILES:
                        ln_rstd(0, t.n + 3)
                if not static or t.n >= 1:
                    p = t - 1
                    ln_rstd(1, p.n + 1)
                    pool.wait_ge(s["h1done"], p.n + 1)
                    pool.wait_ge(s["h1hi"], p.n + 1)
                    nc.gpsimd.tensor_tensor(h1_parts[:, p.slot, D:], h1[:, p.slot, :], h1_parts[:, p.slot, 0:D],
                                            ALU.subtract).then_inc(s["h1lo"], 1)
                if not static or t.n < TILES:
                    pool.wait_ge(s["gstats"], t.n + 1)
                    inverse_root(g_rstd[:, 0, :], g_rstd[:, 1, :], g_moments[:, :, 1], eps[:, 1, :],
                                 HEADS).then_inc(s["grstd"], 1)

            ln_rstd(0, 1)
            ln_rstd(0, 2)
            pool.wait_ge(params, 16 * 16)
            scale_qk(Tile(0, -1), 1)
            for t in range(LOOP_FROM):
                body(Tile(0, t))
            base, STEPS = chain.steps, 3
            with pool.Fori(0, (LOOP_TO - LOOP_FROM + 1) // 2) as i:
                for k in range(2):
                    chain.base, chain.steps = base + i * (2 * STEPS) + STEPS * k, 0
                    body(Tile(i, LOOP_FROM + k))
                    assert chain.steps == STEPS
            chain.base, chain.steps = base + (LOOP_TO - LOOP_FROM + 1) * STEPS, 0
            for t in range(LOOP_TO + 1, TILES + 1):
                body(Tile(0, t))

        @block.scalar
        def _(act):
            def split_weights(ks):
                for k in ks:
                    act.wait_ge(weights_loaded[k % 2], 16 * (k // 2 + 1))
                    if k < KT:
                        dst = w_in[:, 0, k, :]
                    else:
                        dst = w_out[:, 0, 2 * (k - KT):2 * (k - KT) + 2, :].rearrange("p two n -> p (two n)")
                    nc.scalar.activation(dst, stage[:, k % 2, :], ACT.Copy).then_inc(w_hi, 1)

            def copy_out(dst, src, wait, count, done):
                act.wait_ge(s[wait], count)
                nc.scalar.activation(dst, src, ACT.Copy).then_inc(s[done], 1)

            def h_high(t):
                copy_out(h_t[:, 0, :], bank[:, TR_B:TR_B + 2, :].rearrange("p b n -> p (b n)"), "htr", t.n + 2, "hthi")

            def body(t):
                static = isinstance(t.i, int)
                main = not static or t.n < TILES
                p, pp = t - 1, t - 2
                if main:
                    act.wait_ge(s["kvmm"], t.n + 1)
                    act.wait_ge(s["retmm"], t.n) if not static or t.n > 0 else None
                    copy_out(v[:], bank[:, V_B, :], "vdone", t.n + 2, "vcopied")
                if not static or 1 <= t.n <= TILES:
                    if not static or t.n > 1:
                        act.wait_ge(s["outmm"], p.n)
                    copy_out(mix_t[:, 0, 0:RET], bank[:, TR_B, :], "ret_tr", p.n + 1, "ret_hi")
                if main:
                    if not static or t.n > 0:
                        act.wait_ge(s["bandmm"], t.n)
                    copy_out(u[:, t.slot, :], bank[:, U_B, :], "udone", t.n + 2, "ucopied")
                if not static or t.n >= 2:
                    if not static or t.n > 2:
                        act.wait_ge(s["routermm"], pp.n)
                    copy_out(h1_t[:], bank[:, OUT_B:OUT_B + 2, :].rearrange("p b n -> p (b n)"), "h1tr", pp.n + 1,
                             "h1t_copied")
                if main:
                    act.wait_ge(s["gatedone"], t.n + 1)
                    if not static or t.n > 0:
                        act.wait_ge(s["ret_fin"], t.n)
                    nc.scalar.activation(gate[:], bank[:, GATE_B, :], ACT.Silu).then_inc(s["silu"], 1)
                    act.wait_ge(s["qktr"], t.n + 1)
                    pairs = bank[:, TR_B, :].rearrange("p (j n) -> p j n", j=4)
                    nc.scalar.activation(k_t[:], pairs[:, 2:4, :], ACT.Copy).then_inc(s["qkt_copied"], 1)
                    nc.scalar.activation(q_t[0:DK, 0, :, :], pairs[0:DK, 0:2, :], ACT.Copy).then_inc(s["qkt_copied"], 1)
                    nc.scalar.activation(q_t[DK:P, 1, :, :], pairs[DK:P, 0:2, :], ACT.Copy).then_inc(s["qkt_copied"], 1)
                    copy_out(pooled_t[:], bank[:, TR2_B, :], "bandmm", t.n + 1, "band_copied")
                    copy_out(mix_t[:, 0, RET:], pool_out[:], "pool_fin", t.n + 1, "pool_hi")
                    if not static or t.n + 1 < TILES:
                        h_high(t + 1)
                if not static or 1 <= t.n <= TILES:
                    act.wait_ge(s["h1done"], p.n + 1)
                    if not static or t.n > 2:
                        act.wait_ge(stored[p.slot], 32 * p.half)
                    nc.scalar.activation(h1_parts[:, p.slot, 0:D], h1[:, p.slot, :], ACT.Copy).then_inc(s["h1hi"], 1)

            split_weights(range(KT))
            h_high(Tile(0, -1))
            split_weights(range(KT, KT + KT // 2))
            copy_out(v[:], bank[:, V_B, :], "vdone", 1, "vcopied")
            copy_out(u[:, 1, :], bank[:, U_B, :], "udone", 1, "ucopied")
            h_high(Tile(0, 0))
            act.wait_ge(ready, 3)
            run_tiles(act, FIRST, TILES + 1, LOOP_FROM, LOOP_TO, body)

        @block.vector
        def _(dve):
            chain = Chain(dve, dve_chain)

            def low(dst, full, high, wait, count, done):
                dve.wait_ge(s[wait], count)
                nc.vector.tensor_tensor(dst, full, high, ALU.subtract).then_inc(s[done], 1)

            def split_weights(ks):
                for k in ks:
                    if k < KT:
                        hi, lo = w_in[:, 0, k, :], w_in[:, 1, k, :]
                    else:
                        j = 2 * (k - KT)
                        hi, lo = (w_out[:, q, j:j + 2, :].rearrange("p two n -> p (two n)") for q in range(2))
                    dve.wait_ge(weights_loaded[k % 2], 16 * (k // 2 + 1))
                    dve.wait_ge(w_hi, k + 1)
                    nc.vector.tensor_tensor(lo, stage[:, k % 2, :], hi, ALU.subtract).then_inc(w_lo, 1)

            def ln_stats(which, src):
                nc.vector.bn_stats(stats[:, which, 0, :], src[:, 0:BANK])
                chain.link(nc.vector.bn_stats(stats[:, which, 1, :], src[:, BANK:D]), passed)
                return nc.vector.bn_aggr(moments[:, which, :], stats[:, which, :, :])

            def ln_apply(which, dst, src, g, b):
                chain.link(nc.vector.scalar_tensor_tensor(out=dst, in0=src, scalar=moments[:, which, 0:1], in1=g,
                                                          op0=ALU.subtract, op1=ALU.mult))
                return nc.vector.scalar_tensor_tensor(out=dst, in0=dst, scalar=rstd[:, which, 0:1], in1=b,
                                                      op0=ALU.mult, op1=ALU.add)

            def ln0_stats(t):
                dve.wait_ge(x_loaded[t.slot], 16 * ((t + 1).half + 1))
                ln_stats(0, x_in[:, t.slot, :]).then_inc(s["stats0"], 1)

            def ln0_apply(t):
                dve.wait_ge(s["rstd0"], t.n + 2)
                ins = ln_apply(0, h[:, t.slot, :], x_in[:, t.slot, :], ln0_g[:], ln0_b[:])
                return ins

            def rotate(t):
                dve.wait_ge(s["qkdone"], t.n + 2)
                if not (isinstance(t.i, int) and t.n < 0):
                    dve.wait_ge(s["qkscaled"], t.n + 1)
                x = bank[:, QK_B, :].rearrange("p (h s f) -> p h s f", s=2, f=HALF)
                o = rot_a[:].rearrange("p (h s f) -> p h s f", s=2, f=HALF)
                o2 = rot_b[:].rearrange("p (h s f) -> p h s f", s=2, f=HALF)
                c = cos[:, bass.ds(t.n + 1, 1), :].to_broadcast([P, 2 * HEADS, HALF])
                sn = sin[:, bass.ds(t.n + 1, 1), :].to_broadcast([P, 2 * HEADS, HALF])
                nc.vector.tensor_tensor(o[:, :, 0, :], x[:, :, 0, :], c, ALU.mult)
                nc.vector.tensor_tensor(o[:, :, 1, :], x[:, :, 1, :], c, ALU.mult)
                nc.vector.tensor_tensor(o2[:, :, 0, :], x[:, :, 1, :], sn, ALU.mult)
                chain.link(nc.vector.tensor_tensor(o2[:, :, 1, :], x[:, :, 0, :], sn, ALU.mult))
                nc.vector.tensor_tensor(o[:, :, 0, :], o[:, :, 0, :], o2[:, :, 0, :], ALU.subtract)
                nc.vector.tensor_tensor(o[:, :, 1, :], o[:, :, 1, :], o2[:, :, 1, :], ALU.add).then_inc(s["rotdone"], 1)

            def h_low(t):
                low(h_t[:, 1, :], bank[:, TR_B:TR_B + 2, :].rearrange("p b n -> p (b n)"), h_t[:, 0, :], "hthi",
                    t.n + 2, "htlo")

            def new_state(t):
                dve.wait_ge(s["kvmm"], t.n + 2)
                if not (isinstance(t.i, int) and t.n < 0):
                    dve.wait_ge(s["retmm"], t.n + 1)
                chain.link(nc.vector.tensor_tensor(state[:], state[:],
                                                   bank[:, GATE_B, 0:2 * DV].rearrange("p (j n) -> p j n", j=2), ALU.add))
                nc.vector.tensor_tensor(state[:], state[:], chunk_decay[:].unsqueeze(2).to_broadcast([P, 2, DV]),
                                        ALU.mult).then_inc(s["state_new"], 1)

            def body(t):
                static = isinstance(t.i, int)
                main = not static or t.n < TILES
                p, pp = t - 1, t - 2
                if main:
                    rotate(t)
                if not static or 1 <= t.n <= TILES:
                    low(mix_t[:, 1, 0:RET], bank[:, TR_B, :], mix_t[:, 0, 0:RET], "ret_hi", p.n + 1, "ret_lo")
                if not static or t.n + 1 < TILES:
                    ln0_stats(t + 1)
                if not static or t.n >= 2:
                    dve.wait_ge(s["routermm"], pp.n + 1)
                    nc.vector.tensor_tensor(keep["logits"][:, bass.ds(pp.n, 1), :], bank[:, TR2_B, 0:LOGITS].unsqueeze(1),
                                            router_b[:].unsqueeze(1), ALU.add).then_inc(s["logits_done"], 1)
                if not static or 1 <= t.n <= TILES:
                    dve.wait_ge(s["outmm"], p.n + 1)
                    if not static or t.n > 2:
                        dve.wait_ge(stored[p.slot], 32 * p.half)
                        dve.wait_ge(s["h1tr"], p.n - 1)
                    chain.link(nc.vector.scalar_tensor_tensor(
                        out=h1[:, p.slot, :], in0=h[:, p.slot, :], scalar=ALPHA,
                        in1=bank[:, OUT_B:OUT_B + 2, :].rearrange("p b n -> p (b n)"), op0=ALU.mult, op1=ALU.add))
                    ln_stats(1, h1[:, p.slot, :]).then_inc(s["stats1"], 1)
                if not static or t.n + 1 < TILES:
                    ln0_apply(t + 1).then_inc(s["hdone"], 1)
                if main:
                    dve.wait_ge(s["scoremm"], t.n + 1)
                    nc.vector.tensor_tensor(scores[:], bank[:, QK_B, :].rearrange("p (h n) -> p h n", h=HEADS),
                                            causal[:].unsqueeze(1).to_broadcast([P, HEADS, P]),
                                            ALU.mult).then_inc(s["masked"], 1)
                    dve.wait_ge(s["poolmm"], t.n + 1)
                    if not static or t.n > 0:
                        dve.wait_ge(s["pool_lo"], t.n)
                    for g in range(GROUPS_P):
                        cols = slice(g * P, (g + 1) * P)
                        ins = nc.vector.tensor_scalar(pool_out[:, cols], bank[:, V_B, cols], pool_b[:, g:g + 1],
                                                      pool_scale[:, g:g + 1], ALU.add, ALU.mult)
                    ins.then_inc(s["pool_fin"], 1)
                if not static or 1 <= t.n <= TILES:
                    dve.wait_ge(s["rstd1"], p.n + 1)
                    ln_apply(1, h1[:, p.slot, :], h1[:, p.slot, :], ln1_g[:], ln1_b[:]).then_inc(s["h1done"], 1)
                if main:
                    dve.wait_ge(s["retmm"], t.n + 1)
                    for hd in range(HEADS):
                        ins = nc.vector.bn_stats(g_stats[:, hd, :], bank[:, U_B, hd * DV:(hd + 1) * DV])
                    chain.link(ins, passed)
                    for hd in range(HEADS):
                        ins = nc.vector.bn_aggr(g_moments[:, hd, :], g_stats[:, hd, :])
                    ins.then_inc(s["gstats"], 1)
                    new_state(t)
                    low(mix_t[:, 1, RET:], pool_out[:], mix_t[:, 0, RET:], "pool_hi", t.n + 1, "pool_lo")
                    if not static or t.n + 1 < TILES:
                        h_low(t + 1)
                    dve.wait_ge(s["grstd"], t.n + 1)
                    if not static or t.n > 0:
                        dve.wait_ge(s["ret_tr"], t.n)
                    for hd in range(HEADS):
                        cols = slice(hd * DV, (hd + 1) * DV)
                        ins = nc.vector.tensor_scalar(ret[:, cols], bank[:, U_B, cols], g_moments[:, hd, 0:1],
                                                      g_rstd[:, 0, hd:hd + 1], ALU.subtract, ALU.mult)
                    chain.link(ins)
                    dve.wait_ge(s["silu"], t.n + 1)
                    nc.vector.tensor_tensor(ret[:], ret[:], gate[:], ALU.mult).then_inc(s["ret_fin"], 1)

            dve.wait_ge(ready, 3)
            dve.wait_ge(params0, 16 * 4)
            ln0_stats(Tile(0, -1))
            chain.link(ln0_apply(Tile(0, -1)))
            nc.vector.tensor_scalar(h[:, 1, :], h[:, 1, :], meta_rows[:, 0:1], None, ALU.mult).then_inc(s["hdone"], 1)
            split_weights(range(KT))
            h_low(Tile(0, -1))
            ln0_stats(Tile(0, 0))
            ln0_apply(Tile(0, 0)).then_inc(s["hdone"], 1)
            split_weights(range(KT, KT + KT // 2))
            dve.wait_ge(params, 16 * 16)
            rotate(Tile(0, -1))
            new_state(Tile(0, -1))
            h_low(Tile(0, 0))
            for t in range(LOOP_FROM):
                body(Tile(0, t))
            base, STEPS = chain.steps, 9
            with dve.Fori(0, (LOOP_TO - LOOP_FROM + 1) // 2) as i:
                for k in range(2):
                    chain.base, chain.steps = base + i * (2 * STEPS) + STEPS * k, 0
                    body(Tile(i, LOOP_FROM + k))
                    assert chain.steps == STEPS, chain.steps
            chain.base, chain.steps = base + (LOOP_TO - LOOP_FROM + 1) * STEPS, 0
            for t in range(LOOP_TO + 1, TILES + 2):
                body(Tile(0, t))

        @block.tensor
        def _(pe):
            def three_passes(dst, lhs, rhs, kts, done):
                last = kts - 1
                for k in range(kts):
                    nc.tensor.matmul(dst, lhs(0, k), rhs(0, k), start=k == 0, stop=False)
                    nc.tensor.matmul(dst, lhs(0, k), rhs(1, k), start=False, stop=False)
                for k in range(kts):
                    ins = nc.tensor.matmul(dst, lhs(1, k), rhs(0, k), start=False, stop=k == last)
                if done is not None:
                    ins.then_inc(s[done], 1)

            def transpose_h(t):
                pe.wait_ge(s["hdone"], t.n + 2)
                if not (isinstance(t.i, int) and t.n < 0):
                    pe.wait_ge(s["htlo"], t.n + 1)
                if not (isinstance(t.i, int) and t.n < 1):
                    pe.wait_ge(s["qkt_copied"], 3 * t.n)
                    pe.wait_ge(s["band_copied"], t.n)
                for k in range(KT):
                    ins = nc.tensor.transpose(bank[:, TR_B + k // 4, (k % 4) * P:(k % 4 + 1) * P],
                                              h[:, t.slot, k * P:(k + 1) * P], ident[:])
                ins.then_inc(s["htr"], 1)

            def project(b, col, done):
                three_passes(bank[:, b, :], lambda q, k: h_t[:, q, k * P:(k + 1) * P],
                             lambda q, k: w_in[:, q, k, col:col + BANK], KT, done)

            def kv_products(t):
                pe.wait_ge(s["qkscaled"], t.n + 2)
                pe.wait_ge(s["vcopied"], t.n + 2)
                for hd in range(HEADS):
                    r, j = hd % 2, hd // 2
                    ins = nc.tensor.matmul(bank[r * DK:(r + 1) * DK, GATE_B, j * DV:(j + 1) * DV],
                                           qk[:, (HEADS + hd) * DK:(HEADS + hd + 1) * DK],
                                           v[:, hd * DV:(hd + 1) * DV], start=True, stop=True)
                ins.then_inc(s["kvmm"], 1)

            def body(t):
                static = isinstance(t.i, int)
                main = not static or t.n < TILES
                p, pp = t - 1, t - 2
                if main:
                    pe.wait_ge(s["htlo"], t.n + 2)
                    if not static or t.n > 0:
                        pe.wait_ge(s["masked"], t.n)
                    project(QK_B, 0, "qkdone")
                    if not static or t.n > 0:
                        pe.wait_ge(s["pool_fin"], t.n)
                    project(V_B, QK, "vdone")
                if not static or 1 <= t.n <= TILES:
                    pe.wait_ge(s["ret_fin"], p.n + 1)
                    for k in range(HEADS):
                        ins = nc.tensor.transpose(bank[:, TR_B, k * P:(k + 1) * P], ret[:, k * P:(k + 1) * P], ident[:])
                    ins.then_inc(s["ret_tr"], 1)
                if main:
                    if static and t.n == 0:
                        pe.wait_ge(s["ucopied"], 1)
                    project(U_B, QK + 2 * RET, "udone")
                if not static or t.n >= 2:
                    pe.wait_ge(s["h1done"], pp.n + 1)
                    for k in range(KT):
                        ins = nc.tensor.transpose(bank[:, OUT_B + k // 4, (k % 4) * P:(k % 4 + 1) * P],
                                                  h1[:, pp.slot, k * P:(k + 1) * P], ident[:])
                    ins.then_inc(s["h1tr"], 1)
                if main:
                    pe.wait_ge(s["state_new"], t.n + 1)
                    project(GATE_B, QK + RET, "gatedone")
                if not static or t.n >= 2:
                    pe.wait_ge(s["h1t_copied"], pp.n + 1)
                    for k in range(KT):
                        ins = nc.tensor.matmul(bank[:, TR2_B, 0:LOGITS], h1_t[:, k * P:(k + 1) * P], router_w[:, k, :],
                                               start=k == 0, stop=k == KT - 1)
                    ins.then_inc(s["routermm"], 1)
                if not static or 1 <= t.n <= TILES:
                    pe.wait_ge(s["ret_lo"], p.n + 1)
                    pe.wait_ge(s["pool_lo"], p.n + 1)
                    for half in range(2):
                        three_passes(bank[:, OUT_B + half, :], lambda q, k: mix_t[:, q, k * P:(k + 1) * P],
                                     lambda q, k: w_out[:, q, k, half * BANK:(half + 1) * BANK], KT,
                                     "outmm" if half else None)
                if main:
                    pe.wait_ge(s["qkscaled"], t.n + 2)
                    for j in range(4):
                        ins = nc.tensor.transpose(bank[:, TR_B, j * P:(j + 1) * P], qk[:, j * P:(j + 1) * P], ident[:])
                    ins.then_inc(s["qktr"], 1)
                    pe.wait_ge(s["ucopied"], t.n + 2)
                    if not static or t.n >= 2:
                        pe.wait_ge(s["logits_done"], pp.n + 1)
                    for g in range(GROUPS_P):
                        cols = slice(g * P, (g + 1) * P)
                        nc.tensor.matmul(bank[:, TR2_B, cols], u[:, t.slot, cols], band[:, g, :], start=True, stop=False)
                        ins = nc.tensor.matmul(bank[:, TR2_B, cols], u[:, p.slot, cols], band_prev[:, g, :],
                                               start=False, stop=True)
                    ins.then_inc(s["bandmm"], 1)
                    pe.wait_ge(s["qkt_copied"], 3 * t.n + 3)
                    pe.wait_ge(s["rotdone"], t.n + 2)
                    for hd in range(HEADS):
                        ins = nc.tensor.matmul(bank[:, QK_B, hd * P:(hd + 1) * P], k_t[:, hd // 2, :],
                                               q_t[:, hd % 2, hd // 2, :], start=True, stop=True)
                    ins.then_inc(s["scoremm"], 1)
                    pe.wait_ge(s["silu"], t.n + 1)
                    kv_products(t)
                    pe.wait_ge(s["band_copied"], t.n + 1)
                    for g in range(GROUPS_P):
                        cols = slice(g * P, (g + 1) * P)
                        ins = nc.tensor.matmul(bank[:, V_B, cols], pool_w[:, g, :], pooled_t[:, cols],
                                               start=True, stop=True)
                    ins.then_inc(s["poolmm"], 1)
                    pe.wait_ge(s["masked"], t.n + 1)
                    for hd in range(HEADS):
                        cols = slice(hd * DV, (hd + 1) * DV)
                        nc.tensor.matmul(bank[:, U_B, cols], scores[:, hd, :], v[:, cols], start=True, stop=False)
                        ins = nc.tensor.matmul(bank[:, U_B, cols], q_t[:, hd % 2, hd // 2, :],
                                               state[:, hd // 2, :], start=False, stop=True)
                    ins.then_inc(s["retmm"], 1)
                    if not static or t.n + 1 < TILES:
                        transpose_h(t + 1)

            pe.wait_ge(params0, 16 * 4)
            transpose_h(Tile(0, -1))
            pe.wait_ge(w_lo, KT)
            pe.wait_ge(s["htlo"], 1)
            project(QK_B, 0, "qkdone")
            project(V_B, QK, "vdone")
            project(U_B, QK + 2 * RET, "udone")
            kv_products(Tile(0, -1))
            transpose_h(Tile(0, 0))
            pe.wait_ge(w_lo, KT + KT // 2)
            pe.wait_ge(params, 16 * 16)
            run_tiles(pe, FIRST, TILES + 1, LOOP_FROM, LOOP_TO, body)


def router(nc, a, keep):
    ctx = ExitStack()
    with ctx:
        m = Memory(nc, ctx)
        T, G, J, E = TILES, N_GROUPS, PER_GROUP, EXPERTS
        logits = keep["logits"]
        iota = m.sb("iota", [P, P], F32)
        top = m.sb("top", [P, T], F32)
        g_first = m.sb("g_first", [P, T], F32)
        g_exp = m.sb("g_exp", [P, T, G], F32)
        g_cand = m.sb("g_cand", [P, T, G], F32)
        g_prob = m.sb("g_prob", [P, T], F32)
        sel = m.sb("sel", [P, T, J], F32)
        prod = m.sb("prod", [P, T, J], F32)
        cand = m.sb("cand", [P, T, J], F32)
        one_hot = m.sb("one_hot8", [P, T, J], F32)
        best = m.sb("best", [P, 2, T], F32)
        place = m.sb("place", [P, 2, T], F32)
        ratio = m.sb("ratio", [P, T], F32)
        share = m.sb("share", [P, T], F32)
        expert = m.sb("expert", [P, 2, T], F32)
        member = m.sb("member", [P, 2, T, E], F32)
        both = m.sb("both", [P, T, E], F32)
        before = m.sb("before_sb", [P, P], F32)
        ones = m.sb("ones", [P, P], F32)
        count_et = m.sb("count_et", [P, E, T], F32)
        incl_et = m.sb("incl_et", [P, E, T], F32)
        keep_going = m.sb("keep_going", [P, E, T], F32)
        padded = m.sb("padded", [P, E], F32)
        padded_i = m.sb("padded_i", [P, E], I32)
        ends = m.sb("ends", [P, E], F32)
        starts = m.sb("starts", [P, E], F32)
        rank = m.sb("rank", [P, T, E], F32)
        hit = m.sb("hit", [P, T, E], F32)
        dest = m.sb("dest", [P, 2, T], F32)
        dest_i = m.sb("dest_i", [P, 2, T], I32)
        lane = m.sb("lane", [P, 2, T], F32)
        lane_i = m.sb("lane_i", [P, 2, T], I32)
        dblock = m.sb("dblock", [P, 2, T], F32)
        token_no = m.sb("token_no", [P, T], F32)
        lane_hot = m.sb("lane_hot", [P, 2, P], F32)
        block_hot = m.sb("block_hot", [P, 2, BLOCKS], F32)
        tokens_f = m.sb("tokens_f", [P, BLOCKS], F32)
        full = m.sb("full", [1, BLOCKS, E], F32)
        of_block = m.sb("of_block", [1, BLOCKS], F32)
        slot_of = m.sb("slot_of", [1, BLOCKS], F32)
        slot_i = m.sb("slot_i", [1, BLOCKS], I32)
        bank = m.ps("rbank", [P, 8, BANK], F32)
        step, act_step, pe_step, made, loaded = (m.sem(n) for n in ("r_dve", "r_act", "r_pe", "r_made", "r_loaded"))
        hot_made, hot_used = m.sem("hot_made"), m.sem("hot_used")
        block = ctx.enter_context(nc.Block())
        BIG = 1e9

        @block.sync
        def _(sp):
            sp.dma_start(before[:], a["before"]).then_inc(loaded, 16)

        @block.gpsimd
        def _(pool):
            nc.gpsimd.iota(iota[:], pattern=[[1, P]], base=0, channel_multiplier=0,
                           allow_small_or_imprecise_dtypes=True).then_inc(made, 1)
            nc.gpsimd.iota(token_no[:], pattern=[[P, T]], base=0, channel_multiplier=1,
                           allow_small_or_imprecise_dtypes=True).then_inc(made, 1)
            nc.gpsimd.memset(ones[:], 1.0).then_inc(made, 1)
            nc.gpsimd.memset(keep_going[:], 1.0).then_inc(made, 1)

        mark = {}

        @block.vector
        def _(dve):
            chain = Chain(dve, step)
            L = chain.link
            wide = lambda x, n: x.unsqueeze(2).to_broadcast([P, T, n])
            along = lambda n: iota[:, 0:n].unsqueeze(1).to_broadcast([P, T, n])
            dve.wait_ge(made, 4)

            def first_max(values, n, top_out, first_out, cand_t):
                L(nc.vector.tensor_reduce(top_out, values, AX.X, ALU.max))
                L(nc.vector.tensor_tensor(cand_t, values, wide(top_out, n), ALU.is_lt))
                L(nc.vector.scalar_tensor_tensor(out=cand_t, in0=cand_t, scalar=BIG, in1=along(n), op0=ALU.mult,
                                                 op1=ALU.add))
                L(nc.vector.tensor_reduce(first_out, cand_t, AX.X, ALU.min))

            g_logits = logits[:, :, 0:G]
            first_max(g_logits, G, top[:], g_first[:], g_cand[:])
            L(nc.vector.tensor_tensor(g_exp[:], g_logits, wide(top[:], G), ALU.subtract))
            mark["g_shifted"] = chain.steps
            for g in range(G):
                L(nc.vector.tensor_scalar(share[:], g_first[:], float(g), None, ALU.is_equal))
                dst = sel if g == 0 else prod
                L(nc.vector.tensor_tensor(dst[:], logits[:, :, G + g * J:G + (g + 1) * J], wide(share[:], J), ALU.mult))
                if g:
                    L(nc.vector.tensor_tensor(sel[:], sel[:], prod[:], ALU.add))
            first_max(sel[:], J, best[:, 0, :], place[:, 0, :], cand[:])
            L(nc.vector.tensor_tensor(one_hot[:], along(J), wide(place[:, 0, :], J), ALU.is_equal))
            L(nc.vector.scalar_tensor_tensor(out=prod[:], in0=one_hot[:], scalar=-3e38, in1=sel[:], op0=ALU.mult,
                                             op1=ALU.add))
            first_max(prod[:], J, best[:, 1, :], place[:, 1, :], cand[:])
            L(nc.vector.tensor_tensor(ratio[:], best[:, 1, :], best[:, 0, :], ALU.subtract))
            mark["ratio"] = chain.steps
            for k in range(2):
                L(nc.vector.scalar_tensor_tensor(out=expert[:, k, :], in0=g_first[:], scalar=float(J),
                                                 in1=place[:, k, :], op0=ALU.mult, op1=ALU.add))
                L(nc.vector.tensor_tensor(member[:, k, :, :], along(E), wide(expert[:, k, :], E), ALU.is_equal))
            L(nc.vector.tensor_tensor(both[:], member[:, 0, :, :], member[:, 1, :, :], ALU.add))
            mark["both"] = chain.steps
            dve.wait_ge(act_step, 1)
            L(nc.vector.tensor_reduce(g_prob[:], g_exp[:], AX.X, ALU.add))
            L(nc.vector.reciprocal(g_prob[:], g_prob[:]))
            dve.wait_ge(act_step, 2)
            L(nc.vector.tensor_scalar(share[:], ratio[:], 1.0, None, ALU.add))
            L(nc.vector.reciprocal(share[:], share[:]))
            L(nc.vector.tensor_tensor(keep["pair_w"][:, 0, :], g_prob[:], share[:], ALU.mult))
            L(nc.vector.tensor_tensor(keep["pair_w"][:, 1, :], keep["pair_w"][:, 0, :], ratio[:], ALU.mult))
            dve.wait_ge(pe_step, 1)
            for b in range(2):
                tt = slice(b * T // 2, (b + 1) * T // 2)
                L(nc.vector.tensor_copy(count_et[:, :, tt].rearrange("p e t -> p t e"),
                                        bank[:, b, :].rearrange("p (t e) -> p t e", e=E)))
            L(nc.vector.tensor_scalar(keep_going[:, :, 0:1], keep_going[:, :, 0:1], 0.0, None, ALU.mult))
            flat = lambda x: x[:].rearrange("p e t -> p (e t)")
            L(nc.vector.tensor_tensor_scan(flat(incl_et), flat(keep_going), flat(count_et), 0.0, ALU.mult, ALU.add))
            L(nc.vector.tensor_scalar(padded_i[:], incl_et[:, :, T - 1], float(P - 1), None, ALU.add))
            L(nc.vector.tensor_scalar(padded_i[:], padded_i[:], 7, None, ALU.logical_shift_right))
            L(nc.vector.tensor_scalar(padded[:], padded_i[:], 1.0, None, ALU.max))
            L(nc.vector.tensor_tensor_scan(ends[:], ones[:, 0:E], padded[:], 0.0, ALU.mult, ALU.add))
            L(nc.vector.tensor_copy(keep["ends"][:], ends[0:1, :]))
            L(nc.vector.tensor_tensor(starts[:], ends[:], padded[:], ALU.subtract))
            L(nc.vector.tensor_tensor(count_et[:], incl_et[:], count_et[:], ALU.subtract))
            L(nc.vector.scalar_tensor_tensor(out=count_et[:], in0=starts[:].unsqueeze(2).to_broadcast([P, E, T]),
                                             scalar=float(P), in1=count_et[:], op0=ALU.mult, op1=ALU.add))
            dve.wait_ge(pe_step, 2)
            for b in range(2):
                tt = slice(b * T // 2, (b + 1) * T // 2)
                L(nc.vector.tensor_tensor(rank[:, tt, :], bank[:, 2 + b, :].rearrange("p (t e) -> p t e", e=E),
                                          count_et[:, :, tt].rearrange("p e t -> p t e"), ALU.add))
            for k in range(2):
                L(nc.vector.tensor_tensor(hit[:], rank[:], member[:, k, :, :], ALU.mult))
                L(nc.vector.tensor_reduce(dest[:, k, :], hit[:], AX.X, ALU.add))
            L(nc.vector.tensor_copy(dest_i[:], dest[:]))
            L(nc.vector.tensor_copy(keep["dest"][:], dest[:]))
            L(nc.vector.tensor_scalar(lane_i[:], dest_i[:], P - 1, None, ALU.bitwise_and))
            L(nc.vector.tensor_copy(lane[:], lane_i[:]))
            L(nc.vector.tensor_tensor(dblock[:], dest[:], lane[:], ALU.subtract))
            L(nc.vector.tensor_scalar(dblock[:], dblock[:], 1.0 / P, None, ALU.mult))
            L(nc.vector.tensor_tensor(full[:], iota[0:1, 0:BLOCKS].unsqueeze(2).to_broadcast([1, BLOCKS, E]),
                                      ends[0:1, :].unsqueeze(1).to_broadcast([1, BLOCKS, E]), ALU.is_ge))
            L(nc.vector.tensor_reduce(of_block[:], full[:], AX.X, ALU.add))
            L(nc.vector.tensor_scalar(of_block[:], of_block[:], float(E - 1), None, ALU.min))
            L(nc.vector.tensor_copy(slot_i[:], of_block[:]))
            L(nc.vector.tensor_scalar(slot_i[:], slot_i[:], 1, None, ALU.bitwise_and))
            L(nc.vector.tensor_scalar(keep["block_part"][:], of_block[:], 3.0, None, ALU.mult))
            L(nc.vector.tensor_scalar(keep["block_slot"][:], slot_i[:], float(SLOT), None, ALU.mult))
            for n in range(2 * T):
                k, t = n // T, n % T
                if n >= 2:
                    dve.wait_ge(hot_used, n - 1)
                nc.vector.tensor_scalar(lane_hot[:, n % 2, :], iota[:], lane[:, k, t:t + 1], None, ALU.is_equal)
                nc.vector.tensor_scalar(block_hot[:, n % 2, :], iota[:, 0:BLOCKS], dblock[:, k, t:t + 1],
                                        token_no[:, t:t + 1], ALU.is_equal, ALU.mult).then_inc(hot_made, 1)
            dve.wait_ge(pe_step, 3)
            nc.vector.tensor_copy(keep["tokens"][:], bank[:, 4, 0:BLOCKS])

        @block.scalar
        def _(act):
            act.wait_ge(step, mark["g_shifted"])
            nc.scalar.activation(g_exp[:], g_exp[:], ACT.Exp).then_inc(act_step, 1)
            act.wait_ge(step, mark["ratio"])
            nc.scalar.activation(ratio[:], ratio[:], ACT.Exp).then_inc(act_step, 1)

        @block.tensor
        def _(pe):
            pe.wait_ge(loaded, 16)
            pe.wait_ge(step, mark["both"])
            flat = both[:].rearrange("p t e -> p (t e)")
            for b in range(2):
                ins = nc.tensor.matmul(bank[:, b, :], ones[:], flat[:, b * BANK:(b + 1) * BANK], start=True, stop=True)
            ins.then_inc(pe_step, 1)
            for b in range(2):
                ins = nc.tensor.matmul(bank[:, 2 + b, :], before[:], flat[:, b * BANK:(b + 1) * BANK], start=True, stop=True)
            ins.then_inc(pe_step, 1)
            for n in range(2 * T):
                pe.wait_ge(hot_made, n + 1)
                nc.tensor.matmul(bank[:, 4, 0:BLOCKS], lane_hot[:, n % 2, :], block_hot[:, n % 2, :],
                                 start=n == 0, stop=n == 2 * T - 1).then_inc(hot_used, 1)
            pe.wait_ge(hot_used, 2 * T)
            pe.sem_inc(pe_step, 1)


def experts(nc, a, keep):
    ctx = ExitStack()
    with ctx:
        m = Memory(nc, ctx)
        raw = m.sb("raw", [P, 2 * SLOT], F32)
        w_lo = m.sb("w_low", [P, 2 * SLOT], BF16)
        w_hi = raw[:].bitcast(BF16)
        xg = m.sb("xg", [P, 2, 2 * D], BF16)
        x_t = m.sb("x_t", [P, 2, 2 * D], BF16)
        silu_g = m.sb("silu_g", [P, D_E], F32)
        up = m.sb("up", [P, D_E], F32)
        hid = m.sb("hid", [P, D_E], F32)
        hid_parts = m.sb("hid_parts", [P, 2, D_E], BF16)
        hid_t = m.sb("hid_t", [P, 2 * D_E], BF16)
        y = m.sb("y", [P, 2, D], F32)
        index = m.sb("index", [P, 2], U32)
        ident = m.sb("ident_b", [P, P], BF16)
        ident_f = m.sb("ident_f", [P, P], F32)
        GATE_B, UP_B, Y_B = 0, 1, 2
        bank = m.ps("ebank", [P, 4, BANK], F32)
        xtr = m.ps("xtr", [P, 2 * D], BF16)
        htr = m.ps("htr", [P, 2 * D_E], BF16)
        s = {n: m.sem("e_" + n) for n in ("xtr xt_copied gate up silu upcopied hid hidhi hidlo htr ht_copied "
                                          "down ycopied low indexed gone").split()}
        w_loaded = [[m.sem(f"w_loaded{i}{j}") for j in range(3)] for i in range(2)]
        gathered = [m.sem(f"gathered{i}") for i in range(2)]
        stored = [m.sem(f"y_stored{i}") for i in range(2)]
        ready, id_loaded, id_made = m.sem("e_ready"), m.sem("e_id_loaded"), m.sem("e_id_made")
        block = ctx.enter_context(nc.Block())

        @block.sync
        def _(sp):
            sp.dma_start(ident_f[:], a["ident"]).then_inc(id_loaded, 16)
            srcs = [a["w_gate"].rearrange("e (k p) n -> e p k n", p=P), a["w_up"].rearrange("e (k p) n -> e p k n", p=P),
                    a["w_down"].rearrange("e (k p) n -> e p k n", p=P)]

            def load(e):
                for part in range(3):
                    width = D if part == 2 else D_E
                    dst = raw[:, e.slot * SLOT + part * PART:e.slot * SLOT + (part + 1) * PART]
                    sp.dma_start(dst.rearrange("p (k n) -> p k n", n=width),
                                 srcs[part][bass.ds(e.n, 1), :, :, :].squeeze(0)).then_inc(w_loaded[e.slot][part], 16)

            load(Tile(0, 0))
            load(Tile(0, 1))
            with sp.Fori(0, EXPERTS // 2 - 1) as i:
                for k in range(2):
                    e = Tile(i, 2 + k)
                    end = sp.value_load(keep["ends"][0:1, bass.ds((e - 2).n, 1)], min_val=1, max_val=BLOCKS)
                    sp.wait_ge(s["down"], end)
                    load(e)

        @block.vector
        def _(dve):
            dve.wait_ge(id_loaded, 16)
            nc.vector.tensor_copy(ident[:], ident_f[:]).then_inc(id_made, 1)
            with dve.Fori(0, EXPERTS // 2) as i:
                for slot in range(2):
                    for part in range(3):
                        a0 = slot * SLOT + part * PART
                        dve.wait_ge(w_loaded[slot][part], 16 * i + 16)
                        nc.vector.tensor_tensor(w_lo[:, a0:a0 + PART], raw[:, a0:a0 + PART],
                                                w_hi[:, 2 * a0 + 1:2 * (a0 + PART):2], ALU.subtract).then_inc(s["low"], 1)

        @block.gpsimd
        def _(pool):
            nc.gpsimd.memset(hid[:], 0.0).then_inc(ready, 1)

            def gather(b):
                static = isinstance(b.i, int)
                if not static or b.n >= 2:
                    pool.wait_ge(s["xtr"], b.n - 1)
                nc.gpsimd.tensor_copy(index[:, b.slot:b.slot + 1], keep["tokens"][:, bass.ds(b.n, 1)]).then_inc(s["indexed"], 1)
                pool.wait_ge(s["indexed"], b.n + 1)
                pool.sem_inc(s["gone"], 1)
                nc.gpsimd.indirect_dma_start(xg[:, b.slot, :], None, keep["parts_dram"],
                                             bass.IndirectOffsetOnAxis(ap=index[:, b.slot:b.slot + 1], axis=0)
                                             ).then_inc(gathered[b.slot], 16)

            def body(b):
                static = isinstance(b.i, int)
                if not static or b.n + 2 < BLOCKS:
                    gather(b + 2)
                pool.wait_ge(s["silu"], b.n + 1)
                pool.wait_ge(s["upcopied"], b.n + 1)
                if not static or b.n > 0:
                    pool.wait_ge(s["hidlo"], b.n)
                nc.gpsimd.tensor_tensor(hid[:], silu_g[:], up[:], ALU.mult).then_inc(s["hid"], 1)
                pool.wait_ge(s["hidhi"], b.n + 1)
                nc.gpsimd.tensor_tensor(hid_parts[:, 1, :], hid[:], hid_parts[:, 0, :], ALU.subtract).then_inc(s["hidlo"], 1)

            gather(Tile(0, 0))
            gather(Tile(0, 1))
            body(Tile(0, 0))
            with pool.Fori(0, (BLOCKS - 4) // 2) as i:
                body(Tile(i, 1))
                body(Tile(i, 2))
            for b in range(BLOCKS - 3, BLOCKS):
                body(Tile(0, b))

        @block.scalar
        def _(act):
            def copy_out(dst, src, wait, count, done):
                act.wait_ge(s[wait], count)
                nc.scalar.activation(dst, src, ACT.Copy).then_inc(s[done], 1)

            def body(b):
                static = isinstance(b.i, int)
                p = b - 1
                if not static or b.n + 1 < BLOCKS:
                    copy_out(x_t[:, (b + 1).slot, :], xtr[:], "xtr", b.n + 2, "xt_copied")
                if not static or b.n < BLOCKS:
                    act.wait_ge(s["gate"], b.n + 1)
                    if not static or b.n > 0:
                        act.wait_ge(s["hid"], b.n)
                    nc.scalar.activation(silu_g[:], bank[:, GATE_B, :], ACT.Silu).then_inc(s["silu"], 1)
                if not static or b.n > 0:
                    if not static or b.n > 1:
                        act.wait_ge(s["down"], p.n)
                    copy_out(hid_t[:], htr[:], "htr", p.n + 1, "ht_copied")
                if not static or b.n < BLOCKS:
                    copy_out(up[:], bank[:, UP_B, :], "up", b.n + 1, "upcopied")
                    act.wait_ge(s["hid"], b.n + 1)
                    if not static or b.n > 0:
                        act.wait_ge(s["htr"], b.n)
                    nc.scalar.activation(hid_parts[:, 0, :], hid[:], ACT.Copy).then_inc(s["hidhi"], 1)
                if not static or b.n > 0:
                    if not static or b.n > 2:
                        act.wait_ge(stored[p.slot], 16 * p.half)
                    copy_out(y[:, p.slot, :], bank[:, Y_B:Y_B + 2, :].rearrange("p b n -> p (b n)"), "down", p.n + 1,
                             "ycopied")
                    act.wait_ge(s["ycopied"], p.n + 1)
                    act.dma_start(keep["y_dram"][bass.ds(p.n * P, P), :], y[:, p.slot, :]).then_inc(stored[p.slot], 16)

            copy_out(x_t[:, 0, :], xtr[:], "xtr", 1, "xt_copied")
            run_tiles(act, 0, BLOCKS, 1, BLOCKS - 2, body)
            for slot in range(2):
                act.wait_ge(stored[slot], 16 * (BLOCKS // 2))

        @block.tensor
        def _(pe):
            def transpose_x(b):
                static = isinstance(b.i, int)
                pe.wait_ge(gathered[b.slot], 16 * b.half + 16)
                if not static or b.n > 0:
                    pe.wait_ge(s["xt_copied"], b.n)
                for k in range(2 * KT):
                    ins = nc.tensor.transpose(xtr[:, k * P:(k + 1) * P], xg[:, b.slot, k * P:(k + 1) * P], ident[:])
                ins.then_inc(s["xtr"], 1)

            def passes(dst, lhs, at, stride, kts, done):
                hi = lambda k: w_hi[:, bass.ds(at * 2 + (2 * k * stride + 1), BANK, step=2)]
                lo = lambda k: w_lo[:, bass.ds(at + k * stride, BANK)]
                for k in range(kts):
                    nc.tensor.matmul(dst, lhs(0, k), hi(k), start=k == 0, stop=False)
                    nc.tensor.matmul(dst, lhs(0, k), lo(k), start=False, stop=False)
                    ins = nc.tensor.matmul(dst, lhs(1, k), hi(k), start=False, stop=k == kts - 1)
                if done is not None:
                    ins.then_inc(s[done], 1)

            def down(b, at, part):
                pe.wait_ge(s["low"], part + 3)
                pe.wait_ge(s["ht_copied"], b.n + 1)
                if not isinstance(b.i, int) or b.n > 0:
                    pe.wait_ge(s["ycopied"], b.n)
                for half in range(2):
                    passes(bank[:, Y_B + half, :], lambda q, k: hid_t[:, (q * HT + k) * P:(q * HT + k + 1) * P],
                           at + (2 * PART + half * BANK), D, HT, "down" if half else None)

            def where(b):
                at = pe.value_load(keep["block_slot"][0:1, bass.ds(b.n, 1)], min_val=0, max_val=SLOT)
                part = pe.value_load(keep["block_part"][0:1, bass.ds(b.n, 1)], min_val=0, max_val=3 * (EXPERTS - 1))
                return at, part

            def body(b):
                static = isinstance(b.i, int)
                p = b - 1
                if not static or b.n < BLOCKS:
                    at, part = where(b)
                    if not static or b.n + 1 < BLOCKS:
                        transpose_x(b + 1)
                    x = lambda q, k: x_t[:, b.slot, (q * KT + k) * P:(q * KT + k + 1) * P]
                    pe.wait_ge(s["low"], part + 1)
                    pe.wait_ge(s["xt_copied"], b.n + 1)
                    if not static or b.n > 0:
                        pe.wait_ge(s["silu"], b.n)
                    passes(bank[:, GATE_B, :], x, at, D_E, KT, "gate")
                if not static or b.n > 0:
                    pe.wait_ge(s["hidlo"], p.n + 1)
                    pe.wait_ge(s["hidhi"], p.n + 1)
                    if not static or b.n > 1:
                        pe.wait_ge(s["ht_copied"], p.n)
                    for k in range(2 * HT):
                        ins = nc.tensor.transpose(htr[:, k * P:(k + 1) * P],
                                                  hid_parts[:, k // HT, (k % HT) * P:(k % HT + 1) * P], ident[:])
                    ins.then_inc(s["htr"], 1)
                if not static or b.n < BLOCKS:
                    pe.wait_ge(s["low"], part + 2)
                    if not static or b.n > 0:
                        pe.wait_ge(s["upcopied"], b.n)
                    passes(bank[:, UP_B, :], x, at + PART, D_E, KT, "up")
                if not static or b.n > 0:
                    down(p, *where(p))

            pe.wait_ge(id_made, 1)
            transpose_x(Tile(0, 0))
            run_tiles(pe, 0, BLOCKS, 1, BLOCKS - 2, body)


def combine(nc, a, keep):
    ctx = ExitStack()
    with ctx:
        m = Memory(nc, ctx)
        g, b = m.sb("ln2_g_sb", [P, D], F32), m.sb("ln2_b_sb", [P, D], F32)
        rows = m.sb("rows", [P, 2, TOP, D], F32)
        h1 = m.sb("h1_back", [P, 2, D], F32)
        mixed = m.sb("mixed", [P, 2, D], F32)
        index = m.sb("c_index", [P, 2, TOP], U32)
        stats = m.sb("c_stats", [P, 2, 6], F32)
        moments = m.sb("c_moments", [P, 2], F32)
        rstd = m.sb("c_rstd", [P, 2], F32)
        minus_half, eps = m.sb("c_minus_half", [P, 1], F32), m.sb("c_eps", [P, 1], F32)
        s = {n: m.sem("c_" + n) for n in "indexed weighted mixed stats rstd done ready params pool dve passed gone".split()}
        gathered = [m.sem(f"c_gathered{i}") for i in range(2)]
        loaded = [m.sem(f"c_loaded{i}") for i in range(2)]
        stored = [m.sem(f"c_stored{i}") for i in range(2)]
        block = ctx.enter_context(nc.Block())

        @block.sync
        def _(sp):
            def load(t):
                if not isinstance(t.i, int) or t.n >= 2:
                    sp.wait_ge(s["mixed"], t.n - 1)
                sp.dma_start(h1[:, t.slot, :], keep["h1_dram"][bass.ds(t.n * P, P), :]).then_inc(loaded[t.slot], 16)

            def store(t):
                sp.wait_ge(s["done"], t.n + 1)
                sp.dma_start(a["out"][bass.ds(t.n * P, P), :], mixed[:, t.slot, :]).then_inc(stored[t.slot], 16)

            sp.dma_start(g[:], a["ln2_g"].partition_broadcast(P)).then_inc(s["params"], 16)
            sp.dma_start(b[:], a["ln2_b"].partition_broadcast(P)).then_inc(s["params"], 16)
            load(Tile(0, 0))
            load(Tile(0, 1))
            with sp.Fori(0, TILES // 2 - 1) as i:
                for k in range(2):
                    load(Tile(i, k + 2))
                    store(Tile(i, k))
            store(Tile(0, TILES - 2))
            store(Tile(0, TILES - 1))
            for slot in range(2):
                sp.wait_ge(stored[slot], 16 * (TILES // 2))

        @block.gpsimd
        def _(pool):
            nc.gpsimd.memset(minus_half[:], -0.5).then_inc(s["ready"], 1)
            nc.gpsimd.memset(eps[:], LN_EPS).then_inc(s["ready"], 1)
            pool.wait_ge(s["ready"], 2)

            def gather(t):
                if not isinstance(t.i, int) or t.n >= 2:
                    pool.wait_ge(s["mixed"], t.n - 1)
                nc.gpsimd.tensor_copy(index[:, t.slot, :], keep["dest"][:, :, bass.ds(t.n, 1)].squeeze(2)).then_inc(s["indexed"], 1)
                pool.wait_ge(s["indexed"], t.n + 1)
                pool.sem_inc(s["gone"], 1)
                for k in range(TOP):
                    nc.gpsimd.indirect_dma_start(rows[:, t.slot, k, :], None, keep["y_dram"],
                                                 bass.IndirectOffsetOnAxis(ap=index[:, t.slot, k:k + 1], axis=0)
                                                 ).then_inc(gathered[t.slot], 16)

            def root(t):
                pool.wait_ge(s["stats"], t.n + 1)
                nc.gpsimd.tensor_tensor(rstd[:, 1:2], moments[:, 1:2], eps[:], ALU.add).then_inc(s["pool"], 1)
                pool.wait_ge(s["pool"], t.n + 1)
                nc.gpsimd.tensor_tensor(rstd[:, 0:1], rstd[:, 1:2], minus_half[:], ALU.pow).then_inc(s["rstd"], 1)

            gather(Tile(0, 0))
            gather(Tile(0, 1))
            with pool.Fori(0, TILES // 2 - 1) as i:
                for k in range(2):
                    root(Tile(i, k))
                    gather(Tile(i, k + 2))
            root(Tile(0, TILES - 2))
            root(Tile(0, TILES - 1))

        @block.scalar
        def _(act):
            with act.Fori(0, TILES // 2) as i:
                for k in range(2):
                    t = Tile(i, k)
                    act.wait_ge(gathered[k], 32 * i + 32)
                    nc.scalar.activation(rows[:, k, 0, :], rows[:, k, 0, :], ACT.Copy,
                                         scale=keep["pair_w"][:, 0, bass.ds(t.n, 1)]).then_inc(s["weighted"], 1)

        @block.vector
        def _(dve):
            chain = Chain(dve, s["dve"])
            STEPS = 4
            dve.wait_ge(s["params"], 32)

            def body(t, later):
                slot = t.slot
                out = mixed[:, slot, :]
                dve.wait_ge(s["weighted"], t.n + 1)
                if later:
                    dve.wait_ge(stored[slot], 16 * t.half)
                chain.link(nc.vector.scalar_tensor_tensor(out=out, in0=rows[:, slot, 1, :],
                                                          scalar=keep["pair_w"][:, 1, bass.ds(t.n, 1)],
                                                          in1=rows[:, slot, 0, :], op0=ALU.mult, op1=ALU.add))
                dve.wait_ge(loaded[slot], 16 * t.half + 16)
                ins = nc.vector.scalar_tensor_tensor(out=out, in0=h1[:, slot, :], scalar=ALPHA, in1=out, op0=ALU.mult,
                                                     op1=ALU.add)
                ins.then_inc(s["mixed"], 1)
                dve.wait_ge(s["mixed"], t.n + 1)
                nc.vector.bn_stats(stats[:, 0, :], mixed[:, slot, 0:BANK])
                chain.link(nc.vector.bn_stats(stats[:, 1, :], mixed[:, slot, BANK:D]), s["passed"])
                nc.vector.bn_aggr(moments[:], stats[:]).then_inc(s["stats"], 1)
                dve.wait_ge(s["stats"], t.n + 1)
                chain.link(nc.vector.scalar_tensor_tensor(out=out, in0=out, scalar=moments[:, 0:1], in1=g[:],
                                                          op0=ALU.subtract, op1=ALU.mult))
                dve.wait_ge(s["rstd"], t.n + 1)
                nc.vector.scalar_tensor_tensor(out=out, in0=out, scalar=rstd[:, 0:1], in1=b[:], op0=ALU.mult,
                                               op1=ALU.add).then_inc(s["done"], 1)

            body(Tile(0, 0), False)
            body(Tile(0, 1), False)
            STEPS = chain.steps // 2
            with dve.Fori(0, TILES // 2 - 1) as i:
                for k in range(2):
                    chain.base, chain.steps = (2 + k) * STEPS + i * (2 * STEPS), 0
                    body(Tile(i, 2 + k), True)
                    assert chain.steps == STEPS


def program(nc, a, stop=None):
    with ExitStack() as ctx:
        sb = lambda name, shape, dt: ctx.enter_context(nc.sbuf_tensor(name, shape, dt))
        keep = {
            "logits": sb("logits", [P, TILES, LOGITS], F32),
            "pair_w": sb("pair_w", [P, 2, TILES], F32),
            "dest": sb("dest_rows", [P, 2, TILES], U32),
            "tokens": sb("tokens", [P, BLOCKS], U32),
            "ends": sb("ends_i", [1, EXPERTS], U32),
            "block_slot": sb("block_slot", [1, BLOCKS], U32),
            "block_part": sb("block_part", [1, BLOCKS], U32),
            "h1_dram": nc.dram_tensor("h1_dram", [SEQ, D], F32, kind="Internal").ap(),
            "parts_dram": nc.dram_tensor("parts_dram", [SEQ, 2 * D], BF16, kind="Internal").ap(),
            "y_dram": nc.dram_tensor("y_dram", [BLOCKS * P, D], F32, kind="Internal").ap(),
        }
        mixer(nc, a, keep)
        router(nc, a, keep)
        experts(nc, a, keep)
        combine(nc, a, keep)


def laid_out(inputs):
    g = lambda name: np.asarray(inputs[name])
    row = lambda x: np.ascontiguousarray(x).reshape(-1)
    col = lambda x: np.ascontiguousarray(x.reshape(GROUPS_P, P).T)
    arrays = {
        "x": g("x")[0], "meta": g("meta_tokens"), "ln0_g": row(g("ln_emb_g")), "ln0_b": row(g("ln_emb_b")),
        "w_in": g("w_in")[0], "pool_w": g("pool_w")[0], "pool_b": col(g("pool_b")[0]),
        "pool_scale": col(g("pool_scale")[0]), "w_out": g("w_out")[0], "ln1_g": row(g("ln1_g")[0]),
        "ln1_b": row(g("ln1_b")[0]), "rg_w": g("router_group_w")[0], "rg_b": row(g("router_group_b")[0]),
        "re_w": g("router_expert_w")[0], "re_b": row(g("router_expert_b")[0]), "w_gate": g("expert_w_gate")[0],
        "w_up": g("expert_w_up")[0], "w_down": g("expert_w_down")[0], "ln2_g": row(g("ln2_g")[0]),
        "ln2_b": row(g("ln2_b")[0]),
    }
    arrays.update(shape_constants())
    return {"in_" + k: np.ascontiguousarray(v) for k, v in arrays.items()}


def kernel(**inputs):
    import concourse.bacc as bacc
    from concourse.bass_utils import run_bass_kernel_spmd

    arrays = laid_out(inputs)
    nc = bacc.Bacc("TRN2", target_bir_lowering=False, num_devices=1)
    a = {k[3:]: nc.dram_tensor(k, v.shape, mybir.dt.from_np(v.dtype), kind="ExternalInput").ap()
         for k, v in arrays.items()}
    a["out"] = nc.dram_tensor("out", [SEQ, D], F32, kind="ExternalOutput").ap()
    program(nc, a)
    r = run_bass_kernel_spmd(nc, [arrays], core_ids=[0])
    return r.results[0]["out"].reshape(1, SEQ, D)
```

```python
from contextlib import ExitStack

import numpy as np

import concourse.bass as bass
from concourse import mybir

ALU = mybir.AluOpType
ACT = mybir.ActivationFunctionType
AX = mybir.AxisListType
F32 = mybir.dt.float32
BF16 = mybir.dt.bfloat16
F16 = mybir.dt.float16
I32 = mybir.dt.int32
U32 = mybir.dt.uint32

P = 128
D = 1024
KT = D // P
SEQ = 4096
TILES = SEQ // P
N_META = 16
HEADS = 4
DK = 64
DV = 128
HALF = DK // 2
QK = 2 * HEADS * DK
RET = HEADS * DV
POOL_WINDOWS = (2, 4, 8, 16)
GROUPS_P = len(POOL_WINDOWS)
POOL = GROUPS_P * P
IN_COLS = QK + 2 * RET + POOL
BANK = 512
N_GROUPS = 4
PER_GROUP = 8
EXPERTS = N_GROUPS * PER_GROUP
LOGITS = N_GROUPS + EXPERTS
D_E = 512
HT = D_E // P
TOP = 2
BLOCKS = SEQ * TOP // P + EXPERTS
RUN_BLOCKS = BLOCKS + 1
TABLE = RUN_BLOCKS + 2
SLOT = 2 * KT * D_E + HT * D
PART = SLOT // 3
LN_EPS = 1e-5
GN_EPS = 1e-6
ALPHA = 2 ** 0.25
W_SCALE = 256.0


def shape_constants():
    inv = np.power(10000.0, -np.arange(HALF) / HALF).astype(np.float32)
    row = np.arange(P)
    pos = (np.arange(-1, TILES)[:, None] * P + row[None, :] + N_META).astype(np.float32)
    angle = (np.maximum(pos, 0)[:, :, None] * inv).astype(np.float64)
    cos = np.cos(angle).astype(np.float32).transpose(1, 0, 2)
    sin = np.sin(angle).astype(np.float32).transpose(1, 0, 2)
    log_g = np.log1p(-np.power(2.0, -5.0 - np.arange(HEADS)))
    decay = np.concatenate([np.exp((row[:, None] + 1) * log_g), np.exp(-(row[:, None] + 1) * log_g) * DK ** -0.5], 1)
    chunk = np.exp(P * log_g)
    chunk_decay = np.stack([np.repeat(chunk[2 * p:2 * p + 2], DK) for p in range(HEADS // 2)], 1)
    j, i = row[:, None], row[None, :]
    causal = (j <= i).astype(np.float32)
    band = np.stack([((i - j >= 0) & (i - j < w)) / w - (i == j) for w in POOL_WINDOWS], 1)
    band_prev = np.stack([(i - j + P < w) / w for w in POOL_WINDOWS], 1)
    return {
        "cos": np.ascontiguousarray(cos / W_SCALE, np.float32), "sin": np.ascontiguousarray(sin / W_SCALE, np.float32),
        "decay": decay.astype(np.float32), "chunk_decay": chunk_decay.astype(np.float32),
        "causal": causal, "band": band.astype(np.float32), "band_prev": band_prev.astype(np.float32),
        "ident": np.eye(P, dtype=np.float32), "meta_rows": (row >= P - N_META).astype(np.float32)[:, None],
        "before": (j < i).astype(np.float32),
    }


class Tile:

    def __init__(self, i, k):
        self.i, self.k = i, k

    @property
    def n(self):
        return 2 * self.i + self.k

    @property
    def slot(self):
        return self.k % 2

    @property
    def half(self):
        return self.i + self.k // 2

    def __add__(self, d):
        return Tile(self.i, self.k + d)

    def __sub__(self, d):
        return Tile(self.i, self.k - d)


def run_tiles(eng, first, last, loop_from, loop_to, body):
    for t in range(first, loop_from):
        body(Tile(0, t))
    pairs = (loop_to - loop_from + 1) // 2
    with eng.Fori(0, pairs) as i:
        body(Tile(i, loop_from))
        body(Tile(i, loop_from + 1))
    for t in range(loop_to + 1, last + 1):
        body(Tile(0, t))


class Chain:

    def __init__(self, eng, sem):
        self.eng, self.sem, self.base, self.steps = eng, sem, 0, 0

    def link(self, ins, passed=None):
        ins.then_inc(self.sem, 1)
        self.steps += 1
        self.eng.wait_ge(self.sem, self.base + self.steps)
        if passed is not None:
            self.eng.sem_inc(passed, 1)


class Memory:
    def __init__(self, nc, ctx):
        self.nc, self.ctx = nc, ctx

    def sb(self, name, shape, dt):
        return self.ctx.enter_context(self.nc.sbuf_tensor(name, shape, dt))

    def ps(self, name, shape, dt):
        return self.ctx.enter_context(self.nc.psum_tensor(name, shape, dt))

    def sem(self, name):
        return self.ctx.enter_context(self.nc.semaphore(name))


def mixer(nc, a, keep):
    ctx = ExitStack()
    with ctx:
        m = Memory(nc, ctx)
        w_in = [m.sb(f"w_in{q}", [P, KT, IN_COLS], dt) for q, dt in enumerate((BF16, F16))]
        w_out = [m.sb(f"w_out{q}", [P, KT, D], dt) for q, dt in enumerate((BF16, F16))]
        stage = m.sb("stage", [P, 2, 2 * D], F32)
        h1 = stage[:, :, 0:D]
        h1_parts = [stage[:, :, D:3 * D // 2].bitcast(BF16), stage[:, :, 3 * D // 2:2 * D].bitcast(F16)]
        ln0_g, ln0_b = m.sb("ln0_g", [P, D], F32), m.sb("ln0_b", [P, D], F32)
        ln1_g, ln1_b = m.sb("ln1_g", [P, D], F32), m.sb("ln1_b", [P, D], F32)
        cos, sin = m.sb("cos_sb", [P, TILES + 1, HALF], F32), m.sb("sin_sb", [P, TILES + 1, HALF], F32)
        decay = m.sb("decay_sb", [P, 2 * HEADS], F32)
        chunk_decay = m.sb("chunk_decay_sb", [P, 2], F32)
        causal = m.sb("causal_sb", [P, P], F32)
        band, band_prev = m.sb("band_sb", [P, GROUPS_P, P], F32), m.sb("band_prev_sb", [P, GROUPS_P, P], F32)
        ident = m.sb("ident_sb", [P, P], F32)
        meta_rows = m.sb("meta_rows_sb", [P, 1], F32)
        pool_w = m.sb("pool_w_sb", [P, GROUPS_P, P], F32)
        pool_b, pool_scale = m.sb("pool_b_sb", [P, GROUPS_P], F32), m.sb("pool_scale_sb", [P, GROUPS_P], F32)
        router_w = m.sb("router_w_sb", [P, KT, LOGITS], F32)
        router_b = m.sb("router_b_sb", [P, LOGITS], F32)
        x_in = m.sb("x_in", [P, 2, D], F32)
        h = m.sb("h", [P, 2, D], F32)
        h_t = [m.sb(f"h_t{q}", [P, D], dt) for q, dt in enumerate((BF16, F16))]
        mix_t = [m.sb(f"mix_t{q}", [P, D], dt) for q, dt in enumerate((BF16, F16))]
        rot_a, rot_b = m.sb("rot_a", [P, QK], F32), m.sb("rot_b", [P, QK], F32)
        qk = m.sb("qk", [P, QK], F32)
        v = m.sb("v", [P, RET], F32)
        u = m.sb("u", [P, 2, POOL], F32)
        gate = m.sb("gate", [P, RET], F32)
        q_t = m.sb("q_t", [P, 2, 2, P], F32)
        k_t = m.sb("k_t", [P, 2, P], F32)
        scores = m.sb("scores", [P, HEADS, P], F32)
        state = m.sb("state", [P, 2, DV], F32)
        ret = m.sb("ret", [P, RET], F32)
        pooled_t = m.sb("pooled_t", [P, POOL], F32)
        pool_out = m.sb("pool_out", [P, POOL], F32)
        h1_t = m.sb("h1_t", [P, D], F32)
        stats = m.sb("stats", [P, 2, 2, 6], F32)
        moments = m.sb("moments", [P, 2, 2], F32)
        rstd = m.sb("rstd", [P, 2, 2], F32)
        g_stats = m.sb("g_stats", [P, HEADS, 6], F32)
        g_moments = m.sb("g_moments", [P, HEADS, 2], F32)
        g_rstd = m.sb("g_rstd", [P, 2, HEADS], F32)
        minus_half = m.sb("minus_half", [P, HEADS], F32)
        eps = m.sb("eps", [P, 3, HEADS], F32)

        bank = m.ps("bank", [P, 8, BANK], F32)
        QK_B, V_B, U_B, GATE_B, OUT_B, TR_B, TR2_B = 0, 1, 2, 3, 4, 6, 7

        weights_loaded = [m.sem(f"weights_loaded{s}") for s in range(2)]
        w_hi, w_lo = m.sem("w_hi"), m.sem("w_lo")
        params = m.sem("params")
        ready = m.sem("constants_ready")
        x_loaded = [m.sem(f"x_loaded{s}") for s in range(2)]
        stored = [m.sem(f"h1_stored{s}") for s in range(2)]
        names = ("stats0 rstd0 hdone htr hthi htlo qkdone vdone udone gatedone rotdone qkscaled vcopied ucopied "
                 "silu qktr qkt_copied bandmm band_copied scoremm masked poolmm pool_fin pool_hi pool_lo kvmm retmm "
                 "state_new gstats grstd ret_fin ret_tr ret_hi ret_lo outmm residual based stats1 rstd1 h1done h1hi h1lo h1tr "
                 "h1t_copied routermm logits_done").split()
        s = {n: m.sem(n) for n in names}
        dve_chain, pool_chain, passed = m.sem("dve_chain"), m.sem("pool_chain"), m.sem("passed")
        params0 = m.sem("params0")

        FIRST, LOOP_FROM, LOOP_TO = 0, 3, TILES - 2
        block = ctx.enter_context(nc.Block())

        @block.sync
        def _(sp):
            def param(dst, src, sem=params):
                sp.dma_start(dst, src).then_inc(sem, 16)

            def load_x(t, rows=None):
                if not (isinstance(t.i, int) and t.n < 1):
                    sp.wait_ge(s["hdone"], t.n)
                src = a["x"][bass.ds(t.n * P, P), :]
                sp.dma_start(x_in[:, t.slot, :], src).then_inc(x_loaded[t.slot], 16)

            sp.wait_ge(ready, 1)
            sp.dma_start(x_in[P - N_META:P, 1, :], a["meta"]).then_inc(x_loaded[1], 16)
            load_x(Tile(0, 0))
            param(ln0_g[:], a["ln0_g"].partition_broadcast(P), params0)
            param(ln0_b[:], a["ln0_b"].partition_broadcast(P), params0)
            param(ident[:], a["ident"], params0)
            param(meta_rows[:], a["meta_rows"], params0)
            w_in_v = a["w_in"].rearrange("(k p) n -> k p n", p=P)
            w_out_v = a["w_out"].rearrange("(k two p) n -> k p two n", p=P, two=2)
            for k in range(KT + KT // 2):
                if k >= 2:
                    sp.wait_ge(w_lo, k - 1)
                if k < KT:
                    sp.dma_start(stage[:, k % 2, :], w_in_v[k]).then_inc(weights_loaded[k % 2], 16)
                else:
                    sp.dma_start(stage[:, k % 2, :].rearrange("p (two n) -> p two n", two=2),
                                 w_out_v[k - KT]).then_inc(weights_loaded[k % 2], 16)
                if k == 1:
                    param(cos[:], a["cos"])
                    param(sin[:], a["sin"])
                    for dst, name in ((decay, "decay"), (chunk_decay, "chunk_decay"), (causal, "causal"),
                                      (band, "band"), (band_prev, "band_prev"), (pool_b, "pool_b"),
                                      (pool_scale, "pool_scale")):
                        param(dst[:], a[name])
                    param(pool_w[:], a["pool_w"].rearrange("g c d -> c g d"))
                    param(ln1_g[:], a["ln1_g"].partition_broadcast(P))
                    param(ln1_b[:], a["ln1_b"].partition_broadcast(P))
                    param(router_w[:, :, 0:N_GROUPS], a["rg_w"].rearrange("(k p) n -> p k n", p=P))
                    param(router_w[:, :, N_GROUPS:], a["re_w"].rearrange("(k p) n -> p k n", p=P))
                    param(router_b[:, 0:N_GROUPS], a["rg_b"].partition_broadcast(P))
                    param(router_b[:, N_GROUPS:], a["re_b"].partition_broadcast(P))
            load_x(Tile(0, 1))
            load_x(Tile(0, 2))

            def body(t):
                static = isinstance(t.i, int)
                if not static or t.n + 3 < TILES:
                    load_x(t + 3)
                if not static or t.n >= 1:
                    p = t - 1
                    rows = bass.ds(p.n * P, P)
                    sp.wait_ge(s["h1done"], p.n + 1)
                    sp.dma_start(keep["h1_dram"][rows, :], h1[:, p.slot, :]).then_inc(stored[p.slot], 16)
                    sp.wait_ge(s["h1hi"], p.n + 1)
                    sp.wait_ge(s["h1lo"], p.n + 1)
                    sp.dma_start(keep["parts_dram"][rows, :],
                                 stage[:, p.slot, D:2 * D].bitcast(BF16)).then_inc(stored[p.slot], 16)

            for t in range(0, 1):
                body(Tile(0, t))
            with sp.Fori(0, (TILES - 4) // 2) as i:
                body(Tile(i, 1))
                body(Tile(i, 2))
            for t in range(TILES - 3, TILES + 1):
                body(Tile(0, t))
            for slot in range(2):
                sp.wait_ge(stored[slot], TILES // 2 * 32)

        @block.gpsimd
        def _(pool):
            chain = Chain(pool, pool_chain)
            nc.gpsimd.memset(x_in[:, 1, :], 0.0).then_inc(ready, 1)
            nc.gpsimd.memset(q_t[:], 0.0).then_inc(ready, 1)
            nc.gpsimd.memset(state[:], 0.0).then_inc(ready, 1)
            nc.gpsimd.memset(minus_half[:], -0.5)
            nc.gpsimd.memset(eps[:, 0, :], LN_EPS)
            nc.gpsimd.memset(eps[:, 1, :], LN_EPS * W_SCALE ** 2)
            chain.link(nc.gpsimd.memset(eps[:, 2, :], GN_EPS))

            def inverse_root(out, tmp, var, eps_in, n):
                chain.link(nc.gpsimd.tensor_tensor(tmp, var, eps_in, ALU.add))
                return nc.gpsimd.tensor_tensor(out, tmp, minus_half[:, 0:n], ALU.pow)

            def ln_rstd(which, count):
                pool.wait_ge(s[f"stats{which}"], count)
                inverse_root(rstd[:, which, 0:1], rstd[:, which, 1:2], moments[:, which, 1:2],
                             eps[:, which, 0:1], 1).then_inc(s[f"rstd{which}"], 1)

            def scale_qk(t, count):
                pool.wait_ge(s["rotdone"], count)
                nc.gpsimd.tensor_tensor(qk[:].rearrange("p (h d) -> p h d", d=DK),
                                        rot_a[:].rearrange("p (h d) -> p h d", d=DK),
                                        decay[:].unsqueeze(2).to_broadcast([P, 2 * HEADS, DK]),
                                        ALU.mult).then_inc(s["qkscaled"], 1)

            def body(t):
                static = isinstance(t.i, int)
                if not static or t.n < TILES:
                    if not static or t.n >= 0:
                        scale_qk(t, t.n + 2)
                    if not static or t.n + 1 < TILES:
                        ln_rstd(0, t.n + 3)
                if not static or t.n >= 1:
                    p = t - 1
                    ln_rstd(1, p.n + 1)
                if not static or t.n < TILES:
                    pool.wait_ge(s["gstats"], t.n + 1)
                    inverse_root(g_rstd[:, 0, :], g_rstd[:, 1, :], g_moments[:, :, 1], eps[:, 2, :],
                                 HEADS).then_inc(s["grstd"], 1)
                if not static or t.n >= 1:
                    pool.wait_ge(s["h1done"], p.n + 1)
                    pool.wait_ge(s["h1hi"], p.n + 1)
                    nc.gpsimd.tensor_tensor(h1_parts[1][:, p.slot, :], h1[:, p.slot, :], h1_parts[0][:, p.slot, :],
                                            ALU.subtract).then_inc(s["h1lo"], 1)

            ln_rstd(0, 1)
            ln_rstd(0, 2)
            pool.wait_ge(params, 16 * 16)
            scale_qk(Tile(0, -1), 1)
            for t in range(LOOP_FROM):
                body(Tile(0, t))
            base, STEPS = chain.steps, 3
            with pool.Fori(0, (LOOP_TO - LOOP_FROM + 1) // 2) as i:
                for k in range(2):
                    chain.base, chain.steps = base + i * (2 * STEPS) + STEPS * k, 0
                    body(Tile(i, LOOP_FROM + k))
                    assert chain.steps == STEPS
            chain.base, chain.steps = base + (LOOP_TO - LOOP_FROM + 1) * STEPS, 0
            for t in range(LOOP_TO + 1, TILES + 1):
                body(Tile(0, t))

        @block.scalar
        def _(act):
            def split_weights(ks):
                for k in ks:
                    act.wait_ge(weights_loaded[k % 2], 16 * (k // 2 + 1))
                    if k < KT:
                        dst = w_in[0][:, k, :]
                    else:
                        dst = w_out[0][:, 2 * (k - KT):2 * (k - KT) + 2, :].rearrange("p two n -> p (two n)")
                    nc.scalar.activation(dst, stage[:, k % 2, :], ACT.Copy, scale=W_SCALE).then_inc(w_hi, 1)

            def copy_out(dst, src, wait, count, done, scale=1.0):
                act.wait_ge(s[wait], count)
                nc.scalar.activation(dst, src, ACT.Copy, scale=scale).then_inc(s[done], 1)

            def h_high(t):
                copy_out(h_t[0][:], bank[:, TR_B:TR_B + 2, :].rearrange("p b n -> p (b n)"), "htr", t.n + 2, "hthi")

            def body(t):
                static = isinstance(t.i, int)
                main = not static or t.n < TILES
                p, pp = t - 1, t - 2
                if main:
                    act.wait_ge(s["kvmm"], t.n + 1)
                    if not static or t.n > 0:
                        act.wait_ge(s["retmm"], t.n)
                    copy_out(v[:], bank[:, V_B, :], "vdone", t.n + 2, "vcopied", 1 / W_SCALE)
                if not static or 1 <= t.n <= TILES:
                    if not static or t.n > 1:
                        act.wait_ge(s["outmm"], p.n)
                    copy_out(mix_t[0][:, 0:RET], bank[:, TR_B, :], "ret_tr", p.n + 1, "ret_hi")
                if not static or t.n >= 2:
                    if not static or t.n > 2:
                        act.wait_ge(s["routermm"], pp.n)
                    copy_out(h1_t[:], bank[:, OUT_B:OUT_B + 2, :].rearrange("p b n -> p (b n)"), "h1tr", pp.n + 1,
                             "h1t_copied")
                if main:
                    if not static or t.n >= 2:
                        act.wait_ge(stored[t.slot], 32 * t.half)
                    act.wait_ge(s["hdone"], t.n + 2)
                    nc.scalar.activation(h1[:, t.slot, :], h[:, t.slot, :], ACT.Copy,
                                         scale=ALPHA * W_SCALE).then_inc(s["based"], 1)
                    if not static or t.n > 0:
                        act.wait_ge(s["bandmm"], t.n)
                    copy_out(u[:, t.slot, :], bank[:, U_B, :], "udone", t.n + 2, "ucopied", 1 / W_SCALE)
                    act.wait_ge(s["gatedone"], t.n + 1)
                    if not static or t.n > 0:
                        act.wait_ge(s["ret_fin"], t.n)
                    nc.scalar.activation(gate[:], bank[:, GATE_B, :], ACT.Silu, scale=1 / W_SCALE).then_inc(s["silu"], 1)
                    if not static or t.n + 1 < TILES:
                        h_high(t + 1)
                    act.wait_ge(s["qktr"], t.n + 1)
                    pairs = bank[:, TR_B, :].rearrange("p (j n) -> p j n", j=4)
                    nc.scalar.activation(k_t[:], pairs[:, 2:4, :], ACT.Copy).then_inc(s["qkt_copied"], 1)
                    nc.scalar.activation(q_t[0:DK, 0, :, :], pairs[0:DK, 0:2, :], ACT.Copy).then_inc(s["qkt_copied"], 1)
                    nc.scalar.activation(q_t[DK:P, 1, :, :], pairs[DK:P, 0:2, :], ACT.Copy).then_inc(s["qkt_copied"], 1)
                    copy_out(pooled_t[:], bank[:, TR2_B, :], "bandmm", t.n + 1, "band_copied")
                    copy_out(mix_t[0][:, RET:], pool_out[:], "pool_fin", t.n + 1, "pool_hi")
                if not static or 1 <= t.n <= TILES:
                    act.wait_ge(s["h1done"], p.n + 1)
                    nc.scalar.activation(h1_parts[0][:, p.slot, :], h1[:, p.slot, :], ACT.Copy).then_inc(s["h1hi"], 1)

            split_weights(range(KT))
            h_high(Tile(0, -1))
            split_weights(range(KT, KT + KT // 2))
            copy_out(v[:], bank[:, V_B, :], "vdone", 1, "vcopied", 1 / W_SCALE)
            copy_out(u[:, 1, :], bank[:, U_B, :], "udone", 1, "ucopied", 1 / W_SCALE)
            h_high(Tile(0, 0))
            act.wait_ge(ready, 3)
            run_tiles(act, FIRST, TILES + 1, LOOP_FROM, LOOP_TO, body)

        @block.vector
        def _(dve):
            chain = Chain(dve, dve_chain)

            def low(dst, full, high, wait, count, done):
                dve.wait_ge(s[wait], count)
                nc.vector.tensor_tensor(dst, full, high, ALU.subtract).then_inc(s[done], 1)

            def split_weights(ks):
                for k in ks:
                    if k < KT:
                        hi, lo = (w_in[q][:, k, :] for q in range(2))
                    else:
                        j = 2 * (k - KT)
                        hi, lo = (w_out[q][:, j:j + 2, :].rearrange("p two n -> p (two n)") for q in range(2))
                    dve.wait_ge(weights_loaded[k % 2], 16 * (k // 2 + 1))
                    dve.wait_ge(w_hi, k + 1)
                    nc.vector.scalar_tensor_tensor(out=lo, in0=stage[:, k % 2, :], scalar=W_SCALE, in1=hi,
                                                   op0=ALU.mult, op1=ALU.subtract).then_inc(w_lo, 1)

            def ln_stats(which, src):
                nc.vector.bn_stats(stats[:, which, 0, :], src[:, 0:BANK])
                chain.link(nc.vector.bn_stats(stats[:, which, 1, :], src[:, BANK:D]), passed)
                return nc.vector.bn_aggr(moments[:, which, :], stats[:, which, :, :])

            def ln_apply(which, dst, src, g, b):
                chain.link(nc.vector.scalar_tensor_tensor(out=dst, in0=src, scalar=moments[:, which, 0:1], in1=g,
                                                          op0=ALU.subtract, op1=ALU.mult))
                return nc.vector.scalar_tensor_tensor(out=dst, in0=dst, scalar=rstd[:, which, 0:1], in1=b,
                                                      op0=ALU.mult, op1=ALU.add)

            def ln0_stats(t):
                dve.wait_ge(x_loaded[t.slot], 16 * ((t + 1).half + 1))
                ln_stats(0, x_in[:, t.slot, :]).then_inc(s["stats0"], 1)

            def ln0_apply(t):
                if not (isinstance(t.i, int) and t.n < 1):
                    dve.wait_ge(s["htr"], t.n)
                    if not (isinstance(t.i, int) and t.n < 2):
                        dve.wait_ge(s["based"], t.n - 1)
                dve.wait_ge(s["rstd0"], t.n + 2)
                ins = ln_apply(0, h[:, t.slot, :], x_in[:, t.slot, :], ln0_g[:], ln0_b[:])
                return ins

            def rotate(t):
                dve.wait_ge(s["qkdone"], t.n + 2)
                if not (isinstance(t.i, int) and t.n < 0):
                    dve.wait_ge(s["qkscaled"], t.n + 1)
                x = bank[:, QK_B, :].rearrange("p (h s f) -> p h s f", s=2, f=HALF)
                o = rot_a[:].rearrange("p (h s f) -> p h s f", s=2, f=HALF)
                o2 = rot_b[:].rearrange("p (h s f) -> p h s f", s=2, f=HALF)
                c = cos[:, bass.ds(t.n + 1, 1), :].to_broadcast([P, 2 * HEADS, HALF])
                sn = sin[:, bass.ds(t.n + 1, 1), :].to_broadcast([P, 2 * HEADS, HALF])
                nc.vector.tensor_tensor(o[:, :, 0, :], x[:, :, 0, :], c, ALU.mult)
                nc.vector.tensor_tensor(o[:, :, 1, :], x[:, :, 1, :], c, ALU.mult)
                nc.vector.tensor_tensor(o2[:, :, 0, :], x[:, :, 1, :], sn, ALU.mult)
                chain.link(nc.vector.tensor_tensor(o2[:, :, 1, :], x[:, :, 0, :], sn, ALU.mult))
                nc.vector.tensor_tensor(o[:, :, 0, :], o[:, :, 0, :], o2[:, :, 0, :], ALU.subtract)
                nc.vector.tensor_tensor(o[:, :, 1, :], o[:, :, 1, :], o2[:, :, 1, :], ALU.add).then_inc(s["rotdone"], 1)

            def h_low(t):
                low(h_t[1][:], bank[:, TR_B:TR_B + 2, :].rearrange("p b n -> p (b n)"), h_t[0][:], "hthi",
                    t.n + 2, "htlo")

            def new_state(t):
                dve.wait_ge(s["kvmm"], t.n + 2)
                if not (isinstance(t.i, int) and t.n < 0):
                    dve.wait_ge(s["retmm"], t.n + 1)
                chain.link(nc.vector.tensor_tensor(state[:], state[:],
                                                   bank[:, GATE_B, 0:2 * DV].rearrange("p (j n) -> p j n", j=2), ALU.add))
                nc.vector.tensor_tensor(state[:], state[:], chunk_decay[:].unsqueeze(2).to_broadcast([P, 2, DV]),
                                        ALU.mult).then_inc(s["state_new"], 1)

            def body(t):
                static = isinstance(t.i, int)
                main = not static or t.n < TILES
                p, pp = t - 1, t - 2
                if main:
                    rotate(t)
                if not static or 1 <= t.n <= TILES:
                    low(mix_t[1][:, 0:RET], bank[:, TR_B, :], mix_t[0][:, 0:RET], "ret_hi", p.n + 1, "ret_lo")
                if not static or t.n + 1 < TILES:
                    ln0_stats(t + 1)
                    ln0_apply(t + 1).then_inc(s["hdone"], 1)
                if not static or t.n >= 2:
                    dve.wait_ge(s["routermm"], pp.n + 1)
                    nc.vector.tensor_tensor(keep["logits"][:, bass.ds(pp.n, 1), :], bank[:, TR2_B, 0:LOGITS].unsqueeze(1),
                                            router_b[:].unsqueeze(1), ALU.add).then_inc(s["logits_done"], 1)
                if not static or t.n + 1 < TILES:
                    h_low(t + 1)
                if not static or 1 <= t.n <= TILES:
                    dve.wait_ge(s["outmm"], p.n + 1)
                    dve.wait_ge(s["based"], p.n + 1)
                    chain.link(nc.vector.tensor_tensor(
                        h1[:, p.slot, :], h1[:, p.slot, :],
                        bank[:, OUT_B:OUT_B + 2, :].rearrange("p b n -> p (b n)"), ALU.add))
                if main:
                    dve.wait_ge(s["scoremm"], t.n + 1)
                    nc.vector.tensor_tensor(scores[:], bank[:, QK_B, :].rearrange("p (h n) -> p h n", h=HEADS),
                                            causal[:].unsqueeze(1).to_broadcast([P, HEADS, P]),
                                            ALU.mult).then_inc(s["masked"], 1)
                    dve.wait_ge(s["poolmm"], t.n + 1)
                    if not static or t.n > 0:
                        dve.wait_ge(s["pool_lo"], t.n)
                    for g in range(GROUPS_P):
                        cols = slice(g * P, (g + 1) * P)
                        ins = nc.vector.tensor_scalar(pool_out[:, cols], bank[:, V_B, cols], pool_b[:, g:g + 1],
                                                      pool_scale[:, g:g + 1], ALU.add, ALU.mult)
                    ins.then_inc(s["pool_fin"], 1)
                if not static or 1 <= t.n <= TILES:
                    ln_stats(1, h1[:, p.slot, :]).then_inc(s["stats1"], 1)
                if main:
                    dve.wait_ge(s["retmm"], t.n + 1)
                    for hd in range(HEADS):
                        ins = nc.vector.bn_stats(g_stats[:, hd, :], bank[:, U_B, hd * DV:(hd + 1) * DV])
                    chain.link(ins, passed)
                    for hd in range(HEADS):
                        ins = nc.vector.bn_aggr(g_moments[:, hd, :], g_stats[:, hd, :])
                    ins.then_inc(s["gstats"], 1)
                    new_state(t)
                if not static or 1 <= t.n <= TILES:
                    dve.wait_ge(s["rstd1"], p.n + 1)
                    ln_apply(1, h1[:, p.slot, :], h1[:, p.slot, :], ln1_g[:], ln1_b[:]).then_inc(s["h1done"], 1)
                if main:
                    low(mix_t[1][:, RET:], pool_out[:], mix_t[0][:, RET:], "pool_hi", t.n + 1, "pool_lo")
                    dve.wait_ge(s["grstd"], t.n + 1)
                    if not static or t.n > 0:
                        dve.wait_ge(s["ret_tr"], t.n)
                    for hd in range(HEADS):
                        cols = slice(hd * DV, (hd + 1) * DV)
                        ins = nc.vector.tensor_scalar(ret[:, cols], bank[:, U_B, cols], g_moments[:, hd, 0:1],
                                                      g_rstd[:, 0, hd:hd + 1], ALU.subtract, ALU.mult)
                    chain.link(ins)
                    dve.wait_ge(s["silu"], t.n + 1)
                    nc.vector.tensor_tensor(ret[:], ret[:], gate[:], ALU.mult).then_inc(s["ret_fin"], 1)

            dve.wait_ge(ready, 3)
            dve.wait_ge(params0, 16 * 4)
            ln0_stats(Tile(0, -1))
            chain.link(ln0_apply(Tile(0, -1)))
            nc.vector.tensor_scalar(h[:, 1, :], h[:, 1, :], meta_rows[:, 0:1], None, ALU.mult).then_inc(s["hdone"], 1)
            split_weights(range(KT))
            h_low(Tile(0, -1))
            ln0_stats(Tile(0, 0))
            ln0_apply(Tile(0, 0)).then_inc(s["hdone"], 1)
            split_weights(range(KT, KT + KT // 2))
            dve.wait_ge(params, 16 * 16)
            rotate(Tile(0, -1))
            new_state(Tile(0, -1))
            h_low(Tile(0, 0))
            for t in range(LOOP_FROM):
                body(Tile(0, t))
            base, STEPS = chain.steps, 9
            with dve.Fori(0, (LOOP_TO - LOOP_FROM + 1) // 2) as i:
                for k in range(2):
                    chain.base, chain.steps = base + i * (2 * STEPS) + STEPS * k, 0
                    body(Tile(i, LOOP_FROM + k))
                    assert chain.steps == STEPS, chain.steps
            chain.base, chain.steps = base + (LOOP_TO - LOOP_FROM + 1) * STEPS, 0
            for t in range(LOOP_TO + 1, TILES + 2):
                body(Tile(0, t))

        @block.tensor
        def _(pe):
            def three_passes(dst, lhs, rhs, kts, done):
                last = kts - 1
                for k in range(kts):
                    nc.tensor.matmul(dst, lhs(0, k), rhs(0, k), start=k == 0, stop=False)
                    nc.tensor.matmul(dst, lhs(0, k), rhs(1, k), start=False, stop=False)
                for k in range(kts):
                    ins = nc.tensor.matmul(dst, lhs(1, k), rhs(0, k), start=False, stop=k == last)
                if done is not None:
                    ins.then_inc(s[done], 1)

            def transpose_h(t):
                pe.wait_ge(s["hdone"], t.n + 2)
                if not (isinstance(t.i, int) and t.n < 0):
                    pe.wait_ge(s["htlo"], t.n + 1)
                if not (isinstance(t.i, int) and t.n < 2):
                    pe.wait_ge(s["ret_lo"], t.n - 1)
                    if not (isinstance(t.i, int) and t.n < 3):
                        pe.wait_ge(s["logits_done"], t.n - 2)
                for k in range(KT):
                    ins = nc.tensor.transpose(bank[:, TR_B + k // 4, (k % 4) * P:(k % 4 + 1) * P],
                                              h[:, t.slot, k * P:(k + 1) * P], ident[:])
                ins.then_inc(s["htr"], 1)

            def project(b, col, done):
                three_passes(bank[:, b, :], lambda q, k: h_t[q][:, k * P:(k + 1) * P],
                             lambda q, k: w_in[q][:, k, col:col + BANK], KT, done)

            def kv_products(t):
                pe.wait_ge(s["qkscaled"], t.n + 2)
                pe.wait_ge(s["vcopied"], t.n + 2)
                for hd in range(HEADS):
                    r, j = hd % 2, hd // 2
                    ins = nc.tensor.matmul(bank[r * DK:(r + 1) * DK, GATE_B, j * DV:(j + 1) * DV],
                                           qk[:, (HEADS + hd) * DK:(HEADS + hd + 1) * DK],
                                           v[:, hd * DV:(hd + 1) * DV], start=True, stop=True)
                ins.then_inc(s["kvmm"], 1)

            def body(t):
                static = isinstance(t.i, int)
                main = not static or t.n < TILES
                p, pp = t - 1, t - 2
                if main:
                    pe.wait_ge(s["htlo"], t.n + 2)
                    if not static or t.n > 0:
                        pe.wait_ge(s["masked"], t.n)
                    project(QK_B, 0, "qkdone")
                    if not static or t.n > 0:
                        pe.wait_ge(s["pool_fin"], t.n)
                    project(V_B, QK, "vdone")
                if not static or 1 <= t.n <= TILES:
                    pe.wait_ge(s["ret_fin"], p.n + 1)
                    for k in range(HEADS):
                        ins = nc.tensor.transpose(bank[:, TR_B, k * P:(k + 1) * P], ret[:, k * P:(k + 1) * P], ident[:])
                    ins.then_inc(s["ret_tr"], 1)
                if not static or t.n >= 2:
                    pe.wait_ge(s["h1done"], pp.n + 1)
                    for k in range(KT):
                        ins = nc.tensor.transpose(bank[:, OUT_B + k // 4, (k % 4) * P:(k % 4 + 1) * P],
                                                  h1[:, pp.slot, k * P:(k + 1) * P], ident[:])
                    ins.then_inc(s["h1tr"], 1)
                if main:
                    if static and t.n == 0:
                        pe.wait_ge(s["ucopied"], 1)
                    project(U_B, QK + 2 * RET, "udone")
                if not static or t.n >= 2:
                    pe.wait_ge(s["h1t_copied"], pp.n + 1)
                    for k in range(KT):
                        ins = nc.tensor.matmul(bank[:, TR2_B, 0:LOGITS], h1_t[:, k * P:(k + 1) * P], router_w[:, k, :],
                                               start=k == 0, stop=k == KT - 1)
                    ins.then_inc(s["routermm"], 1)
                if main:
                    pe.wait_ge(s["state_new"], t.n + 1)
                    project(GATE_B, QK + RET, "gatedone")
                    if not static or t.n + 1 < TILES:
                        transpose_h(t + 1)
                if not static or 1 <= t.n <= TILES:
                    pe.wait_ge(s["ret_lo"], p.n + 1)
                    pe.wait_ge(s["pool_lo"], p.n + 1)
                    for half in range(2):
                        three_passes(bank[:, OUT_B + half, :], lambda q, k: mix_t[q][:, k * P:(k + 1) * P],
                                     lambda q, k: w_out[q][:, k, half * BANK:(half + 1) * BANK], KT,
                                     "outmm" if half else None)
                if main:
                    pe.wait_ge(s["qkscaled"], t.n + 2)
                    if not static or t.n + 1 < TILES:
                        pe.wait_ge(s["htlo"], t.n + 3)
                    else:
                        pe.wait_ge(s["logits_done"], pp.n + 1)
                    for j in range(4):
                        ins = nc.tensor.transpose(bank[:, TR_B, j * P:(j + 1) * P], qk[:, j * P:(j + 1) * P], ident[:])
                    ins.then_inc(s["qktr"], 1)
                    pe.wait_ge(s["ucopied"], t.n + 2)
                    for g in range(GROUPS_P):
                        cols = slice(g * P, (g + 1) * P)
                        nc.tensor.matmul(bank[:, TR2_B, cols], u[:, t.slot, cols], band[:, g, :], start=True, stop=False)
                        ins = nc.tensor.matmul(bank[:, TR2_B, cols], u[:, p.slot, cols], band_prev[:, g, :],
                                               start=False, stop=True)
                    ins.then_inc(s["bandmm"], 1)
                    pe.wait_ge(s["qkt_copied"], 3 * t.n + 3)
                    pe.wait_ge(s["rotdone"], t.n + 2)
                    for hd in range(HEADS):
                        ins = nc.tensor.matmul(bank[:, QK_B, hd * P:(hd + 1) * P], k_t[:, hd // 2, :],
                                               q_t[:, hd % 2, hd // 2, :], start=True, stop=True)
                    ins.then_inc(s["scoremm"], 1)
                    pe.wait_ge(s["silu"], t.n + 1)
                    kv_products(t)
                    pe.wait_ge(s["band_copied"], t.n + 1)
                    for g in range(GROUPS_P):
                        cols = slice(g * P, (g + 1) * P)
                        ins = nc.tensor.matmul(bank[:, V_B, cols], pool_w[:, g, :], pooled_t[:, cols],
                                               start=True, stop=True)
                    ins.then_inc(s["poolmm"], 1)
                    pe.wait_ge(s["masked"], t.n + 1)
                    for hd in range(HEADS):
                        cols = slice(hd * DV, (hd + 1) * DV)
                        nc.tensor.matmul(bank[:, U_B, cols], scores[:, hd, :], v[:, cols], start=True, stop=False)
                        ins = nc.tensor.matmul(bank[:, U_B, cols], q_t[:, hd % 2, hd // 2, :],
                                               state[:, hd // 2, :], start=False, stop=True)
                    ins.then_inc(s["retmm"], 1)

            pe.wait_ge(params0, 16 * 4)
            transpose_h(Tile(0, -1))
            pe.wait_ge(w_lo, KT)
            pe.wait_ge(s["htlo"], 1)
            project(QK_B, 0, "qkdone")
            project(V_B, QK, "vdone")
            project(U_B, QK + 2 * RET, "udone")
            kv_products(Tile(0, -1))
            transpose_h(Tile(0, 0))
            pe.wait_ge(w_lo, KT + KT // 2)
            pe.wait_ge(params, 16 * 16)
            run_tiles(pe, FIRST, TILES + 1, LOOP_FROM, LOOP_TO, body)


def router(nc, a, keep):
    ctx = ExitStack()
    with ctx:
        m = Memory(nc, ctx)
        T, G, J, E = TILES, N_GROUPS, PER_GROUP, EXPERTS
        logits = keep["logits"]
        iota = m.sb("iota", [P, P], F32)
        top = m.sb("top", [P, T], F32)
        g_first = m.sb("g_first", [P, T], F32)
        g_exp = m.sb("g_exp", [P, T, G], F32)
        g_cand = m.sb("g_cand", [P, T, G], F32)
        g_prob = m.sb("g_prob", [P, T], F32)
        sel = m.sb("sel", [P, T, J], F32)
        prod = m.sb("prod", [P, T, J], F32)
        cand = m.sb("cand", [P, T, J], F32)
        one_hot = m.sb("one_hot8", [P, T, J], F32)
        best = m.sb("best", [P, 2, T], F32)
        place = m.sb("place", [P, 2, T], F32)
        ratio = m.sb("ratio", [P, T], F32)
        share = m.sb("share", [P, T], F32)
        expert = m.sb("expert", [P, 2, T], F32)
        member = m.sb("member", [P, 2, T, E], F32)
        both = m.sb("both", [P, T, E], F32)
        before = m.sb("before_sb", [P, P], F32)
        ones = m.sb("ones", [P, P], F32)
        count_et = m.sb("count_et", [P, E, T], F32)
        incl_et = m.sb("incl_et", [P, E, T], F32)
        keep_going = m.sb("keep_going", [P, E, T], F32)
        padded = m.sb("padded", [P, E], F32)
        padded_i = m.sb("padded_i", [P, E], I32)
        ends = m.sb("ends", [P, E], F32)
        starts = m.sb("starts", [P, E], F32)
        rank = m.sb("rank", [P, T, E], F32)
        hit = m.sb("hit", [P, T, E], F32)
        dest = m.sb("dest", [P, 2, T], F32)
        dest_i = m.sb("dest_i", [P, 2, T], I32)
        lane = m.sb("lane", [P, 2, T], F32)
        lane_i = m.sb("lane_i", [P, 2, T], I32)
        dblock = m.sb("dblock", [P, 2, T], F32)
        token_no = m.sb("token_no", [P, T], F32)
        lane_hot = m.sb("lane_hot", [P, 2, P], F32)
        block_hot = m.sb("block_hot", [P, 2, TABLE], F32)
        full = m.sb("full", [1, RUN_BLOCKS, E], F32)
        of_block = m.sb("of_block", [1, RUN_BLOCKS], F32)
        slot_i = m.sb("slot_i", [1, RUN_BLOCKS], I32)
        blocks_i = m.sb("blocks_i", [1, 1], U32)
        bank = m.ps("rbank", [P, 8, BANK], F32)
        step, act_step, pe_step, made, loaded = (m.sem(n) for n in ("r_dve", "r_act", "r_pe", "r_made", "r_loaded"))
        hot_made, hot_used = m.sem("hot_made"), m.sem("hot_used")
        block = ctx.enter_context(nc.Block())
        BIG = 1e9

        @block.sync
        def _(sp):
            sp.dma_start(before[:], a["before"]).then_inc(loaded, 16)

        @block.gpsimd
        def _(pool):
            nc.gpsimd.iota(iota[:], pattern=[[1, P]], base=0, channel_multiplier=0,
                           allow_small_or_imprecise_dtypes=True).then_inc(made, 1)
            nc.gpsimd.iota(token_no[:], pattern=[[P, T]], base=0, channel_multiplier=1,
                           allow_small_or_imprecise_dtypes=True).then_inc(made, 1)
            nc.gpsimd.memset(ones[:], 1.0).then_inc(made, 1)
            nc.gpsimd.memset(keep_going[:], 1.0).then_inc(made, 1)

        mark = {}

        @block.vector
        def _(dve):
            chain = Chain(dve, step)
            L = chain.link
            wide = lambda x, n: x.unsqueeze(2).to_broadcast([P, T, n])
            along = lambda n: iota[:, 0:n].unsqueeze(1).to_broadcast([P, T, n])
            dve.wait_ge(made, 4)

            def first_max(values, n, top_out, first_out, cand_t):
                L(nc.vector.tensor_reduce(top_out, values, AX.X, ALU.max))
                L(nc.vector.tensor_tensor(cand_t, values, wide(top_out, n), ALU.is_lt))
                L(nc.vector.scalar_tensor_tensor(out=cand_t, in0=cand_t, scalar=BIG, in1=along(n), op0=ALU.mult,
                                                 op1=ALU.add))
                L(nc.vector.tensor_reduce(first_out, cand_t, AX.X, ALU.min))

            g_logits = logits[:, :, 0:G]
            first_max(g_logits, G, top[:], g_first[:], g_cand[:])
            L(nc.vector.tensor_tensor(g_exp[:], g_logits, wide(top[:], G), ALU.subtract))
            mark["g_shifted"] = chain.steps
            for g in range(G):
                L(nc.vector.tensor_scalar(share[:], g_first[:], float(g), None, ALU.is_equal))
                dst = sel if g == 0 else prod
                L(nc.vector.tensor_tensor(dst[:], logits[:, :, G + g * J:G + (g + 1) * J], wide(share[:], J), ALU.mult))
                if g:
                    L(nc.vector.tensor_tensor(sel[:], sel[:], prod[:], ALU.add))
            first_max(sel[:], J, best[:, 0, :], place[:, 0, :], cand[:])
            L(nc.vector.tensor_tensor(one_hot[:], along(J), wide(place[:, 0, :], J), ALU.is_equal))
            L(nc.vector.scalar_tensor_tensor(out=prod[:], in0=one_hot[:], scalar=-3e38, in1=sel[:], op0=ALU.mult,
                                             op1=ALU.add))
            first_max(prod[:], J, best[:, 1, :], place[:, 1, :], cand[:])
            L(nc.vector.tensor_tensor(ratio[:], best[:, 1, :], best[:, 0, :], ALU.subtract))
            mark["ratio"] = chain.steps
            for k in range(2):
                L(nc.vector.scalar_tensor_tensor(out=expert[:, k, :], in0=g_first[:], scalar=float(J),
                                                 in1=place[:, k, :], op0=ALU.mult, op1=ALU.add))
                L(nc.vector.tensor_tensor(member[:, k, :, :], along(E), wide(expert[:, k, :], E), ALU.is_equal))
            L(nc.vector.tensor_tensor(both[:], member[:, 0, :, :], member[:, 1, :, :], ALU.add))
            mark["both"] = chain.steps
            dve.wait_ge(act_step, 1)
            L(nc.vector.tensor_reduce(g_prob[:], g_exp[:], AX.X, ALU.add))
            L(nc.vector.reciprocal(g_prob[:], g_prob[:]))
            dve.wait_ge(act_step, 2)
            L(nc.vector.tensor_scalar(share[:], ratio[:], 1.0, None, ALU.add))
            L(nc.vector.reciprocal(share[:], share[:]))
            L(nc.vector.tensor_tensor(keep["pair_w"][:, 0, :], g_prob[:], share[:], ALU.mult))
            L(nc.vector.tensor_tensor(keep["pair_w"][:, 1, :], keep["pair_w"][:, 0, :], ratio[:], ALU.mult))
            dve.wait_ge(pe_step, 1)
            for b in range(2):
                tt = slice(b * T // 2, (b + 1) * T // 2)
                L(nc.vector.tensor_copy(count_et[:, :, tt].rearrange("p e t -> p t e"),
                                        bank[:, b, :].rearrange("p (t e) -> p t e", e=E)))
            L(nc.vector.tensor_scalar(keep_going[:, :, 0:1], keep_going[:, :, 0:1], 0.0, None, ALU.mult))
            flat = lambda x: x[:].rearrange("p e t -> p (e t)")
            L(nc.vector.tensor_tensor_scan(flat(incl_et), flat(keep_going), flat(count_et), 0.0, ALU.mult, ALU.add))
            L(nc.vector.tensor_scalar(padded_i[:], incl_et[:, :, T - 1], float(P - 1), None, ALU.add))
            L(nc.vector.tensor_scalar(padded_i[:], padded_i[:], 7, None, ALU.logical_shift_right))
            L(nc.vector.tensor_scalar(padded[:], padded_i[:], 1.0, None, ALU.max))
            L(nc.vector.tensor_tensor_scan(ends[:], ones[:, 0:E], padded[:], 0.0, ALU.mult, ALU.add))
            L(nc.vector.tensor_copy(keep["ends"][:], ends[0:1, :]))
            L(nc.vector.tensor_copy(blocks_i[:], ends[0:1, E - 1:E]))
            L(nc.vector.tensor_scalar(keep["pairs"][:], blocks_i[:], 1, None, ALU.logical_shift_right))
            L(nc.vector.tensor_scalar(keep["unused"][:], keep["pairs"][:], -1.0, float(BLOCKS // 2), ALU.mult, ALU.add))
            L(nc.vector.tensor_tensor(starts[:], ends[:], padded[:], ALU.subtract))
            L(nc.vector.tensor_tensor(count_et[:], incl_et[:], count_et[:], ALU.subtract))
            L(nc.vector.scalar_tensor_tensor(out=count_et[:], in0=starts[:].unsqueeze(2).to_broadcast([P, E, T]),
                                             scalar=float(P), in1=count_et[:], op0=ALU.mult, op1=ALU.add))
            dve.wait_ge(pe_step, 2)
            for b in range(2):
                tt = slice(b * T // 2, (b + 1) * T // 2)
                L(nc.vector.tensor_tensor(rank[:, tt, :], bank[:, 2 + b, :].rearrange("p (t e) -> p t e", e=E),
                                          count_et[:, :, tt].rearrange("p e t -> p t e"), ALU.add))
            for k in range(2):
                L(nc.vector.tensor_tensor(hit[:], rank[:], member[:, k, :, :], ALU.mult))
                L(nc.vector.tensor_reduce(dest[:, k, :], hit[:], AX.X, ALU.add))
            L(nc.vector.tensor_copy(dest_i[:], dest[:]))
            L(nc.vector.tensor_copy(keep["dest"][:], dest[:]))
            L(nc.vector.tensor_scalar(lane_i[:], dest_i[:], P - 1, None, ALU.bitwise_and))
            L(nc.vector.tensor_copy(lane[:], lane_i[:]))
            L(nc.vector.tensor_tensor(dblock[:], dest[:], lane[:], ALU.subtract))
            L(nc.vector.tensor_scalar(dblock[:], dblock[:], 1.0 / P, None, ALU.mult))
            L(nc.vector.tensor_tensor(full[:], iota[0:1, 0:RUN_BLOCKS].unsqueeze(2).to_broadcast([1, RUN_BLOCKS, E]),
                                      ends[0:1, :].unsqueeze(1).to_broadcast([1, RUN_BLOCKS, E]), ALU.is_ge))
            L(nc.vector.tensor_reduce(of_block[:], full[:], AX.X, ALU.add))
            L(nc.vector.tensor_scalar(of_block[:], of_block[:], float(E - 1), None, ALU.min))
            L(nc.vector.tensor_copy(slot_i[:], of_block[:]))
            L(nc.vector.tensor_scalar(slot_i[:], slot_i[:], 1, None, ALU.bitwise_and))
            L(nc.vector.tensor_scalar(keep["block_part"][:], of_block[:], 3.0, None, ALU.mult))
            L(nc.vector.tensor_scalar(keep["block_slot"][:], slot_i[:], float(SLOT), None, ALU.mult))
            for n in range(2 * T):
                k, t = n // T, n % T
                if n >= 2:
                    dve.wait_ge(hot_used, n - 1)
                nc.vector.tensor_scalar(lane_hot[:, n % 2, :], iota[:], lane[:, k, t:t + 1], None, ALU.is_equal)
                nc.vector.tensor_scalar(block_hot[:, n % 2, :], iota[:, 0:TABLE], dblock[:, k, t:t + 1],
                                        token_no[:, t:t + 1], ALU.is_equal, ALU.mult).then_inc(hot_made, 1)
            dve.wait_ge(pe_step, 3)
            nc.vector.tensor_copy(keep["tokens"][:], bank[:, 4, 0:TABLE])

        @block.scalar
        def _(act):
            act.wait_ge(step, mark["g_shifted"])
            nc.scalar.activation(g_exp[:], g_exp[:], ACT.Exp).then_inc(act_step, 1)
            act.wait_ge(step, mark["ratio"])
            nc.scalar.activation(ratio[:], ratio[:], ACT.Exp).then_inc(act_step, 1)

        @block.tensor
        def _(pe):
            pe.wait_ge(loaded, 16)
            pe.wait_ge(step, mark["both"])
            flat = both[:].rearrange("p t e -> p (t e)")
            for b in range(2):
                ins = nc.tensor.matmul(bank[:, b, :], ones[:], flat[:, b * BANK:(b + 1) * BANK], start=True, stop=True)
            ins.then_inc(pe_step, 1)
            for b in range(2):
                ins = nc.tensor.matmul(bank[:, 2 + b, :], before[:], flat[:, b * BANK:(b + 1) * BANK], start=True, stop=True)
            ins.then_inc(pe_step, 1)
            for n in range(2 * T):
                pe.wait_ge(hot_made, n + 1)
                nc.tensor.matmul(bank[:, 4, 0:TABLE], lane_hot[:, n % 2, :], block_hot[:, n % 2, :],
                                 start=n == 0, stop=n == 2 * T - 1).then_inc(hot_used, 1)
            pe.wait_ge(hot_used, 2 * T)
            pe.sem_inc(pe_step, 1)


def experts(nc, a, keep):
    ctx = ExitStack()
    with ctx:
        m = Memory(nc, ctx)
        raw = m.sb("raw", [P, 2 * SLOT], F32)
        w_lo = m.sb("w_low", [P, 2 * SLOT], BF16)
        w_hi = raw[:].bitcast(BF16)
        xg = m.sb("xg", [P, 2, 2 * D], BF16)
        x_t = [m.sb(f"x_t{q}", [P, 2, D], dt) for q, dt in enumerate((BF16, F16))]
        silu_g = m.sb("silu_g", [P, D_E], F32)
        up = m.sb("up", [P, D_E], F32)
        hid = m.sb("hid", [P, D_E], F32)
        hid_parts = [m.sb(f"hid_parts{q}", [P, D_E], dt) for q, dt in enumerate((BF16, F16))]
        hid_t = [m.sb(f"hid_t{q}", [P, D_E], dt) for q, dt in enumerate((BF16, F16))]
        y = m.sb("y", [P, 2, D], F32)
        index = m.sb("index", [P, 2], U32)
        zeros = m.sb("zeros", [P, D], F32)
        ident = [m.sb(f"ident_{q}", [P, P], dt) for q, dt in enumerate((BF16, F16))]
        ident_f = m.sb("ident_f", [P, P], F32)
        GATE_B, UP_B, Y_B = 0, 1, 2
        bank = m.ps("ebank", [P, 4, BANK], F32)
        xtr = [m.ps(f"xtr{q}", [P, D], dt) for q, dt in enumerate((BF16, F16))]
        htr = [m.ps(f"htr{q}", [P, D_E], dt) for q, dt in enumerate((BF16, F16))]
        xg_parts = [xg[:, :, 0:D], xg[:, :, D:2 * D].bitcast(F16)]
        s = {n: m.sem("e_" + n) for n in ("xtr xt_copied gate up silu upcopied hid hidhi hidlo htr ht_copied "
                                          "down ycopied low indexed gone ended").split()}
        w_loaded = [[m.sem(f"w_loaded{i}{j}") for j in range(3)] for i in range(2)]
        gathered = [m.sem(f"gathered{i}") for i in range(2)]
        stored = [m.sem(f"y_stored{i}") for i in range(2)]
        rest_stored = m.sem("rest_stored")
        ready, id_loaded, id_made = m.sem("e_ready"), m.sem("e_id_loaded"), m.sem("e_id_made")
        block = ctx.enter_context(nc.Block())

        def pairs_of(eng):
            return eng.value_load(keep["pairs"][:], min_val=EXPERTS // 2, max_val=BLOCKS // 2)

        @block.sync
        def _(sp):
            sp.dma_start(ident_f[:], a["ident"]).then_inc(id_loaded, 16)
            srcs = [a["w_gate"].rearrange("e (k p) n -> e p k n", p=P), a["w_up"].rearrange("e (k p) n -> e p k n", p=P),
                    a["w_down"].rearrange("e (k p) n -> e p k n", p=P)]

            def load(e):
                for part in range(3):
                    width = D if part == 2 else D_E
                    dst = raw[:, e.slot * SLOT + part * PART:e.slot * SLOT + (part + 1) * PART]
                    sp.dma_start(dst.rearrange("p (k n) -> p k n", n=width),
                                 srcs[part][bass.ds(e.n, 1), :, :, :].squeeze(0)).then_inc(w_loaded[e.slot][part], 16)

            load(Tile(0, 0))
            load(Tile(0, 1))
            pairs = pairs_of(sp)
            sp.wait_ge(ready, 2)
            with sp.Fori(pairs, BLOCKS // 2) as i:
                for k in range(1, 3):
                    sp.dma_start(keep["y_dram"][bass.ds((2 * i + k) * P, P), :], zeros[:]).then_inc(rest_stored, 16)
            with sp.Fori(0, EXPERTS // 2 - 1) as i:
                for k in range(2):
                    e = Tile(i, 2 + k)
                    end = sp.value_load(keep["ends"][0:1, bass.ds((e - 2).n, 1)], min_val=1, max_val=BLOCKS)
                    sp.wait_ge(s["down"], end)
                    load(e)
            unused = sp.value_load(keep["unused"][:], min_val=0, max_val=(BLOCKS - EXPERTS) // 2)
            sp.wait_ge(rest_stored, 32 * unused)
            sp.sem_inc(s["ended"], 1)

        @block.vector
        def _(dve):
            dve.wait_ge(id_loaded, 16)
            nc.vector.tensor_copy(ident[0][:], ident_f[:]).then_inc(id_made, 1)
            nc.vector.tensor_copy(ident[1][:], ident_f[:]).then_inc(id_made, 1)
            with dve.Fori(0, EXPERTS // 2) as i:
                for slot in range(2):
                    for part in range(3):
                        a0 = slot * SLOT + part * PART
                        dve.wait_ge(w_loaded[slot][part], 16 * i + 16)
                        nc.vector.tensor_tensor(w_lo[:, a0:a0 + PART], raw[:, a0:a0 + PART],
                                                w_hi[:, 2 * a0 + 1:2 * (a0 + PART):2], ALU.subtract).then_inc(s["low"], 1)

        @block.gpsimd
        def _(pool):
            nc.gpsimd.memset(hid[:], 0.0).then_inc(ready, 1)
            nc.gpsimd.memset(zeros[:], 0.0).then_inc(ready, 1)

            def gather(b):
                static = isinstance(b.i, int)
                if not static or b.n >= 2:
                    pool.wait_ge(s["xtr"], b.n - 1)
                nc.gpsimd.tensor_copy(index[:, b.slot:b.slot + 1], keep["tokens"][:, bass.ds(b.n, 1)]).then_inc(s["indexed"], 1)
                pool.wait_ge(s["indexed"], b.n + 1)
                pool.sem_inc(s["gone"], 1)
                nc.gpsimd.indirect_dma_start(xg[:, b.slot, :], None, keep["parts_dram"],
                                             bass.IndirectOffsetOnAxis(ap=index[:, b.slot:b.slot + 1], axis=0)
                                             ).then_inc(gathered[b.slot], 16)

            def body(b):
                static = isinstance(b.i, int)
                gather(b + 2)
                pool.wait_ge(s["silu"], b.n + 1)
                pool.wait_ge(s["upcopied"], b.n + 1)
                if not static or b.n > 0:
                    pool.wait_ge(s["hidlo"], b.n)
                nc.gpsimd.tensor_tensor(hid[:], silu_g[:], up[:], ALU.mult).then_inc(s["hid"], 1)
                pool.wait_ge(s["hidhi"], b.n + 1)
                nc.gpsimd.tensor_tensor(hid_parts[1][:], hid[:], hid_parts[0][:], ALU.subtract).then_inc(s["hidlo"], 1)

            gather(Tile(0, 0))
            gather(Tile(0, 1))
            body(Tile(0, 0))
            pairs = pairs_of(pool)
            with pool.Fori(0, pairs) as i:
                body(Tile(i, 1))
                body(Tile(i, 2))
            pool.wait_ge(gathered[0], 16 * (pairs + 2))
            pool.sem_inc(s["ended"], 1)

        @block.scalar
        def _(act):
            def copy_out(dst, src, wait, count, done):
                act.wait_ge(s[wait], count)
                nc.scalar.activation(dst, src, ACT.Copy).then_inc(s[done], 1)

            def copy_x(b):
                for q in range(2):
                    copy_out(x_t[q][:, b.slot, :], xtr[q][:], "xtr", b.n + 1, "xt_copied")

            def hid_out(p):
                act.wait_ge(s["down"], p.n)
                for q in range(2):
                    copy_out(hid_t[q][:], htr[q][:], "htr", p.n + 1, "ht_copied")

            def y_out(p):
                act.wait_ge(stored[p.slot], 16 * p.half)
                copy_out(y[:, p.slot, :], bank[:, Y_B:Y_B + 2, :].rearrange("p b n -> p (b n)"), "down", p.n + 1,
                         "ycopied")
                act.wait_ge(s["ycopied"], p.n + 1)
                act.dma_start(keep["y_dram"][bass.ds(p.n * P, P), :], y[:, p.slot, :]).then_inc(stored[p.slot], 16)

            def body(b, before=True):
                copy_x(b + 1)
                act.wait_ge(s["gate"], b.n + 1)
                if before:
                    act.wait_ge(s["hid"], b.n)
                nc.scalar.activation(silu_g[:], bank[:, GATE_B, :], ACT.Silu).then_inc(s["silu"], 1)
                if before:
                    hid_out(b - 1)
                copy_out(up[:], bank[:, UP_B, :], "up", b.n + 1, "upcopied")
                act.wait_ge(s["hid"], b.n + 1)
                if before:
                    act.wait_ge(s["htr"], b.n)
                nc.scalar.activation(hid_parts[0][:], hid[:], ACT.Copy).then_inc(s["hidhi"], 1)
                if before:
                    y_out(b - 1)

            copy_x(Tile(0, 0))
            body(Tile(0, 0), before=False)
            pairs = pairs_of(act)
            with act.Fori(0, pairs) as i:
                body(Tile(i, 1))
                body(Tile(i, 2))
            hid_out(Tile(pairs, 0))
            y_out(Tile(pairs, 0))
            act.wait_ge(stored[0], 16 * (pairs + 1))
            act.wait_ge(stored[1], 16 * pairs)
            act.sem_inc(s["ended"], 1)

        @block.tensor
        def _(pe):
            def transpose_x(b):
                static = isinstance(b.i, int)
                pe.wait_ge(gathered[b.slot], 16 * b.half + 16)
                if not static or b.n > 0:
                    pe.wait_ge(s["xt_copied"], 2 * b.n)
                for q in range(2):
                    for k in range(KT):
                        cols = slice(k * P, (k + 1) * P)
                        ins = nc.tensor.transpose(xtr[q][:, cols], xg_parts[q][:, b.slot, cols], ident[q][:])
                ins.then_inc(s["xtr"], 1)

            def passes(dst, lhs, at, stride, kts, done):
                hi = lambda k: w_hi[:, bass.ds(at * 2 + (2 * k * stride + 1), BANK, step=2)]
                lo = lambda k: w_lo[:, bass.ds(at + k * stride, BANK)]
                for k in range(kts):
                    nc.tensor.matmul(dst, lhs(0, k), hi(k), start=k == 0, stop=False)
                    nc.tensor.matmul(dst, lhs(0, k), lo(k), start=False, stop=False)
                    ins = nc.tensor.matmul(dst, lhs(1, k), hi(k), start=False, stop=k == kts - 1)
                if done is not None:
                    ins.then_inc(s[done], 1)

            def down(b, at, part):
                pe.wait_ge(s["low"], part + 3)
                pe.wait_ge(s["ht_copied"], 2 * b.n + 2)
                if not isinstance(b.i, int) or b.n > 0:
                    pe.wait_ge(s["ycopied"], b.n)
                for half in range(2):
                    passes(bank[:, Y_B + half, :], lambda q, k: hid_t[q][:, k * P:(k + 1) * P],
                           at + (2 * PART + half * BANK), D, HT, "down" if half else None)

            def where(b):
                at = pe.value_load(keep["block_slot"][0:1, bass.ds(b.n, 1)], min_val=0, max_val=SLOT)
                part = pe.value_load(keep["block_part"][0:1, bass.ds(b.n, 1)], min_val=0, max_val=3 * (EXPERTS - 1))
                return at, part

            def transpose_hid(p):
                pe.wait_ge(s["hidlo"], p.n + 1)
                pe.wait_ge(s["hidhi"], p.n + 1)
                pe.wait_ge(s["ht_copied"], 2 * p.n)
                for q in range(2):
                    for k in range(HT):
                        cols = slice(k * P, (k + 1) * P)
                        ins = nc.tensor.transpose(htr[q][:, cols], hid_parts[q][:, cols], ident[q][:])
                ins.then_inc(s["htr"], 1)

            def body(b, before=True):
                at, part = where(b)
                transpose_x(b + 1)
                x = lambda q, k: x_t[q][:, b.slot, k * P:(k + 1) * P]
                pe.wait_ge(s["low"], part + 1)
                pe.wait_ge(s["xt_copied"], 2 * b.n + 2)
                if before:
                    pe.wait_ge(s["silu"], b.n)
                passes(bank[:, GATE_B, :], x, at, D_E, KT, "gate")
                if before:
                    transpose_hid(b - 1)
                pe.wait_ge(s["low"], part + 2)
                if before:
                    pe.wait_ge(s["upcopied"], b.n)
                passes(bank[:, UP_B, :], x, at + PART, D_E, KT, "up")
                if before:
                    down(b - 1, *where(b - 1))

            pe.wait_ge(id_made, 2)
            transpose_x(Tile(0, 0))
            body(Tile(0, 0), before=False)
            pairs = pairs_of(pe)
            with pe.Fori(0, pairs) as i:
                body(Tile(i, 1))
                body(Tile(i, 2))
            last = Tile(pairs, 0)
            transpose_hid(last)
            down(last, *where(last))


def combine(nc, a, keep):
    ctx = ExitStack()
    with ctx:
        m = Memory(nc, ctx)
        g, b = m.sb("ln2_g_sb", [P, D], F32), m.sb("ln2_b_sb", [P, D], F32)
        rows = m.sb("rows", [P, 2, TOP, D], F32)
        h1 = m.sb("h1_back", [P, 2, D], F32)
        mixed = m.sb("mixed", [P, 2, D], F32)
        index = m.sb("c_index", [P, 2, TOP], U32)
        stats = m.sb("c_stats", [P, 2, 6], F32)
        moments = m.sb("c_moments", [P, 2], F32)
        rstd = m.sb("c_rstd", [P, 2], F32)
        minus_half, eps = m.sb("c_minus_half", [P, 1], F32), m.sb("c_eps", [P, 1], F32)
        s = {n: m.sem("c_" + n) for n in "indexed weighted mixed stats rstd done ready params pool dve passed gone".split()}
        gathered = [m.sem(f"c_gathered{i}") for i in range(2)]
        loaded = [m.sem(f"c_loaded{i}") for i in range(2)]
        stored = [m.sem(f"c_stored{i}") for i in range(2)]
        block = ctx.enter_context(nc.Block())

        @block.sync
        def _(sp):
            def load(t):
                if not isinstance(t.i, int) or t.n >= 2:
                    sp.wait_ge(s["mixed"], t.n - 1)
                sp.dma_start(h1[:, t.slot, :], keep["h1_dram"][bass.ds(t.n * P, P), :]).then_inc(loaded[t.slot], 16)

            def store(t):
                sp.wait_ge(s["done"], t.n + 1)
                sp.dma_start(a["out"][bass.ds(t.n * P, P), :], mixed[:, t.slot, :]).then_inc(stored[t.slot], 16)

            sp.dma_start(g[:], a["ln2_g"].partition_broadcast(P)).then_inc(s["params"], 16)
            sp.dma_start(b[:], a["ln2_b"].partition_broadcast(P)).then_inc(s["params"], 16)
            load(Tile(0, 0))
            load(Tile(0, 1))
            with sp.Fori(0, TILES // 2 - 1) as i:
                for k in range(2):
                    load(Tile(i, k + 2))
                    store(Tile(i, k))
            store(Tile(0, TILES - 2))
            store(Tile(0, TILES - 1))
            for slot in range(2):
                sp.wait_ge(stored[slot], 16 * (TILES // 2))

        @block.gpsimd
        def _(pool):
            nc.gpsimd.memset(minus_half[:], -0.5).then_inc(s["ready"], 1)
            nc.gpsimd.memset(eps[:], LN_EPS).then_inc(s["ready"], 1)
            pool.wait_ge(s["ready"], 2)

            def gather(t):
                if not isinstance(t.i, int) or t.n >= 2:
                    pool.wait_ge(s["mixed"], t.n - 1)
                nc.gpsimd.tensor_copy(index[:, t.slot, :], keep["dest"][:, :, bass.ds(t.n, 1)].squeeze(2)).then_inc(s["indexed"], 1)
                pool.wait_ge(s["indexed"], t.n + 1)
                pool.sem_inc(s["gone"], 1)
                for k in range(TOP):
                    nc.gpsimd.indirect_dma_start(rows[:, t.slot, k, :], None, keep["y_dram"],
                                                 bass.IndirectOffsetOnAxis(ap=index[:, t.slot, k:k + 1], axis=0)
                                                 ).then_inc(gathered[t.slot], 16)

            def root(t):
                pool.wait_ge(s["stats"], t.n + 1)
                nc.gpsimd.tensor_tensor(rstd[:, 1:2], moments[:, 1:2], eps[:], ALU.add).then_inc(s["pool"], 1)
                pool.wait_ge(s["pool"], t.n + 1)
                nc.gpsimd.tensor_tensor(rstd[:, 0:1], rstd[:, 1:2], minus_half[:], ALU.pow).then_inc(s["rstd"], 1)

            gather(Tile(0, 0))
            gather(Tile(0, 1))
            with pool.Fori(0, TILES // 2 - 1) as i:
                for k in range(2):
                    root(Tile(i, k))
                    gather(Tile(i, k + 2))
            root(Tile(0, TILES - 2))
            root(Tile(0, TILES - 1))

        @block.scalar
        def _(act):
            with act.Fori(0, TILES // 2) as i:
                for k in range(2):
                    t = Tile(i, k)
                    act.wait_ge(gathered[k], 32 * i + 32)
                    nc.scalar.activation(rows[:, k, 0, :], rows[:, k, 0, :], ACT.Copy,
                                         scale=keep["pair_w"][:, 0, bass.ds(t.n, 1)]).then_inc(s["weighted"], 1)

        @block.vector
        def _(dve):
            chain = Chain(dve, s["dve"])
            STEPS = 4
            dve.wait_ge(s["params"], 32)

            def body(t, later):
                slot = t.slot
                out = mixed[:, slot, :]
                dve.wait_ge(s["weighted"], t.n + 1)
                if later:
                    dve.wait_ge(stored[slot], 16 * t.half)
                chain.link(nc.vector.scalar_tensor_tensor(out=out, in0=rows[:, slot, 1, :],
                                                          scalar=keep["pair_w"][:, 1, bass.ds(t.n, 1)],
                                                          in1=rows[:, slot, 0, :], op0=ALU.mult, op1=ALU.add))
                dve.wait_ge(loaded[slot], 16 * t.half + 16)
                ins = nc.vector.scalar_tensor_tensor(out=out, in0=h1[:, slot, :], scalar=ALPHA, in1=out, op0=ALU.mult,
                                                     op1=ALU.add)
                ins.then_inc(s["mixed"], 1)
                dve.wait_ge(s["mixed"], t.n + 1)
                nc.vector.bn_stats(stats[:, 0, :], mixed[:, slot, 0:BANK])
                chain.link(nc.vector.bn_stats(stats[:, 1, :], mixed[:, slot, BANK:D]), s["passed"])
                nc.vector.bn_aggr(moments[:], stats[:]).then_inc(s["stats"], 1)
                dve.wait_ge(s["stats"], t.n + 1)
                chain.link(nc.vector.scalar_tensor_tensor(out=out, in0=out, scalar=moments[:, 0:1], in1=g[:],
                                                          op0=ALU.subtract, op1=ALU.mult))
                dve.wait_ge(s["rstd"], t.n + 1)
                nc.vector.scalar_tensor_tensor(out=out, in0=out, scalar=rstd[:, 0:1], in1=b[:], op0=ALU.mult,
                                               op1=ALU.add).then_inc(s["done"], 1)

            body(Tile(0, 0), False)
            body(Tile(0, 1), False)
            STEPS = chain.steps // 2
            with dve.Fori(0, TILES // 2 - 1) as i:
                for k in range(2):
                    chain.base, chain.steps = (2 + k) * STEPS + i * (2 * STEPS), 0
                    body(Tile(i, 2 + k), True)
                    assert chain.steps == STEPS


def program(nc, a, stop=None):
    with ExitStack() as ctx:
        sb = lambda name, shape, dt: ctx.enter_context(nc.sbuf_tensor(name, shape, dt))
        keep = {
            "logits": sb("logits", [P, TILES, LOGITS], F32),
            "pair_w": sb("pair_w", [P, 2, TILES], F32),
            "dest": sb("dest_rows", [P, 2, TILES], U32),
            "tokens": sb("tokens", [P, TABLE], U32),
            "pairs": sb("pairs", [1, 1], U32),
            "unused": sb("unused", [1, 1], U32),
            "ends": sb("ends_i", [1, EXPERTS], U32),
            "block_slot": sb("block_slot", [1, RUN_BLOCKS], U32),
            "block_part": sb("block_part", [1, RUN_BLOCKS], U32),
            "h1_dram": nc.dram_tensor("h1_dram", [SEQ, D], F32, kind="Internal").ap(),
            "parts_dram": nc.dram_tensor("parts_dram", [SEQ, 2 * D], BF16, kind="Internal").ap(),
            "y_dram": nc.dram_tensor("y_dram", [RUN_BLOCKS * P, D], F32, kind="Internal").ap(),
        }
        mixer(nc, a, keep)
        router(nc, a, keep)
        experts(nc, a, keep)
        combine(nc, a, keep)


def laid_out(inputs):
    g = lambda name: np.asarray(inputs[name])
    row = lambda x: np.ascontiguousarray(x).reshape(-1)
    col = lambda x: np.ascontiguousarray(x.reshape(GROUPS_P, P).T)
    arrays = {
        "x": g("x")[0], "meta": g("meta_tokens"), "ln0_g": row(g("ln_emb_g")), "ln0_b": row(g("ln_emb_b")),
        "w_in": g("w_in")[0], "pool_w": g("pool_w")[0], "pool_b": col(g("pool_b")[0]),
        "pool_scale": col(g("pool_scale")[0]), "w_out": g("w_out")[0], "ln1_g": row(g("ln1_g")[0]),
        "ln1_b": row(g("ln1_b")[0]), "rg_w": g("router_group_w")[0], "rg_b": row(g("router_group_b")[0]),
        "re_w": g("router_expert_w")[0], "re_b": row(g("router_expert_b")[0]), "w_gate": g("expert_w_gate")[0],
        "w_up": g("expert_w_up")[0], "w_down": g("expert_w_down")[0], "ln2_g": row(g("ln2_g")[0]),
        "ln2_b": row(g("ln2_b")[0]),
    }
    arrays.update(shape_constants())
    return {"in_" + k: np.ascontiguousarray(v) for k, v in arrays.items()}


def kernel(**inputs):
    import concourse.bacc as bacc
    from concourse.bass_utils import run_bass_kernel_spmd

    arrays = laid_out(inputs)
    nc = bacc.Bacc("TRN2", target_bir_lowering=False, num_devices=1)
    a = {k[3:]: nc.dram_tensor(k, v.shape, mybir.dt.from_np(v.dtype), kind="ExternalInput").ap()
         for k, v in arrays.items()}
    a["out"] = nc.dram_tensor("out", [SEQ, D], F32, kind="ExternalOutput").ap()
    program(nc, a)
    r = run_bass_kernel_spmd(nc, [arrays], core_ids=[0])
    return r.results[0]["out"].reshape(1, SEQ, D)
```

```python
from contextlib import ExitStack

import numpy as np

import concourse.bass as bass
from concourse import mybir

ALU = mybir.AluOpType
ACT = mybir.ActivationFunctionType
AX = mybir.AxisListType
F32 = mybir.dt.float32
BF16 = mybir.dt.bfloat16
F16 = mybir.dt.float16
I32 = mybir.dt.int32
U32 = mybir.dt.uint32

P = 128
D = 1024
KT = D // P
SEQ = 4096
TILES = SEQ // P
N_META = 16
HEADS = 4
DK = 64
DV = 128
HALF = DK // 2
QK = 2 * HEADS * DK
RET = HEADS * DV
POOL_WINDOWS = (2, 4, 8, 16)
GROUPS_P = len(POOL_WINDOWS)
POOL = GROUPS_P * P
IN_COLS = QK + 2 * RET + POOL
BANK = 512
N_GROUPS = 4
PER_GROUP = 8
EXPERTS = N_GROUPS * PER_GROUP
LOGITS = N_GROUPS + EXPERTS
D_E = 512
HT = D_E // P
TOP = 2
BLOCKS = SEQ * TOP // P + EXPERTS
RUN_BLOCKS = BLOCKS + 1
TABLE = RUN_BLOCKS + 2
SLOT = 2 * KT * D_E + HT * D
PART = SLOT // 3
LN_EPS = 1e-5
GN_EPS = 1e-6
ALPHA = 2 ** 0.25
W_SCALE = 256.0


def shape_constants():
    inv = np.power(10000.0, -np.arange(HALF) / HALF).astype(np.float32)
    row = np.arange(P)
    pos = (np.arange(-1, TILES)[:, None] * P + row[None, :] + N_META).astype(np.float32)
    angle = (np.maximum(pos, 0)[:, :, None] * inv).astype(np.float64)
    cos = np.cos(angle).astype(np.float32).transpose(1, 0, 2)
    sin = np.sin(angle).astype(np.float32).transpose(1, 0, 2)
    log_g = np.log1p(-np.power(2.0, -5.0 - np.arange(HEADS)))
    decay = np.concatenate([np.exp((row[:, None] + 1) * log_g), np.exp(-(row[:, None] + 1) * log_g) * DK ** -0.5], 1)
    chunk = np.exp(P * log_g)
    chunk_decay = np.stack([np.repeat(chunk[2 * p:2 * p + 2], DK) for p in range(HEADS // 2)], 1)
    j, i = row[:, None], row[None, :]
    causal = (j <= i).astype(np.float32)
    band = np.stack([((i - j >= 0) & (i - j < w)) / w - (i == j) for w in POOL_WINDOWS], 1)
    band_prev = np.stack([(i - j + P < w) / w for w in POOL_WINDOWS], 1)
    return {
        "cos": np.ascontiguousarray(cos / W_SCALE, np.float32), "sin": np.ascontiguousarray(sin / W_SCALE, np.float32),
        "decay": decay.astype(np.float32), "chunk_decay": chunk_decay.astype(np.float32),
        "causal": causal, "band": band.astype(np.float16), "band_prev": band_prev.astype(np.float16),
        "ident": np.eye(P, dtype=np.float32), "meta_rows": (row >= P - N_META).astype(np.float32)[:, None],
        "before": (j < i).astype(np.float32),
    }


class Tile:

    def __init__(self, i, k, slots=2):
        self.i, self.k, self.slots = i, k, slots

    @property
    def n(self):
        return self.slots * self.i + self.k

    @property
    def slot(self):
        return self.k % self.slots

    @property
    def round(self):
        return self.i + self.k // self.slots

    def __add__(self, d):
        return Tile(self.i, self.k + d, self.slots)

    def __sub__(self, d):
        return self + -d


def run_tiles(eng, first, last, loop_from, loop_to, body):
    for t in range(first, loop_from):
        body(Tile(0, t))
    pairs = (loop_to - loop_from + 1) // 2
    with eng.Fori(0, pairs) as i:
        body(Tile(i, loop_from))
        body(Tile(i, loop_from + 1))
    for t in range(loop_to + 1, last + 1):
        body(Tile(0, t))


def wait_past(eng, sem, value):
    if not (isinstance(value, int) and value <= 0):
        eng.wait_ge(sem, value)


class Chain:

    def __init__(self, eng, sem):
        self.eng, self.sem, self.base, self.steps = eng, sem, 0, 0

    def link(self, ins, passed=None):
        ins.then_inc(self.sem, 1)
        self.steps += 1
        self.eng.wait_ge(self.sem, self.base + self.steps)
        if passed is not None:
            self.eng.sem_inc(passed, 1)


class Memory:
    def __init__(self, nc, ctx):
        self.nc, self.ctx = nc, ctx

    def sb(self, name, shape, dt):
        return self.ctx.enter_context(self.nc.sbuf_tensor(name, shape, dt))

    def ps(self, name, shape, dt):
        return self.ctx.enter_context(self.nc.psum_tensor(name, shape, dt))

    def sem(self, name):
        return self.ctx.enter_context(self.nc.semaphore(name))


def mixer(nc, a, keep):
    ctx = ExitStack()
    with ctx:
        m = Memory(nc, ctx)
        w_in = [m.sb(f"w_in{q}", [P, KT, IN_COLS], dt) for q, dt in enumerate((BF16, F16))]
        w_out = [m.sb(f"w_out{q}", [P, KT, D], dt) for q, dt in enumerate((BF16, F16))]
        stage = m.sb("stage", [P, 2, 2 * D], F32)
        h1 = stage[:, :, 0:D]
        h1_parts = [stage[:, :, D:3 * D // 2].bitcast(BF16), stage[:, :, 3 * D // 2:2 * D].bitcast(F16)]
        parked = [w[:].rearrange("p k n -> p (k n)").bitcast(F32)[:, i * 2 * D:(i + 1) * 2 * D]
                  for w in w_out for i in range(2)]
        chunk_at = [stage[:, 0, :], stage[:, 1, :]] + parked
        CHUNKS = KT + KT // 2

        def chunk_buffer(k):
            buffer = k if k < len(chunk_at) else k % 2
            return buffer, 1 + sum(chunk_buffer(j)[0] == buffer for j in range(k))

        ln0_g, ln0_b = m.sb("ln0_g", [P, D], F32), m.sb("ln0_b", [P, D], F32)
        ln1_g, ln1_b = m.sb("ln1_g", [P, D], F32), m.sb("ln1_b", [P, D], F32)
        cos, sin = m.sb("cos_sb", [P, TILES + 1, HALF], F32), m.sb("sin_sb", [P, TILES + 1, HALF], F32)
        decay = m.sb("decay_sb", [P, 2 * HEADS], F32)
        chunk_decay = m.sb("chunk_decay_sb", [P, 2], F32)
        causal = m.sb("causal_sb", [P, P], F32)
        band, band_prev = m.sb("band_sb", [P, GROUPS_P, P], F16), m.sb("band_prev_sb", [P, GROUPS_P, P], F16)
        ident = m.sb("ident_sb", [P, P], F32)
        meta_rows = m.sb("meta_rows_sb", [P, 1], F32)
        pool_w = m.sb("pool_w_sb", [P, GROUPS_P, P], F32)
        pool_b, pool_scale = m.sb("pool_b_sb", [P, GROUPS_P], F32), m.sb("pool_scale_sb", [P, GROUPS_P], F32)
        router_w = m.sb("router_w_sb", [P, KT, LOGITS], F32)
        router_b = m.sb("router_b_sb", [P, LOGITS], F32)
        x_in = m.sb("x_in", [P, 2, D], F32)
        h = m.sb("h", [P, 2, D], F32)
        h_t = [m.sb(f"h_t{q}", [P, D], dt) for q, dt in enumerate((BF16, F16))]
        mix_t = [m.sb(f"mix_t{q}", [P, D], dt) for q, dt in enumerate((BF16, F16))]
        rot_a, rot_b = m.sb("rot_a", [P, QK], F32), m.sb("rot_b", [P, QK], F32)
        qk = m.sb("qk", [P, QK], F32)
        v = m.sb("v", [P, RET], F32)
        u = [m.sb(f"u{q}", [P, 2, POOL], dt) for q, dt in enumerate((BF16, F16))]
        gate = m.sb("gate", [P, RET], F32)
        q_t = m.sb("q_t", [P, 2, 2, P], F32)
        k_t = m.sb("k_t", [P, 2, P], F32)
        scores = m.sb("scores", [P, HEADS, P], F32)
        state = m.sb("state", [P, 2, DV], F32)
        ret = m.sb("ret", [P, RET], F32)
        pooled_t = m.sb("pooled_t", [P, POOL], F32)
        pool_out = m.sb("pool_out", [P, POOL], F32)
        h1_t = m.sb("h1_t", [P, D], F32)
        stats = m.sb("stats", [P, 2, 2, 6], F32)
        moments = m.sb("moments", [P, 2, 2], F32)
        rstd = m.sb("rstd", [P, 2, 2], F32)
        g_stats = m.sb("g_stats", [P, HEADS, 6], F32)
        g_moments = m.sb("g_moments", [P, HEADS, 2], F32)
        g_rstd = m.sb("g_rstd", [P, 2, HEADS], F32)
        minus_half = m.sb("minus_half", [P, HEADS], F32)
        eps = m.sb("eps", [P, 3, HEADS], F32)

        bank = m.ps("bank", [P, 8, BANK], F32)
        QK_B, V_B, U_B, GATE_B, OUT_B, TR_B, TR2_B = 0, 1, 2, 3, 4, 6, 7

        weights_loaded = [m.sem(f"weights_loaded{s}") for s in range(len(chunk_at))]
        w_hi, w_lo = m.sem("w_hi"), m.sem("w_lo")
        params = m.sem("params")
        ready = m.sem("constants_ready")
        x_loaded = [m.sem(f"x_loaded{s}") for s in range(2)]
        stored = [m.sem(f"h1_stored{s}") for s in range(2)]
        names = ("stats0 rstd0 hdone htr hthi htlo qkdone vdone udone gatedone rotdone qkscaled vcopied u_hi u_lo "
                 "silu qktr qkt_copied bandmm band_copied scoremm masked poolmm pool_fin pool_hi pool_lo kvmm retmm "
                 "state_new gstats grstd ret_fin ret_tr ret_hi ret_lo outmm residual based stats1 rstd1 h1done h1hi h1lo h1tr "
                 "h1t_copied routermm logits_done").split()
        s = {n: m.sem(n) for n in names}
        dve_chain, pool_chain, passed = m.sem("dve_chain"), m.sem("pool_chain"), m.sem("passed")
        params0, params1 = m.sem("params0"), m.sem("params1")

        FIRST, LOOP_FROM, LOOP_TO = 0, 3, TILES - 2
        block = ctx.enter_context(nc.Block())

        @block.sync
        def _(sp):
            def param(dst, src, sem=params):
                sp.dma_start(dst, src).then_inc(sem, 16)

            def load_x(t, rows=None):
                if not (isinstance(t.i, int) and t.n < 1):
                    sp.wait_ge(s["hdone"], t.n)
                src = a["x"][bass.ds(t.n * P, P), :]
                sp.dma_start(x_in[:, t.slot, :], src).then_inc(x_loaded[t.slot], 16)

            w_in_v = a["w_in"].rearrange("(k p) n -> k p n", p=P)
            w_out_v = a["w_out"].rearrange("(k two p) n -> k p two n", p=P, two=2)

            def load_chunk(k):
                buffer, uses = chunk_buffer(k)
                if uses > 1:
                    sp.wait_ge(w_lo, 1 + max(j for j in range(k) if chunk_buffer(j)[0] == buffer))
                dst = chunk_at[buffer]
                if k < KT:
                    sp.dma_start(dst, w_in_v[k]).then_inc(weights_loaded[buffer], 16)
                else:
                    sp.dma_start(dst.rearrange("p (two n) -> p two n", two=2),
                                 w_out_v[k - KT]).then_inc(weights_loaded[buffer], 16)

            load_chunk(0)
            sp.wait_ge(ready, 1)
            sp.dma_start(x_in[P - N_META:P, 1, :], a["meta"]).then_inc(x_loaded[1], 16)
            param(ln0_g[:], a["ln0_g"].partition_broadcast(P), params0)
            param(ln0_b[:], a["ln0_b"].partition_broadcast(P), params0)
            param(ident[:], a["ident"], params0)
            param(meta_rows[:], a["meta_rows"], params0)
            load_chunk(1)
            load_x(Tile(0, 0))
            for k in range(2, KT):
                load_chunk(k)
            for dst, name in ((cos, "cos"), (sin, "sin"), (decay, "decay"), (chunk_decay, "chunk_decay")):
                param(dst[:], a[name], params1)
            for dst, name in ((causal, "causal"),
                              (band, "band"), (band_prev, "band_prev"), (pool_b, "pool_b"),
                              (pool_scale, "pool_scale")):
                param(dst[:], a[name])
            load_chunk(KT)
            load_chunk(KT + 1)
            param(pool_w[:], a["pool_w"].rearrange("g c d -> c g d"))
            param(ln1_g[:], a["ln1_g"].partition_broadcast(P))
            param(ln1_b[:], a["ln1_b"].partition_broadcast(P))
            param(router_w[:, :, 0:N_GROUPS], a["rg_w"].rearrange("(k p) n -> p k n", p=P))
            param(router_w[:, :, N_GROUPS:], a["re_w"].rearrange("(k p) n -> p k n", p=P))
            param(router_b[:, 0:N_GROUPS], a["rg_b"].partition_broadcast(P))
            param(router_b[:, N_GROUPS:], a["re_b"].partition_broadcast(P))
            load_x(Tile(0, 1))
            load_chunk(KT + 2)
            load_chunk(KT + 3)
            load_x(Tile(0, 2))

            def body(t):
                static = isinstance(t.i, int)
                if not static or t.n + 3 < TILES:
                    load_x(t + 3)
                if not static or t.n >= 1:
                    p = t - 1
                    rows = bass.ds(p.n * P, P)
                    sp.wait_ge(s["h1done"], p.n + 1)
                    sp.dma_start(keep["h1_dram"][rows, :], h1[:, p.slot, :]).then_inc(stored[p.slot], 16)
                    sp.wait_ge(s["h1hi"], p.n + 1)
                    sp.wait_ge(s["h1lo"], p.n + 1)
                    sp.dma_start(keep["parts_dram"][rows, :],
                                 stage[:, p.slot, D:2 * D].bitcast(BF16)).then_inc(stored[p.slot], 16)

            for t in range(0, 1):
                body(Tile(0, t))
            with sp.Fori(0, (TILES - 4) // 2) as i:
                body(Tile(i, 1))
                body(Tile(i, 2))
            for t in range(TILES - 3, TILES + 1):
                body(Tile(0, t))
            for slot in range(2):
                sp.wait_ge(stored[slot], TILES // 2 * 32)

        @block.gpsimd
        def _(pool):
            chain = Chain(pool, pool_chain)
            nc.gpsimd.memset(x_in[:, 1, :], 0.0).then_inc(ready, 1)
            nc.gpsimd.memset(q_t[:], 0.0).then_inc(ready, 1)
            nc.gpsimd.memset(state[:], 0.0).then_inc(ready, 1)
            nc.gpsimd.memset(minus_half[:], -0.5)
            nc.gpsimd.memset(eps[:, 0, :], LN_EPS)
            nc.gpsimd.memset(eps[:, 1, :], LN_EPS * W_SCALE ** 2)
            chain.link(nc.gpsimd.memset(eps[:, 2, :], GN_EPS))

            def inverse_root(out, tmp, var, eps_in, n):
                chain.link(nc.gpsimd.tensor_tensor(tmp, var, eps_in, ALU.add))
                return nc.gpsimd.tensor_tensor(out, tmp, minus_half[:, 0:n], ALU.pow)

            def ln_rstd(which, count):
                pool.wait_ge(s[f"stats{which}"], count)
                inverse_root(rstd[:, which, 0:1], rstd[:, which, 1:2], moments[:, which, 1:2],
                             eps[:, which, 0:1], 1).then_inc(s[f"rstd{which}"], 1)

            def scale_qk(t, count):
                pool.wait_ge(s["rotdone"], count)
                nc.gpsimd.tensor_tensor(qk[:].rearrange("p (h d) -> p h d", d=DK),
                                        rot_a[:].rearrange("p (h d) -> p h d", d=DK),
                                        decay[:].unsqueeze(2).to_broadcast([P, 2 * HEADS, DK]),
                                        ALU.mult).then_inc(s["qkscaled"], 1)

            def body(t):
                static = isinstance(t.i, int)
                if not static or t.n < TILES:
                    if not static or t.n >= 0:
                        scale_qk(t, t.n + 2)
                    if not static or t.n + 1 < TILES:
                        ln_rstd(0, t.n + 3)
                if not static or t.n >= 1:
                    p = t - 1
                    ln_rstd(1, p.n + 1)
                if not static or t.n < TILES:
                    pool.wait_ge(s["gstats"], t.n + 1)
                    inverse_root(g_rstd[:, 0, :], g_rstd[:, 1, :], g_moments[:, :, 1], eps[:, 2, :],
                                 HEADS).then_inc(s["grstd"], 1)
                if not static or t.n >= 1:
                    pool.wait_ge(s["h1done"], p.n + 1)
                    pool.wait_ge(s["h1hi"], p.n + 1)
                    nc.gpsimd.tensor_tensor(h1_parts[1][:, p.slot, :], h1[:, p.slot, :], h1_parts[0][:, p.slot, :],
                                            ALU.subtract).then_inc(s["h1lo"], 1)

            ln_rstd(0, 1)
            ln_rstd(0, 2)
            pool.wait_ge(params1, 16 * 4)
            scale_qk(Tile(0, -1), 1)
            for t in range(LOOP_FROM):
                body(Tile(0, t))
            base, STEPS = chain.steps, 3
            with pool.Fori(0, (LOOP_TO - LOOP_FROM + 1) // 2) as i:
                for k in range(2):
                    chain.base, chain.steps = base + i * (2 * STEPS) + STEPS * k, 0
                    body(Tile(i, LOOP_FROM + k))
                    assert chain.steps == STEPS
            chain.base, chain.steps = base + (LOOP_TO - LOOP_FROM + 1) * STEPS, 0
            for t in range(LOOP_TO + 1, TILES + 1):
                body(Tile(0, t))

        @block.scalar
        def _(act):
            def split_weights(ks):
                for k in ks:
                    buffer, uses = chunk_buffer(k)
                    act.wait_ge(weights_loaded[buffer], 16 * uses)
                    if k == KT:
                        act.wait_ge(w_lo, len(chunk_at))
                    if k < KT:
                        dst = w_in[0][:, k, :]
                    else:
                        dst = w_out[0][:, 2 * (k - KT):2 * (k - KT) + 2, :].rearrange("p two n -> p (two n)")
                    nc.scalar.activation(dst, chunk_at[buffer], ACT.Copy, scale=W_SCALE).then_inc(w_hi, 1)

            def copy_out(dst, src, wait, count, done, scale=1.0):
                act.wait_ge(s[wait], count)
                nc.scalar.activation(dst, src, ACT.Copy, scale=scale).then_inc(s[done], 1)

            def h_high(t):
                copy_out(h_t[0][:], bank[:, TR_B:TR_B + 2, :].rearrange("p b n -> p (b n)"), "htr", t.n + 2, "hthi")

            def body(t):
                static = isinstance(t.i, int)
                main = not static or t.n < TILES
                p, pp = t - 1, t - 2
                if main:
                    act.wait_ge(s["kvmm"], t.n + 1)
                    if not static or t.n > 0:
                        act.wait_ge(s["retmm"], t.n)
                    copy_out(v[:], bank[:, V_B, :], "vdone", t.n + 2, "vcopied", 1 / W_SCALE)
                if not static or 1 <= t.n <= TILES:
                    if not static or t.n > 1:
                        act.wait_ge(s["outmm"], p.n)
                    copy_out(mix_t[0][:, 0:RET], bank[:, TR_B, :], "ret_tr", p.n + 1, "ret_hi")
                if not static or t.n >= 2:
                    if not static or t.n > 2:
                        act.wait_ge(s["routermm"], pp.n)
                    copy_out(h1_t[:], bank[:, OUT_B:OUT_B + 2, :].rearrange("p b n -> p (b n)"), "h1tr", pp.n + 1,
                             "h1t_copied")
                if main:
                    if not static or t.n >= 2:
                        act.wait_ge(stored[t.slot], 32 * t.round)
                    act.wait_ge(s["hdone"], t.n + 2)
                    nc.scalar.activation(h1[:, t.slot, :], h[:, t.slot, :], ACT.Copy,
                                         scale=ALPHA * W_SCALE).then_inc(s["based"], 1)
                    if not static or t.n > 0:
                        act.wait_ge(s["bandmm"], t.n)
                    copy_out(u[0][:, t.slot, :], bank[:, U_B, :], "udone", t.n + 2, "u_hi", 1 / W_SCALE)
                    act.wait_ge(s["gatedone"], t.n + 1)
                    if not static or t.n > 0:
                        act.wait_ge(s["ret_fin"], t.n)
                    nc.scalar.activation(gate[:], bank[:, GATE_B, :], ACT.Silu, scale=1 / W_SCALE).then_inc(s["silu"], 1)
                    if not static or t.n + 1 < TILES:
                        h_high(t + 1)
                    act.wait_ge(s["qktr"], t.n + 1)
                    pairs = bank[:, TR_B, :].rearrange("p (j n) -> p j n", j=4)
                    nc.scalar.activation(k_t[:], pairs[:, 2:4, :], ACT.Copy).then_inc(s["qkt_copied"], 1)
                    nc.scalar.activation(q_t[0:DK, 0, :, :], pairs[0:DK, 0:2, :], ACT.Copy).then_inc(s["qkt_copied"], 1)
                    nc.scalar.activation(q_t[DK:P, 1, :, :], pairs[DK:P, 0:2, :], ACT.Copy).then_inc(s["qkt_copied"], 1)
                    copy_out(pooled_t[:], bank[:, TR2_B, :], "bandmm", t.n + 1, "band_copied")
                    copy_out(mix_t[0][:, RET:], pool_out[:], "pool_fin", t.n + 1, "pool_hi")
                if not static or 1 <= t.n <= TILES:
                    act.wait_ge(s["h1done"], p.n + 1)
                    nc.scalar.activation(h1_parts[0][:, p.slot, :], h1[:, p.slot, :], ACT.Copy).then_inc(s["h1hi"], 1)

            split_weights(range(2))
            h_high(Tile(0, -1))
            split_weights(range(2, KT))
            copy_out(v[:], bank[:, V_B, :], "vdone", 1, "vcopied", 1 / W_SCALE)
            copy_out(u[0][:, 1, :], bank[:, U_B, :], "udone", 1, "u_hi", 1 / W_SCALE)
            h_high(Tile(0, 0))
            split_weights(range(KT, CHUNKS))
            act.wait_ge(ready, 3)
            act.wait_ge(w_lo, CHUNKS)
            run_tiles(act, FIRST, TILES + 1, LOOP_FROM, LOOP_TO, body)

        @block.vector
        def _(dve):
            chain = Chain(dve, dve_chain)

            def low(dst, full, high, wait, count, done):
                dve.wait_ge(s[wait], count)
                nc.vector.tensor_tensor(dst, full, high, ALU.subtract).then_inc(s[done], 1)

            def split_weights(ks):
                for k in ks:
                    if k < KT:
                        hi, lo = (w_in[q][:, k, :] for q in range(2))
                    else:
                        j = 2 * (k - KT)
                        hi, lo = (w_out[q][:, j:j + 2, :].rearrange("p two n -> p (two n)") for q in range(2))
                    buffer, uses = chunk_buffer(k)
                    dve.wait_ge(weights_loaded[buffer], 16 * uses)
                    dve.wait_ge(w_hi, k + 1)
                    nc.vector.scalar_tensor_tensor(out=lo, in0=chunk_at[buffer], scalar=W_SCALE, in1=hi,
                                                   op0=ALU.mult, op1=ALU.subtract).then_inc(w_lo, 1)

            def ln_stats(which, src):
                nc.vector.bn_stats(stats[:, which, 0, :], src[:, 0:BANK])
                chain.link(nc.vector.bn_stats(stats[:, which, 1, :], src[:, BANK:D]), passed)
                return nc.vector.bn_aggr(moments[:, which, :], stats[:, which, :, :])

            def ln_apply(which, dst, src, g, b):
                chain.link(nc.vector.scalar_tensor_tensor(out=dst, in0=src, scalar=moments[:, which, 0:1], in1=g,
                                                          op0=ALU.subtract, op1=ALU.mult))
                return nc.vector.scalar_tensor_tensor(out=dst, in0=dst, scalar=rstd[:, which, 0:1], in1=b,
                                                      op0=ALU.mult, op1=ALU.add)

            def ln0_stats(t):
                dve.wait_ge(x_loaded[t.slot], 16 * ((t + 1).round + 1))
                ln_stats(0, x_in[:, t.slot, :]).then_inc(s["stats0"], 1)

            def ln0_apply(t):
                if not (isinstance(t.i, int) and t.n < 1):
                    dve.wait_ge(s["htr"], t.n)
                    if not (isinstance(t.i, int) and t.n < 2):
                        dve.wait_ge(s["based"], t.n - 1)
                dve.wait_ge(s["rstd0"], t.n + 2)
                ins = ln_apply(0, h[:, t.slot, :], x_in[:, t.slot, :], ln0_g[:], ln0_b[:])
                return ins

            def rotate(t):
                dve.wait_ge(s["qkdone"], t.n + 2)
                if not (isinstance(t.i, int) and t.n < 0):
                    dve.wait_ge(s["qkscaled"], t.n + 1)
                x = bank[:, QK_B, :].rearrange("p (h s f) -> p h s f", s=2, f=HALF)
                o = rot_a[:].rearrange("p (h s f) -> p h s f", s=2, f=HALF)
                o2 = rot_b[:].rearrange("p (h s f) -> p h s f", s=2, f=HALF)
                c = cos[:, bass.ds(t.n + 1, 1), :].to_broadcast([P, 2 * HEADS, HALF])
                sn = sin[:, bass.ds(t.n + 1, 1), :].to_broadcast([P, 2 * HEADS, HALF])
                nc.vector.tensor_tensor(o[:, :, 0, :], x[:, :, 0, :], c, ALU.mult)
                nc.vector.tensor_tensor(o[:, :, 1, :], x[:, :, 1, :], c, ALU.mult)
                nc.vector.tensor_tensor(o2[:, :, 0, :], x[:, :, 1, :], sn, ALU.mult)
                chain.link(nc.vector.tensor_tensor(o2[:, :, 1, :], x[:, :, 0, :], sn, ALU.mult))
                nc.vector.tensor_tensor(o[:, :, 0, :], o[:, :, 0, :], o2[:, :, 0, :], ALU.subtract)
                nc.vector.tensor_tensor(o[:, :, 1, :], o[:, :, 1, :], o2[:, :, 1, :], ALU.add).then_inc(s["rotdone"], 1)

            def h_low(t):
                low(h_t[1][:], bank[:, TR_B:TR_B + 2, :].rearrange("p b n -> p (b n)"), h_t[0][:], "hthi",
                    t.n + 2, "htlo")

            def u_low(t):
                dve.wait_ge(s["u_hi"], t.n + 2)
                nc.vector.scalar_tensor_tensor(out=u[1][:, t.slot, :], in0=bank[:, U_B, :], scalar=1 / W_SCALE,
                                               in1=u[0][:, t.slot, :], op0=ALU.mult,
                                               op1=ALU.subtract).then_inc(s["u_lo"], 1)

            def new_state(t):
                dve.wait_ge(s["kvmm"], t.n + 2)
                if not (isinstance(t.i, int) and t.n < 0):
                    dve.wait_ge(s["retmm"], t.n + 1)
                chain.link(nc.vector.tensor_tensor(state[:], state[:],
                                                   bank[:, GATE_B, 0:2 * DV].rearrange("p (j n) -> p j n", j=2), ALU.add))
                nc.vector.tensor_tensor(state[:], state[:], chunk_decay[:].unsqueeze(2).to_broadcast([P, 2, DV]),
                                        ALU.mult).then_inc(s["state_new"], 1)

            def body(t):
                static = isinstance(t.i, int)
                main = not static or t.n < TILES
                p, pp = t - 1, t - 2
                if main:
                    rotate(t)
                if not static or 1 <= t.n <= TILES:
                    low(mix_t[1][:, 0:RET], bank[:, TR_B, :], mix_t[0][:, 0:RET], "ret_hi", p.n + 1, "ret_lo")
                if not static or t.n + 1 < TILES:
                    ln0_stats(t + 1)
                    ln0_apply(t + 1).then_inc(s["hdone"], 1)
                if not static or t.n >= 2:
                    dve.wait_ge(s["routermm"], pp.n + 1)
                    nc.vector.tensor_tensor(keep["logits"][:, bass.ds(pp.n, 1), :], bank[:, TR2_B, 0:LOGITS].unsqueeze(1),
                                            router_b[:].unsqueeze(1), ALU.add).then_inc(s["logits_done"], 1)
                if main:
                    u_low(t)
                if not static or t.n + 1 < TILES:
                    h_low(t + 1)
                if not static or 1 <= t.n <= TILES:
                    dve.wait_ge(s["outmm"], p.n + 1)
                    dve.wait_ge(s["based"], p.n + 1)
                    chain.link(nc.vector.tensor_tensor(
                        h1[:, p.slot, :], h1[:, p.slot, :],
                        bank[:, OUT_B:OUT_B + 2, :].rearrange("p b n -> p (b n)"), ALU.add))
                if main:
                    dve.wait_ge(s["scoremm"], t.n + 1)
                    nc.vector.tensor_tensor(scores[:], bank[:, QK_B, :].rearrange("p (h n) -> p h n", h=HEADS),
                                            causal[:].unsqueeze(1).to_broadcast([P, HEADS, P]),
                                            ALU.mult).then_inc(s["masked"], 1)
                    dve.wait_ge(s["poolmm"], t.n + 1)
                    if not static or t.n > 0:
                        dve.wait_ge(s["pool_lo"], t.n)
                    for g in range(GROUPS_P):
                        cols = slice(g * P, (g + 1) * P)
                        ins = nc.vector.tensor_scalar(pool_out[:, cols], bank[:, V_B, cols], pool_b[:, g:g + 1],
                                                      pool_scale[:, g:g + 1], ALU.add, ALU.mult)
                    ins.then_inc(s["pool_fin"], 1)
                if not static or 1 <= t.n <= TILES:
                    ln_stats(1, h1[:, p.slot, :]).then_inc(s["stats1"], 1)
                if main:
                    dve.wait_ge(s["retmm"], t.n + 1)
                    for hd in range(HEADS):
                        ins = nc.vector.bn_stats(g_stats[:, hd, :], bank[:, U_B, hd * DV:(hd + 1) * DV])
                    chain.link(ins, passed)
                    for hd in range(HEADS):
                        ins = nc.vector.bn_aggr(g_moments[:, hd, :], g_stats[:, hd, :])
                    ins.then_inc(s["gstats"], 1)
                    new_state(t)
                if not static or 1 <= t.n <= TILES:
                    dve.wait_ge(s["rstd1"], p.n + 1)
                    ln_apply(1, h1[:, p.slot, :], h1[:, p.slot, :], ln1_g[:], ln1_b[:]).then_inc(s["h1done"], 1)
                if main:
                    low(mix_t[1][:, RET:], pool_out[:], mix_t[0][:, RET:], "pool_hi", t.n + 1, "pool_lo")
                    dve.wait_ge(s["grstd"], t.n + 1)
                    if not static or t.n > 0:
                        dve.wait_ge(s["ret_tr"], t.n)
                    for hd in range(HEADS):
                        cols = slice(hd * DV, (hd + 1) * DV)
                        ins = nc.vector.tensor_scalar(ret[:, cols], bank[:, U_B, cols], g_moments[:, hd, 0:1],
                                                      g_rstd[:, 0, hd:hd + 1], ALU.subtract, ALU.mult)
                    chain.link(ins)
                    dve.wait_ge(s["silu"], t.n + 1)
                    nc.vector.tensor_tensor(ret[:], ret[:], gate[:], ALU.mult).then_inc(s["ret_fin"], 1)

            dve.wait_ge(ready, 3)
            dve.wait_ge(params0, 16 * 4)
            ln0_stats(Tile(0, -1))
            chain.link(ln0_apply(Tile(0, -1)))
            nc.vector.tensor_scalar(h[:, 1, :], h[:, 1, :], meta_rows[:, 0:1], None, ALU.mult).then_inc(s["hdone"], 1)
            split_weights(range(2))
            h_low(Tile(0, -1))
            split_weights(range(2, 4))
            ln0_stats(Tile(0, 0))
            ln0_apply(Tile(0, 0)).then_inc(s["hdone"], 1)
            split_weights(range(4, KT))
            dve.wait_ge(params1, 16 * 4)
            rotate(Tile(0, -1))
            u_low(Tile(0, -1))
            new_state(Tile(0, -1))
            h_low(Tile(0, 0))
            split_weights(range(KT, CHUNKS))
            dve.wait_ge(params, 16 * 12)
            for t in range(LOOP_FROM):
                body(Tile(0, t))
            base, STEPS = chain.steps, 9
            with dve.Fori(0, (LOOP_TO - LOOP_FROM + 1) // 2) as i:
                for k in range(2):
                    chain.base, chain.steps = base + i * (2 * STEPS) + STEPS * k, 0
                    body(Tile(i, LOOP_FROM + k))
                    assert chain.steps == STEPS, chain.steps
            chain.base, chain.steps = base + (LOOP_TO - LOOP_FROM + 1) * STEPS, 0
            for t in range(LOOP_TO + 1, TILES + 2):
                body(Tile(0, t))

        @block.tensor
        def _(pe):
            def three_passes(dst, lhs, rhs, kts, done):
                last = kts - 1
                for k in range(kts):
                    nc.tensor.matmul(dst, lhs(0, k), rhs(0, k), start=k == 0, stop=False)
                    nc.tensor.matmul(dst, lhs(0, k), rhs(1, k), start=False, stop=False)
                for k in range(kts):
                    ins = nc.tensor.matmul(dst, lhs(1, k), rhs(0, k), start=False, stop=k == last)
                if done is not None:
                    ins.then_inc(s[done], 1)

            def transpose_h(t):
                pe.wait_ge(s["hdone"], t.n + 2)
                if not (isinstance(t.i, int) and t.n < 0):
                    pe.wait_ge(s["htlo"], t.n + 1)
                if not (isinstance(t.i, int) and t.n < 2):
                    pe.wait_ge(s["ret_lo"], t.n - 1)
                    if not (isinstance(t.i, int) and t.n < 3):
                        pe.wait_ge(s["logits_done"], t.n - 2)
                for k in range(KT):
                    ins = nc.tensor.transpose(bank[:, TR_B + k // 4, (k % 4) * P:(k % 4 + 1) * P],
                                              h[:, t.slot, k * P:(k + 1) * P], ident[:])
                ins.then_inc(s["htr"], 1)

            def project(b, col, done):
                three_passes(bank[:, b, :], lambda q, k: h_t[q][:, k * P:(k + 1) * P],
                             lambda q, k: w_in[q][:, k, col:col + BANK], KT, done)

            def kv_products(t):
                pe.wait_ge(s["qkscaled"], t.n + 2)
                pe.wait_ge(s["vcopied"], t.n + 2)
                for hd in range(HEADS):
                    r, j = hd % 2, hd // 2
                    ins = nc.tensor.matmul(bank[r * DK:(r + 1) * DK, GATE_B, j * DV:(j + 1) * DV],
                                           qk[:, (HEADS + hd) * DK:(HEADS + hd + 1) * DK],
                                           v[:, hd * DV:(hd + 1) * DV], start=True, stop=True)
                ins.then_inc(s["kvmm"], 1)

            def body(t):
                static = isinstance(t.i, int)
                main = not static or t.n < TILES
                p, pp = t - 1, t - 2
                if main:
                    pe.wait_ge(s["htlo"], t.n + 2)
                    if not static or t.n > 0:
                        pe.wait_ge(s["masked"], t.n)
                    project(QK_B, 0, "qkdone")
                    if not static or t.n > 0:
                        pe.wait_ge(s["pool_fin"], t.n)
                    project(V_B, QK, "vdone")
                if not static or 1 <= t.n <= TILES:
                    pe.wait_ge(s["ret_fin"], p.n + 1)
                    for k in range(HEADS):
                        ins = nc.tensor.transpose(bank[:, TR_B, k * P:(k + 1) * P], ret[:, k * P:(k + 1) * P], ident[:])
                    ins.then_inc(s["ret_tr"], 1)
                if not static or t.n >= 2:
                    pe.wait_ge(s["h1done"], pp.n + 1)
                    for k in range(KT):
                        ins = nc.tensor.transpose(bank[:, OUT_B + k // 4, (k % 4) * P:(k % 4 + 1) * P],
                                                  h1[:, pp.slot, k * P:(k + 1) * P], ident[:])
                    ins.then_inc(s["h1tr"], 1)
                if main:
                    if static and t.n == 0:
                        pe.wait_ge(s["u_lo"], 1)
                    project(U_B, QK + 2 * RET, "udone")
                if not static or t.n >= 2:
                    pe.wait_ge(s["h1t_copied"], pp.n + 1)
                    for k in range(KT):
                        ins = nc.tensor.matmul(bank[:, TR2_B, 0:LOGITS], h1_t[:, k * P:(k + 1) * P], router_w[:, k, :],
                                               start=k == 0, stop=k == KT - 1)
                    ins.then_inc(s["routermm"], 1)
                if main:
                    pe.wait_ge(s["state_new"], t.n + 1)
                    project(GATE_B, QK + RET, "gatedone")
                    if not static or t.n + 1 < TILES:
                        transpose_h(t + 1)
                if not static or 1 <= t.n <= TILES:
                    pe.wait_ge(s["ret_lo"], p.n + 1)
                    pe.wait_ge(s["pool_lo"], p.n + 1)
                    if static and t.n == 1:
                        pe.wait_ge(w_lo, CHUNKS)
                    for half in range(2):
                        three_passes(bank[:, OUT_B + half, :], lambda q, k: mix_t[q][:, k * P:(k + 1) * P],
                                     lambda q, k: w_out[q][:, k, half * BANK:(half + 1) * BANK], KT,
                                     "outmm" if half else None)
                if main:
                    pe.wait_ge(s["qkscaled"], t.n + 2)
                    if not static or t.n + 1 < TILES:
                        pe.wait_ge(s["htlo"], t.n + 3)
                    else:
                        pe.wait_ge(s["logits_done"], pp.n + 1)
                    for j in range(4):
                        ins = nc.tensor.transpose(bank[:, TR_B, j * P:(j + 1) * P], qk[:, j * P:(j + 1) * P], ident[:])
                    ins.then_inc(s["qktr"], 1)
                    pe.wait_ge(s["u_lo"], t.n + 2)
                    for g in range(GROUPS_P):
                        cols = slice(g * P, (g + 1) * P)
                        for q in range(2):
                            nc.tensor.matmul(bank[:, TR2_B, cols], u[q][:, t.slot, cols], band[:, g, :],
                                             start=q == 0, stop=False)
                            ins = nc.tensor.matmul(bank[:, TR2_B, cols], u[q][:, p.slot, cols], band_prev[:, g, :],
                                                   start=False, stop=q == 1)
                    ins.then_inc(s["bandmm"], 1)
                    pe.wait_ge(s["qkt_copied"], 3 * t.n + 3)
                    pe.wait_ge(s["rotdone"], t.n + 2)
                    for hd in range(HEADS):
                        ins = nc.tensor.matmul(bank[:, QK_B, hd * P:(hd + 1) * P], k_t[:, hd // 2, :],
                                               q_t[:, hd % 2, hd // 2, :], start=True, stop=True)
                    ins.then_inc(s["scoremm"], 1)
                    pe.wait_ge(s["silu"], t.n + 1)
                    kv_products(t)
                    pe.wait_ge(s["band_copied"], t.n + 1)
                    for g in range(GROUPS_P):
                        cols = slice(g * P, (g + 1) * P)
                        ins = nc.tensor.matmul(bank[:, V_B, cols], pool_w[:, g, :], pooled_t[:, cols],
                                               start=True, stop=True)
                    ins.then_inc(s["poolmm"], 1)
                    pe.wait_ge(s["masked"], t.n + 1)
                    for hd in range(HEADS):
                        cols = slice(hd * DV, (hd + 1) * DV)
                        nc.tensor.matmul(bank[:, U_B, cols], scores[:, hd, :], v[:, cols], start=True, stop=False)
                        ins = nc.tensor.matmul(bank[:, U_B, cols], q_t[:, hd % 2, hd // 2, :],
                                               state[:, hd // 2, :], start=False, stop=True)
                    ins.then_inc(s["retmm"], 1)

            pe.wait_ge(params0, 16 * 4)
            transpose_h(Tile(0, -1))
            pe.wait_ge(s["htlo"], 1)
            for k in range(KT):
                pe.wait_ge(w_lo, k + 1)
                for b, col, done in ((QK_B, 0, "qkdone"), (V_B, QK, "vdone"), (U_B, QK + 2 * RET, "udone")):
                    for q_h, q_w in ((0, 0), (0, 1), (1, 0)):
                        ins = nc.tensor.matmul(bank[:, b, :], h_t[q_h][:, k * P:(k + 1) * P],
                                               w_in[q_w][:, k, col:col + BANK], start=k == 0 and q_h + q_w == 0,
                                               stop=k == KT - 1 and q_h == 1)
                    if k == KT - 1:
                        ins.then_inc(s[done], 1)
            transpose_h(Tile(0, 0))
            kv_products(Tile(0, -1))
            pe.wait_ge(params, 16 * 12)
            run_tiles(pe, FIRST, TILES + 1, LOOP_FROM, LOOP_TO, body)


def weight_slots(nc, ctx):
    m = Memory(nc, ctx)
    raw = m.sb("raw", [P, 2 * SLOT], F32)
    return {
        "raw": raw, "hi": raw[:].bitcast(BF16),
        "lo": m.sb("w_low", [P, 2 * SLOT], BF16),
        "ident": [m.sb(f"ident_{q}", [P, P], dt) for q, dt in enumerate((BF16, F16))],
        "loaded": [[m.sem(f"w_loaded{i}{j}") for j in range(3)] for i in range(2)],
        "low": m.sem("w_low_made"),
    }


def load_expert(eng, a, w, e, free=None):
    sources = (("w_gate", D_E), ("w_up", D_E), ("w_down", D))
    for part, (name, width) in enumerate(sources):
        at = e.slot * SLOT + part * PART
        if free is not None:
            eng.wait_ge(free[0][part], free[1])
        src = a[name].rearrange("e (k p) n -> e p k n", p=P)[bass.ds(e.n, 1), :, :, :].squeeze(0)
        eng.dma_start(w["raw"][:, at:at + PART].rearrange("p (k n) -> p k n", n=width),
                      src).then_inc(w["loaded"][e.slot][part], 16)


def low_parts(eng, engine, w, slot, count):
    for part in range(3):
        at = slot * SLOT + part * PART
        eng.wait_ge(w["loaded"][slot][part], 16 * count)
        engine.tensor_tensor(w["lo"][:, at:at + PART], w["raw"][:, at:at + PART],
                             w["hi"][:, 2 * at + 1:2 * (at + PART):2], ALU.subtract).then_inc(w["low"], 1)


def router(nc, a, keep, w):
    ctx = ExitStack()
    with ctx:
        m = Memory(nc, ctx)
        T, G, J, E = TILES, N_GROUPS, PER_GROUP, EXPERTS
        logits = keep["logits"]
        iota = m.sb("iota", [P, P], F32)
        top = m.sb("top", [P, T], F32)
        g_first = m.sb("g_first", [P, T], F32)
        g_exp = m.sb("g_exp", [P, T, G], F32)
        g_cand = m.sb("g_cand", [P, T, G], F32)
        g_prob = m.sb("g_prob", [P, T], F32)
        sel = m.sb("sel", [P, T, J], F32)
        prod = m.sb("prod", [P, T, J], F32)
        cand = m.sb("cand", [P, T, J], F32)
        one_hot = m.sb("one_hot8", [P, T, J], F32)
        best = m.sb("best", [P, 2, T], F32)
        place = m.sb("place", [P, 2, T], F32)
        ratio = m.sb("ratio", [P, T], F32)
        share = m.sb("share", [P, T], F32)
        expert = m.sb("expert", [P, 2, T], F32)
        member = m.sb("member", [P, 2, T, E], F32)
        both = m.sb("both", [P, T, E], F32)
        before = m.sb("before_sb", [P, P], F32)
        ones = m.sb("ones", [P, P], F32)
        count_et = m.sb("count_et", [P, E, T], F32)
        incl_et = m.sb("incl_et", [P, E, T], F32)
        keep_going = m.sb("keep_going", [P, E, T], F32)
        padded = m.sb("padded", [P, E], F32)
        padded_i = m.sb("padded_i", [P, E], I32)
        ends = m.sb("ends", [P, E], F32)
        starts = m.sb("starts", [P, E], F32)
        rank = m.sb("rank", [P, T, E], F32)
        dest = m.sb("dest", [P, 2, T], F32)
        dest_i = m.sb("dest_i", [P, 2, T], I32)
        lane = m.sb("lane", [P, 2, T], F32)
        lane_i = m.sb("lane_i", [P, 2, T], I32)
        dblock = m.sb("dblock", [P, 2, T], F32)
        token_no = m.sb("token_no", [P, T], F32)
        HOT = 6
        lane_hot = m.sb("lane_hot", [P, HOT, P], F32)
        block_hot = m.sb("block_hot", [P, HOT, TABLE], F32)
        ident_f = m.sb("ident_f", [P, P], F32)
        full = m.sb("full", [1, RUN_BLOCKS, E], BF16)
        of_block = m.sb("of_block", [1, RUN_BLOCKS], F32)
        slot_i = m.sb("slot_i", [1, RUN_BLOCKS], I32)
        blocks_i = m.sb("blocks_i", [1, 1], U32)
        bank = m.ps("rbank", [P, 8, BANK], F32)
        step, act_step, pe_step, made, loaded = (m.sem(n) for n in ("r_dve", "r_act", "r_pe", "r_made", "r_loaded"))
        id_loaded, places = m.sem("r_id_loaded"), m.sem("places_known")
        lane_made, hot_used = m.sem("lane_made"), m.sem("hot_used")
        block_made = [m.sem(f"block_made{i}") for i in range(2)]
        block = ctx.enter_context(nc.Block())
        BIG = 1e9

        @block.sync
        def _(sp):
            sp.dma_start(before[:], a["before"]).then_inc(loaded, 16)
            sp.dma_start(ident_f[:], a["ident"]).then_inc(id_loaded, 16)
            load_expert(sp, a, w, Tile(0, 0))
            load_expert(sp, a, w, Tile(0, 1))

        @block.gpsimd
        def _(pool):
            nc.gpsimd.iota(iota[:], pattern=[[1, P]], base=0, channel_multiplier=0,
                           allow_small_or_imprecise_dtypes=True).then_inc(made, 1)
            nc.gpsimd.iota(token_no[:], pattern=[[P, T]], base=0, channel_multiplier=1,
                           allow_small_or_imprecise_dtypes=True).then_inc(made, 1)
            nc.gpsimd.memset(ones[:], 1.0).then_inc(made, 1)
            nc.gpsimd.memset(keep_going[:], 1.0).then_inc(made, 1)
            low_parts(pool, nc.gpsimd, w, 0, 1)
            pool.wait_ge(made, 4)
            pool.wait_ge(places, 1)
            for n in range(0, 2 * T, 2):
                k, t = n // T, n % T
                wait_past(pool, hot_used, n - HOT + 1)
                nc.gpsimd.tensor_scalar(block_hot[:, n % HOT, :], iota[:, 0:TABLE], dblock[:, k, t:t + 1],
                                        token_no[:, t:t + 1], ALU.is_equal, ALU.mult).then_inc(block_made[0], 1)

        mark = {}

        @block.vector
        def _(dve):
            chain = Chain(dve, step)
            L = chain.link
            wide = lambda x, n: x.unsqueeze(2).to_broadcast([P, T, n])
            along = lambda n: iota[:, 0:n].unsqueeze(1).to_broadcast([P, T, n])
            dve.wait_ge(made, 4)

            def first_max(values, n, top_out, first_out, cand_t):
                L(nc.vector.tensor_reduce(top_out, values, AX.X, ALU.max))
                L(nc.vector.tensor_tensor(cand_t, values, wide(top_out, n), ALU.is_lt))
                L(nc.vector.scalar_tensor_tensor(out=cand_t, in0=cand_t, scalar=BIG, in1=along(n), op0=ALU.mult,
                                                 op1=ALU.add))
                L(nc.vector.tensor_reduce(first_out, cand_t, AX.X, ALU.min))

            g_logits = logits[:, :, 0:G]
            first_max(g_logits, G, top[:], g_first[:], g_cand[:])
            L(nc.vector.tensor_tensor(g_exp[:], g_logits, wide(top[:], G), ALU.subtract))
            mark["g_shifted"] = chain.steps
            for g in range(G):
                L(nc.vector.tensor_scalar(share[:], g_first[:], float(g), None, ALU.is_equal))
                dst = sel if g == 0 else prod
                L(nc.vector.tensor_tensor(dst[:], logits[:, :, G + g * J:G + (g + 1) * J], wide(share[:], J), ALU.mult))
                if g:
                    L(nc.vector.tensor_tensor(sel[:], sel[:], prod[:], ALU.add))
            first_max(sel[:], J, best[:, 0, :], place[:, 0, :], cand[:])
            L(nc.vector.tensor_tensor(one_hot[:], along(J), wide(place[:, 0, :], J), ALU.is_equal))
            L(nc.vector.scalar_tensor_tensor(out=prod[:], in0=one_hot[:], scalar=-3e38, in1=sel[:], op0=ALU.mult,
                                             op1=ALU.add))
            first_max(prod[:], J, best[:, 1, :], place[:, 1, :], cand[:])
            L(nc.vector.tensor_tensor(ratio[:], best[:, 1, :], best[:, 0, :], ALU.subtract))
            mark["ratio"] = chain.steps
            for k in range(2):
                L(nc.vector.scalar_tensor_tensor(out=expert[:, k, :], in0=g_first[:], scalar=float(J),
                                                 in1=place[:, k, :], op0=ALU.mult, op1=ALU.add))
                L(nc.vector.tensor_tensor(member[:, k, :, :], along(E), wide(expert[:, k, :], E), ALU.is_equal))
            L(nc.vector.tensor_tensor(both[:], member[:, 0, :, :], member[:, 1, :, :], ALU.add))
            mark["both"] = chain.steps
            dve.wait_ge(act_step, 1)
            L(nc.vector.tensor_reduce(g_prob[:], g_exp[:], AX.X, ALU.add))
            L(nc.vector.reciprocal(g_prob[:], g_prob[:]))
            dve.wait_ge(act_step, 2)
            L(nc.vector.tensor_scalar(share[:], ratio[:], 1.0, None, ALU.add))
            L(nc.vector.reciprocal(share[:], share[:]))
            L(nc.vector.tensor_tensor(keep["pair_w"][:, 0, :], g_prob[:], share[:], ALU.mult))
            L(nc.vector.tensor_tensor(keep["pair_w"][:, 1, :], keep["pair_w"][:, 0, :], ratio[:], ALU.mult))
            dve.wait_ge(pe_step, 1)
            for b in range(2):
                tt = slice(b * T // 2, (b + 1) * T // 2)
                L(nc.vector.tensor_copy(count_et[:, :, tt].rearrange("p e t -> p t e"),
                                        bank[:, b, :].rearrange("p (t e) -> p t e", e=E)))
            L(nc.vector.tensor_scalar(keep_going[:, :, 0:1], keep_going[:, :, 0:1], 0.0, None, ALU.mult))
            flat = lambda x: x[:].rearrange("p e t -> p (e t)")
            L(nc.vector.tensor_tensor_scan(flat(incl_et), flat(keep_going), flat(count_et), 0.0, ALU.mult, ALU.add))
            L(nc.vector.tensor_scalar(padded_i[:], incl_et[:, :, T - 1], float(P - 1), None, ALU.add))
            L(nc.vector.tensor_scalar(padded_i[:], padded_i[:], 7, None, ALU.logical_shift_right))
            L(nc.vector.tensor_scalar(padded[:], padded_i[:], 1.0, None, ALU.max))
            L(nc.vector.tensor_tensor_scan(ends[:], ones[:, 0:E], padded[:], 0.0, ALU.mult, ALU.add))
            L(nc.vector.tensor_copy(keep["ends"][:], ends[0:1, :]))
            L(nc.vector.tensor_copy(blocks_i[:], ends[0:1, E - 1:E]))
            L(nc.vector.tensor_scalar(keep["pairs"][:], blocks_i[:], 1, None, ALU.logical_shift_right))
            L(nc.vector.tensor_scalar(keep["unused"][:], keep["pairs"][:], -1.0, float(BLOCKS // 2), ALU.mult, ALU.add))
            L(nc.vector.tensor_tensor(starts[:], ends[:], padded[:], ALU.subtract))
            L(nc.vector.tensor_tensor(count_et[:], incl_et[:], count_et[:], ALU.subtract))
            L(nc.vector.scalar_tensor_tensor(out=count_et[:], in0=starts[:].unsqueeze(2).to_broadcast([P, E, T]),
                                             scalar=float(P), in1=count_et[:], op0=ALU.mult, op1=ALU.add))
            dve.wait_ge(pe_step, 2)
            for b in range(2):
                tt = slice(b * T // 2, (b + 1) * T // 2)
                L(nc.vector.tensor_tensor(rank[:, tt, :], bank[:, 2 + b, :].rearrange("p (t e) -> p t e", e=E),
                                          count_et[:, :, tt].rearrange("p e t -> p t e"), ALU.add))
            for k in range(2):
                hit = keep_going[:].rearrange("p e t -> p (e t)").rearrange("p (t e) -> p t e", e=E)
                L(nc.vector.tensor_tensor(hit, rank[:], member[:, k, :, :], ALU.mult))
                L(nc.vector.tensor_reduce(dest[:, k, :], hit, AX.X, ALU.add))
            L(nc.vector.tensor_copy(dest_i[:], dest[:]))
            L(nc.vector.tensor_scalar(lane_i[:], dest_i[:], P - 1, None, ALU.bitwise_and))
            L(nc.vector.tensor_copy(lane[:], lane_i[:]))
            L(nc.vector.tensor_tensor(dblock[:], dest[:], lane[:], ALU.subtract))
            L(nc.vector.tensor_scalar(dblock[:], dblock[:], 1.0 / P, None, ALU.mult))
            dve.sem_inc(places, 1)
            for n in range(2 * T):
                k, t = n // T, n % T
                wait_past(dve, hot_used, n - HOT + 1)
                nc.vector.tensor_scalar(lane_hot[:, n % HOT, :], iota[:], lane[:, k, t:t + 1], None,
                                        ALU.is_equal).then_inc(lane_made, 1)
                if n % 2:
                    nc.vector.tensor_scalar(block_hot[:, n % HOT, :], iota[:, 0:TABLE], dblock[:, k, t:t + 1],
                                            token_no[:, t:t + 1], ALU.is_equal, ALU.mult).then_inc(block_made[1], 1)
            L(nc.vector.tensor_copy(keep["dest"][:], dest[:]))
            L(nc.vector.tensor_tensor(full[:], iota[0:1, 0:RUN_BLOCKS].unsqueeze(2).to_broadcast([1, RUN_BLOCKS, E]),
                                      ends[0:1, :].unsqueeze(1).to_broadcast([1, RUN_BLOCKS, E]), ALU.is_ge))
            L(nc.vector.tensor_reduce(of_block[:], full[:], AX.X, ALU.add))
            L(nc.vector.tensor_scalar(of_block[:], of_block[:], float(E - 1), None, ALU.min))
            L(nc.vector.tensor_copy(slot_i[:], of_block[:]))
            L(nc.vector.tensor_scalar(slot_i[:], slot_i[:], 1, None, ALU.bitwise_and))
            L(nc.vector.tensor_scalar(keep["block_part"][:], of_block[:], 3.0, None, ALU.mult))
            L(nc.vector.tensor_scalar(keep["block_slot"][:], slot_i[:], float(SLOT), None, ALU.mult))
            dve.wait_ge(pe_step, 3)
            nc.vector.tensor_copy(keep["tokens"][:], bank[:, 4, 0:TABLE])

        @block.scalar
        def _(act):
            act.wait_ge(step, mark["g_shifted"])
            nc.scalar.activation(g_exp[:], g_exp[:], ACT.Exp).then_inc(act_step, 1)
            act.wait_ge(step, mark["ratio"])
            nc.scalar.activation(ratio[:], ratio[:], ACT.Exp).then_inc(act_step, 1)
            act.wait_ge(id_loaded, 16)
            for q in range(2):
                nc.scalar.activation(w["ident"][q][:], ident_f[:], ACT.Copy)

        @block.tensor
        def _(pe):
            pe.wait_ge(loaded, 16)
            pe.wait_ge(step, mark["both"])
            flat = both[:].rearrange("p t e -> p (t e)")
            for b in range(2):
                ins = nc.tensor.matmul(bank[:, b, :], ones[:], flat[:, b * BANK:(b + 1) * BANK], start=True, stop=True)
            ins.then_inc(pe_step, 1)
            for b in range(2):
                ins = nc.tensor.matmul(bank[:, 2 + b, :], before[:], flat[:, b * BANK:(b + 1) * BANK], start=True, stop=True)
            ins.then_inc(pe_step, 1)
            for n in range(2 * T):
                pe.wait_ge(lane_made, n + 1)
                pe.wait_ge(block_made[n % 2], n // 2 + 1)
                nc.tensor.matmul(bank[:, 4, 0:TABLE], lane_hot[:, n % HOT, :], block_hot[:, n % HOT, :],
                                 start=n == 0, stop=n == 2 * T - 1).then_inc(hot_used, 1)
            pe.wait_ge(hot_used, 2 * T)
            pe.sem_inc(pe_step, 1)


def experts(nc, a, keep, w):
    ctx = ExitStack()
    with ctx:
        m = Memory(nc, ctx)
        w_lo, w_hi, ident = w["lo"], w["hi"], w["ident"]
        xg = m.sb("xg", [P, 2, 2 * D], BF16)
        x_t = [m.sb(f"x_t{q}", [P, 2, D], dt) for q, dt in enumerate((BF16, F16))]
        silu_g = m.sb("silu_g", [P, D_E], F32)
        up = m.sb("up", [P, D_E], F32)
        hid = m.sb("hid", [P, D_E], F32)
        hid_parts = [m.sb(f"hid_parts{q}", [P, D_E], dt) for q, dt in enumerate((BF16, F16))]
        hid_t = [m.sb(f"hid_t{q}", [P, D_E], dt) for q, dt in enumerate((BF16, F16))]
        y = m.sb("y", [P, 2, D], F32)
        index = m.sb("index", [P, 2], U32)
        zeros = m.sb("zeros", [P, D], F32)
        GATE_B, UP_B, Y_B = 0, 1, 2
        bank = m.ps("ebank", [P, 4, BANK], F32)
        xtr = [m.ps(f"xtr{q}", [P, D], dt) for q, dt in enumerate((BF16, F16))]
        htr = [m.ps(f"htr{q}", [P, D_E], dt) for q, dt in enumerate((BF16, F16))]
        xg_parts = [xg[:, :, 0:D], xg[:, :, D:2 * D].bitcast(F16)]
        s = {n: m.sem("e_" + n) for n in ("xtr xt_copied gate up silu upcopied hid hidhi hidlo htr ht_copied "
                                          "down ycopied indexed gone ended").split()}
        gathered = [m.sem(f"gathered{i}") for i in range(2)]
        stored = [m.sem(f"y_stored{i}") for i in range(2)]
        rest_stored = m.sem("rest_stored")
        ready = m.sem("e_ready")
        block = ctx.enter_context(nc.Block())

        def pairs_of(eng):
            return eng.value_load(keep["pairs"][:], min_val=EXPERTS // 2, max_val=BLOCKS // 2)

        @block.sync
        def _(sp):
            pairs = pairs_of(sp)
            sp.wait_ge(ready, 1)
            sp.sem_inc(rest_stored, 1)
            with sp.Fori(pairs, BLOCKS // 2) as i:
                for k in range(1, 3):
                    sp.dma_start(keep["y_dram"][bass.ds((2 * i + k) * P, P), :], zeros[:]).then_inc(rest_stored, 16)
            with sp.Fori(0, EXPERTS // 2 - 1) as i:
                for k in range(2):
                    e = Tile(i, 2 + k)
                    end = sp.value_load(keep["ends"][0:1, bass.ds((e - 2).n, 1)], min_val=1, max_val=BLOCKS)
                    load_expert(sp, a, w, e, ([s["gate"], s["up"], s["down"]], end))
            unused = sp.value_load(keep["unused"][:], min_val=0, max_val=(BLOCKS - EXPERTS) // 2)
            sp.wait_ge(rest_stored, 32 * unused + 1)
            sp.sem_inc(s["ended"], 1)

        @block.vector
        def _(dve):
            low_parts(dve, nc.vector, w, 1, 1)
            with dve.Fori(1, EXPERTS // 2) as i:
                for slot in range(2):
                    low_parts(dve, nc.vector, w, slot, i + 1)

        @block.gpsimd
        def _(pool):
            def gather(b):
                wait_past(pool, s["xtr"], b.n - 1)
                nc.gpsimd.tensor_copy(index[:, b.slot:b.slot + 1], keep["tokens"][:, bass.ds(b.n, 1)]).then_inc(s["indexed"], 1)
                pool.wait_ge(s["indexed"], b.n + 1)
                pool.sem_inc(s["gone"], 1)
                nc.gpsimd.indirect_dma_start(xg[:, b.slot, :], None, keep["parts_dram"],
                                             bass.IndirectOffsetOnAxis(ap=index[:, b.slot:b.slot + 1], axis=0)
                                             ).then_inc(gathered[b.slot], 16)

            def body(b):
                gather(b + 2)
                pool.wait_ge(s["silu"], b.n + 1)
                pool.wait_ge(s["upcopied"], b.n + 1)
                wait_past(pool, s["hidlo"], b.n)
                nc.gpsimd.tensor_tensor(hid[:], silu_g[:], up[:], ALU.mult).then_inc(s["hid"], 1)
                pool.wait_ge(s["hidhi"], b.n + 1)
                nc.gpsimd.tensor_tensor(hid_parts[1][:], hid[:], hid_parts[0][:], ALU.subtract).then_inc(s["hidlo"], 1)

            gather(Tile(0, 0))
            gather(Tile(0, 1))
            nc.gpsimd.memset(zeros[:], 0.0).then_inc(ready, 1)
            body(Tile(0, 0))
            pairs = pairs_of(pool)
            body(Tile(0, 1))
            body(Tile(0, 2))
            with pool.Fori(1, pairs) as i:
                body(Tile(i, 1))
                body(Tile(i, 2))
            pool.wait_ge(gathered[0], 16 * (pairs + 2))
            pool.sem_inc(s["ended"], 1)

        @block.scalar
        def _(act):
            def copy_out(dst, src, wait, count, done):
                act.wait_ge(s[wait], count)
                nc.scalar.activation(dst, src, ACT.Copy).then_inc(s[done], 1)

            def copy_x(b):
                for q in range(2):
                    copy_out(x_t[q][:, b.slot, :], xtr[q][:], "xtr", b.n + 1, "xt_copied")

            def hid_out(p):
                wait_past(act, s["down"], p.n)
                for q in range(2):
                    copy_out(hid_t[q][:], htr[q][:], "htr", p.n + 1, "ht_copied")

            def y_out(p):
                wait_past(act, stored[p.slot], 16 * p.round)
                copy_out(y[:, p.slot, :], bank[:, Y_B:Y_B + 2, :].rearrange("p b n -> p (b n)"), "down", p.n + 1,
                         "ycopied")
                act.wait_ge(s["ycopied"], p.n + 1)
                act.dma_start(keep["y_dram"][bass.ds(p.n * P, P), :], y[:, p.slot, :]).then_inc(stored[p.slot], 16)

            def body(b, before=True):
                copy_x(b + 1)
                act.wait_ge(s["gate"], b.n + 1)
                wait_past(act, s["hid"], b.n)
                nc.scalar.activation(silu_g[:], bank[:, GATE_B, :], ACT.Silu).then_inc(s["silu"], 1)
                if before:
                    hid_out(b - 1)
                copy_out(up[:], bank[:, UP_B, :], "up", b.n + 1, "upcopied")
                act.wait_ge(s["hid"], b.n + 1)
                wait_past(act, s["htr"], b.n)
                nc.scalar.activation(hid_parts[0][:], hid[:], ACT.Copy).then_inc(s["hidhi"], 1)
                if before:
                    y_out(b - 1)

            copy_x(Tile(0, 0))
            body(Tile(0, 0), before=False)
            pairs = pairs_of(act)
            body(Tile(0, 1))
            body(Tile(0, 2))
            with act.Fori(1, pairs) as i:
                body(Tile(i, 1))
                body(Tile(i, 2))
            hid_out(Tile(pairs, 0))
            y_out(Tile(pairs, 0))
            act.wait_ge(stored[0], 16 * (pairs + 1))
            act.wait_ge(stored[1], 16 * pairs)
            act.sem_inc(s["ended"], 1)

        @block.tensor
        def _(pe):
            def transpose_x(b):
                pe.wait_ge(gathered[b.slot], 16 * b.round + 16)
                wait_past(pe, s["xt_copied"], 2 * b.n)
                for q in range(2):
                    for k in range(KT):
                        cols = slice(k * P, (k + 1) * P)
                        ins = nc.tensor.transpose(xtr[q][:, cols], xg_parts[q][:, b.slot, cols], ident[q][:])
                ins.then_inc(s["xtr"], 1)

            def passes(dst, lhs, at, stride, kts, done):
                hi = lambda k: w_hi[:, bass.ds(at * 2 + (2 * k * stride + 1), BANK, step=2)]
                lo = lambda k: w_lo[:, bass.ds(at + k * stride, BANK)]
                for k in range(kts):
                    nc.tensor.matmul(dst, lhs(0, k), hi(k), start=k == 0, stop=False)
                    nc.tensor.matmul(dst, lhs(0, k), lo(k), start=False, stop=False)
                    ins = nc.tensor.matmul(dst, lhs(1, k), hi(k), start=False, stop=k == kts - 1)
                if done is not None:
                    ins.then_inc(s[done], 1)

            def down(b, at, part):
                pe.wait_ge(w["low"], part + 3)
                pe.wait_ge(s["ht_copied"], 2 * b.n + 2)
                wait_past(pe, s["ycopied"], b.n)
                for half in range(2):
                    passes(bank[:, Y_B + half, :], lambda q, k: hid_t[q][:, k * P:(k + 1) * P],
                           at + (2 * PART + half * BANK), D, HT, "down" if half else None)

            def where(b):
                at = pe.value_load(keep["block_slot"][0:1, bass.ds(b.n, 1)], min_val=0, max_val=SLOT)
                part = pe.value_load(keep["block_part"][0:1, bass.ds(b.n, 1)], min_val=0, max_val=3 * (EXPERTS - 1))
                return at, part

            def transpose_hid(p):
                pe.wait_ge(s["hidlo"], p.n + 1)
                pe.wait_ge(s["hidhi"], p.n + 1)
                wait_past(pe, s["ht_copied"], 2 * p.n)
                for q in range(2):
                    for k in range(HT):
                        cols = slice(k * P, (k + 1) * P)
                        ins = nc.tensor.transpose(htr[q][:, cols], hid_parts[q][:, cols], ident[q][:])
                ins.then_inc(s["htr"], 1)

            def body(b, before=True):
                at, part = where(b)
                transpose_x(b + 1)
                x = lambda q, k: x_t[q][:, b.slot, k * P:(k + 1) * P]
                pe.wait_ge(w["low"], part + 1)
                pe.wait_ge(s["xt_copied"], 2 * b.n + 2)
                wait_past(pe, s["silu"], b.n)
                passes(bank[:, GATE_B, :], x, at, D_E, KT, "gate")
                if before:
                    transpose_hid(b - 1)
                pe.wait_ge(w["low"], part + 2)
                wait_past(pe, s["upcopied"], b.n)
                passes(bank[:, UP_B, :], x, at + PART, D_E, KT, "up")
                if before:
                    down(b - 1, *where(b - 1))

            transpose_x(Tile(0, 0))
            body(Tile(0, 0), before=False)
            pairs = pairs_of(pe)
            body(Tile(0, 1))
            body(Tile(0, 2))
            with pe.Fori(1, pairs) as i:
                body(Tile(i, 1))
                body(Tile(i, 2))
            last = Tile(pairs, 0)
            transpose_hid(last)
            down(last, *where(last))


def combine(nc, a, keep):
    ctx = ExitStack()
    with ctx:
        m = Memory(nc, ctx)
        SLOTS = 4
        QUADS = TILES // SLOTS
        g, b = m.sb("ln2_g_sb", [P, D], F32), m.sb("ln2_b_sb", [P, D], F32)
        rows = m.sb("rows", [P, SLOTS, TOP, D], F32)
        h1 = m.sb("h1_back", [P, SLOTS, D], F32)
        mixed = m.sb("mixed", [P, SLOTS, D], F32)
        index = m.sb("c_index", [P, SLOTS, TOP], U32)
        stats = m.sb("c_stats", [P, 2, 6], F32)
        moments = m.sb("c_moments", [P, SLOTS, 2], F32)
        rstd = m.sb("c_rstd", [P, SLOTS, 2], F32)
        minus_half, eps = m.sb("c_minus_half", [P, 1], F32), m.sb("c_eps", [P, 1], F32)
        s = {n: m.sem("c_" + n) for n in ("indexed weighted mixed stats centred scaled rstd done_dve done_pool ready params "
                                          "pool dve passed gone").split()}
        gathered = [m.sem(f"c_gathered{i}") for i in range(SLOTS)]
        loaded = [m.sem(f"c_loaded{i}") for i in range(SLOTS)]
        stored = [m.sem(f"c_stored{i}") for i in range(SLOTS)]
        DVE_COLS, POOL_COLS = slice(0, D // 2), slice(D // 2, D)
        block = ctx.enter_context(nc.Block())

        def tile(i, k):
            return Tile(i, k, SLOTS)

        @block.sync
        def _(sp):
            def load(t):
                wait_past(sp, s["mixed"], t.n - SLOTS + 1)
                sp.dma_start(h1[:, t.slot, :], keep["h1_dram"][bass.ds(t.n * P, P), :]).then_inc(loaded[t.slot], 16)

            def store(t):
                sp.wait_ge(s["done_dve"], t.n + 1)
                sp.wait_ge(s["done_pool"], t.n + 1)
                sp.dma_start(a["out"][bass.ds(t.n * P, P), :], mixed[:, t.slot, :]).then_inc(stored[t.slot], 16)

            load(tile(0, 0))
            sp.dma_start(g[:], a["ln2_g"].partition_broadcast(P)).then_inc(s["params"], 16)
            sp.dma_start(b[:], a["ln2_b"].partition_broadcast(P)).then_inc(s["params"], 16)
            for k in range(1, SLOTS):
                load(tile(0, k))
            with sp.Fori(0, QUADS - 1) as i:
                for k in range(SLOTS):
                    load(tile(i, k + SLOTS))
                    store(tile(i, k))
            for k in range(SLOTS):
                store(tile(QUADS - 1, k))
            for slot in range(SLOTS):
                sp.wait_ge(stored[slot], 16 * QUADS)

        @block.gpsimd
        def _(pool):
            def gather(t):
                wait_past(pool, s["mixed"], t.n - SLOTS + 1)
                nc.gpsimd.tensor_copy(index[:, t.slot, :],
                                      keep["dest"][:, :, bass.ds(t.n, 1)].squeeze(2)).then_inc(s["indexed"], 1)
                pool.wait_ge(s["indexed"], t.n + 1)
                pool.sem_inc(s["gone"], 1)
                for k in range(TOP):
                    nc.gpsimd.indirect_dma_start(rows[:, t.slot, k, :], None, keep["y_dram"],
                                                 bass.IndirectOffsetOnAxis(ap=index[:, t.slot, k:k + 1], axis=0)
                                                 ).then_inc(gathered[t.slot], 16)

            def root(t):
                pool.wait_ge(s["stats"], t.n + 1)
                nc.gpsimd.tensor_tensor(rstd[:, t.slot, 1:2], moments[:, t.slot, 1:2], eps[:],
                                        ALU.add).then_inc(s["pool"], 1)
                pool.wait_ge(s["pool"], t.n + 1)
                nc.gpsimd.tensor_tensor(rstd[:, t.slot, 0:1], rstd[:, t.slot, 1:2], minus_half[:],
                                        ALU.pow).then_inc(s["rstd"], 1)

            def add_bias(t):
                pool.wait_ge(s["scaled"], t.n + 1)
                out = mixed[:, t.slot, POOL_COLS]
                nc.gpsimd.tensor_tensor(out, out, b[:, POOL_COLS], ALU.add).then_inc(s["done_pool"], 1)

            for k in range(SLOTS):
                gather(tile(0, k))
            nc.gpsimd.memset(minus_half[:], -0.5).then_inc(s["ready"], 1)
            nc.gpsimd.memset(eps[:], LN_EPS).then_inc(s["ready"], 1)
            pool.wait_ge(s["ready"], 2)
            pool.wait_ge(s["params"], 32)
            for k in range(SLOTS):
                root(tile(0, k))
                gather(tile(0, k + SLOTS))
                if k:
                    add_bias(tile(0, k - 1))
            with pool.Fori(1, QUADS - 1) as i:
                for k in range(SLOTS):
                    root(tile(i, k))
                    gather(tile(i, k + SLOTS))
                    add_bias(tile(i, k - 1))
            for k in range(SLOTS):
                root(tile(QUADS - 1, k))
                add_bias(tile(QUADS - 1, k - 1))
            add_bias(tile(QUADS - 1, SLOTS - 1))

        @block.scalar
        def _(act):
            def weight(t):
                act.wait_ge(gathered[t.slot], 32 * t.round + 32)
                nc.scalar.activation(rows[:, t.slot, 0, :], rows[:, t.slot, 0, :], ACT.Copy,
                                     scale=keep["pair_w"][:, 0, bass.ds(t.n, 1)]).then_inc(s["weighted"], 1)

            def scale(t):
                act.wait_ge(s["rstd"], t.n + 1)
                act.wait_ge(s["centred"], t.n + 1)
                nc.scalar.activation(mixed[:, t.slot, :], mixed[:, t.slot, :], ACT.Copy,
                                     scale=rstd[:, t.slot, 0:1]).then_inc(s["scaled"], 1)

            weight(tile(0, 0))
            with act.Fori(0, QUADS - 1) as i:
                for k in range(SLOTS):
                    weight(tile(i, k + 1))
                    scale(tile(i, k))
            for k in range(SLOTS):
                if k + 1 < SLOTS:
                    weight(tile(QUADS - 1, k + 1))
                scale(tile(QUADS - 1, k))

        @block.vector
        def _(dve):
            chain = Chain(dve, s["dve"])
            STEPS = 2

            def add_bias(t):
                dve.wait_ge(s["scaled"], t.n + 1)
                out = mixed[:, t.slot, DVE_COLS]
                nc.vector.tensor_tensor(out, out, b[:, DVE_COLS], ALU.add).then_inc(s["done_dve"], 1)

            def body(t):
                chain.base, chain.steps = STEPS * t.n, 0
                slot = t.slot
                out = mixed[:, slot, :]
                dve.wait_ge(s["weighted"], t.n + 1)
                wait_past(dve, stored[slot], 16 * t.round)
                chain.link(nc.vector.scalar_tensor_tensor(out=out, in0=rows[:, slot, 1, :],
                                                          scalar=keep["pair_w"][:, 1, bass.ds(t.n, 1)],
                                                          in1=rows[:, slot, 0, :], op0=ALU.mult, op1=ALU.add))
                dve.wait_ge(loaded[slot], 16 * t.round + 16)
                ins = nc.vector.scalar_tensor_tensor(out=out, in0=h1[:, slot, :], scalar=ALPHA, in1=out, op0=ALU.mult,
                                                     op1=ALU.add)
                ins.then_inc(s["mixed"], 1)
                dve.wait_ge(s["mixed"], t.n + 1)
                nc.vector.bn_stats(stats[:, 0, :], mixed[:, slot, 0:BANK])
                chain.link(nc.vector.bn_stats(stats[:, 1, :], mixed[:, slot, BANK:D]), s["passed"])
                nc.vector.bn_aggr(moments[:, slot, :], stats[:]).then_inc(s["stats"], 1)
                dve.wait_ge(s["stats"], t.n + 1)
                nc.vector.scalar_tensor_tensor(out=out, in0=out, scalar=moments[:, slot, 0:1], in1=g[:],
                                               op0=ALU.subtract, op1=ALU.mult).then_inc(s["centred"], 1)
                assert chain.steps == STEPS

            dve.wait_ge(s["params"], 32)
            for k in range(SLOTS):
                body(tile(0, k))
                if k:
                    add_bias(tile(0, k - 1))
            with dve.Fori(1, QUADS) as i:
                for k in range(SLOTS):
                    body(tile(i, k))
                    add_bias(tile(i, k - 1))
            add_bias(tile(QUADS - 1, SLOTS - 1))


def program(nc, a, stop=None):
    with ExitStack() as ctx:
        sb = lambda name, shape, dt: ctx.enter_context(nc.sbuf_tensor(name, shape, dt))
        keep = {
            "logits": sb("logits", [P, TILES, LOGITS], F32),
            "pair_w": sb("pair_w", [P, 2, TILES], F32),
            "dest": sb("dest_rows", [P, 2, TILES], U32),
            "tokens": sb("tokens", [P, TABLE], U32),
            "pairs": sb("pairs", [1, 1], U32),
            "unused": sb("unused", [1, 1], U32),
            "ends": sb("ends_i", [1, EXPERTS], U32),
            "block_slot": sb("block_slot", [1, RUN_BLOCKS], U32),
            "block_part": sb("block_part", [1, RUN_BLOCKS], U32),
            "h1_dram": nc.dram_tensor("h1_dram", [SEQ, D], F32, kind="Internal").ap(),
            "parts_dram": nc.dram_tensor("parts_dram", [SEQ, 2 * D], BF16, kind="Internal").ap(),
            "y_dram": nc.dram_tensor("y_dram", [RUN_BLOCKS * P, D], F32, kind="Internal").ap(),
        }
        mixer(nc, a, keep)
        with ExitStack() as slots_ctx:
            w = weight_slots(nc, slots_ctx)
            router(nc, a, keep, w)
            experts(nc, a, keep, w)
        combine(nc, a, keep)


def laid_out(inputs):
    g = lambda name: np.asarray(inputs[name])
    row = lambda x: np.ascontiguousarray(x).reshape(-1)
    col = lambda x: np.ascontiguousarray(x.reshape(GROUPS_P, P).T)
    arrays = {
        "x": g("x")[0], "meta": g("meta_tokens"), "ln0_g": row(g("ln_emb_g")), "ln0_b": row(g("ln_emb_b")),
        "w_in": g("w_in")[0], "pool_w": g("pool_w")[0], "pool_b": col(g("pool_b")[0]),
        "pool_scale": col(g("pool_scale")[0]), "w_out": g("w_out")[0], "ln1_g": row(g("ln1_g")[0]),
        "ln1_b": row(g("ln1_b")[0]), "rg_w": g("router_group_w")[0], "rg_b": row(g("router_group_b")[0]),
        "re_w": g("router_expert_w")[0], "re_b": row(g("router_expert_b")[0]), "w_gate": g("expert_w_gate")[0],
        "w_up": g("expert_w_up")[0], "w_down": g("expert_w_down")[0], "ln2_g": row(g("ln2_g")[0]),
        "ln2_b": row(g("ln2_b")[0]),
    }
    arrays.update(shape_constants())
    return {"in_" + k: np.ascontiguousarray(v) for k, v in arrays.items()}


def kernel(**inputs):
    import concourse.bacc as bacc
    from concourse.bass_utils import run_bass_kernel_spmd

    arrays = laid_out(inputs)
    nc = bacc.Bacc("TRN2", target_bir_lowering=False, num_devices=1)
    a = {k[3:]: nc.dram_tensor(k, v.shape, mybir.dt.from_np(v.dtype), kind="ExternalInput").ap()
         for k, v in arrays.items()}
    a["out"] = nc.dram_tensor("out", [SEQ, D], F32, kind="ExternalOutput").ap()
    program(nc, a)
    r = run_bass_kernel_spmd(nc, [arrays], core_ids=[0])
    return r.results[0]["out"].reshape(1, SEQ, D)
```
